# Optimizing a Trainium2 kernel written in Bass

```python
import math
import jax, jax.numpy as jnp
from jax import lax
import numpy as np

D_MODEL = 2048
BATCH = 1
SEQ = 512
DEPTH = 1

CHUNK = 64
D_CONV = 1024
CONV_WIDTH = 3
CONV_GROUPS = 16
D_SSM = 1024
SSM_GROUP = 16
N_SSM_GROUPS = D_SSM // SSM_GROUP
SSM_STATE = 64
DT_MIN = 1e-3
DT_MAX = 1e-1
N_EXPERTS = 16
N_EXPERT_GROUPS = 4
EXPERTS_PER_GROUP = N_EXPERTS // N_EXPERT_GROUPS
TOP_K = 2
D_FF = 1024
ROW_BLOCK = 128
LN_EPS = 1e-5
ALPHA = (2 * DEPTH) ** 0.25
BETA = (8 * DEPTH) ** -0.25
D_IN_PROJ = 3 * D_CONV + D_SSM + 2 * D_MODEL

kernel_name = "hybrid_conv_s5_moe_deepnorm"

def layer_norm(x, g, b):
    xf = x.astype(jnp.float32)
    mu = jnp.mean(xf, axis=-1, keepdims=True)
    var = jnp.mean(jnp.square(xf - mu), axis=-1, keepdims=True)
    y = (xf - mu) * lax.rsqrt(var + LN_EPS) * g.astype(jnp.float32) + b.astype(jnp.float32)
    return y.astype(x.dtype)

def causal_conv3(v, w):
    vp = jnp.pad(v, ((0, 0), (CONV_WIDTH - 1, 0), (0, 0)))
    L = v.shape[1]
    return w[0] * vp[:, 0:L] + w[1] * vp[:, 1:L + 1] + w[2] * vp[:, 2:L + 2]

def _complex_linear_combine(left, right):
    ar1, ai1, br1, bi1 = left
    ar2, ai2, br2, bi2 = right
    ar = ar2 * ar1 - ai2 * ai1
    ai = ar2 * ai1 + ai2 * ar1
    br = ar2 * br1 - ai2 * bi1 + br2
    bi = ar2 * bi1 + ai2 * br1 + bi2
    return (ar, ai, br, bi)

def s5_mixer(u, a_re, a_im, log_dt, b_re, b_im, c_re, c_im, d_skip):
    f32 = jnp.float32
    bsz, seq, _ = u.shape
    G, H, P = N_SSM_GROUPS, SSM_GROUP, SSM_STATE
    uf = u.astype(f32).reshape(bsz, seq, G, H)
    dt = jnp.exp(log_dt.astype(f32))[:, None]
    lam_re = jnp.minimum(a_re.astype(f32), -1e-4)
    lam_im = a_im.astype(f32)
    mag = jnp.exp(lam_re * dt)
    ang = lam_im * dt
    abar_re = mag * jnp.cos(ang)
    abar_im = mag * jnp.sin(ang)
    den = lam_re * lam_re + lam_im * lam_im
    num_re = abar_re - 1.0
    num_im = abar_im
    co_re = (num_re * lam_re + num_im * lam_im) / den
    co_im = (num_im * lam_re - num_re * lam_im) / den
    b_re = b_re.astype(f32)
    b_im = b_im.astype(f32)
    bb_re = co_re[..., None] * b_re - co_im[..., None] * b_im
    bb_im = co_re[..., None] * b_im + co_im[..., None] * b_re
    bu_re = jnp.einsum('blgh,gph->blgp', uf, bb_re)
    bu_im = jnp.einsum('blgh,gph->blgp', uf, bb_im)
    a_seq_re = jnp.broadcast_to(abar_re, (1, seq, G, P))
    a_seq_im = jnp.broadcast_to(abar_im, (1, seq, G, P))
    _, _, s_re, s_im = lax.associative_scan(
        _complex_linear_combine, (a_seq_re, a_seq_im, bu_re, bu_im), axis=1)
    y = (jnp.einsum('ghp,blgp->blgh', c_re.astype(f32), s_re)
         - jnp.einsum('ghp,blgp->blgh', c_im.astype(f32), s_im)
         + d_skip.astype(f32).reshape(G, H) * uf)
    return y.reshape(bsz, seq, D_SSM)

def route(xt, w_router, b_router):
    logits = xt.astype(jnp.float32) @ w_router.astype(jnp.float32) + b_router.astype(jnp.float32)
    probs = jax.nn.softmax(logits, axis=-1)
    grouped = probs.reshape(-1, N_EXPERT_GROUPS, EXPERTS_PER_GROUP)
    group_score = jnp.sum(lax.top_k(grouped, TOP_K)[0], axis=-1)
    best_group = jnp.argmax(group_score, axis=-1).astype(jnp.int32)
    in_group = jnp.take_along_axis(grouped, best_group[:, None, None], axis=1)[:, 0]
    top_v, top_i = lax.top_k(in_group, TOP_K)
    ids = best_group[:, None] * EXPERTS_PER_GROUP + top_i.astype(jnp.int32)
    weights = top_v / jnp.sum(top_v, axis=-1, keepdims=True)
    return ids, weights

def moe_ffn(x, w_router, b_router, w_gate, w_up, w_down):
    bsz, seq, d = x.shape
    T = bsz * seq
    TK = T * TOP_K
    xt = x.reshape(T, d)
    ids, weights = route(xt, w_router, b_router)
    e_flat = ids.reshape(TK)
    w_flat = weights.reshape(TK)
    counts = jnp.bincount(e_flat, length=N_EXPERTS)
    padded = ((counts + ROW_BLOCK - 1) // ROW_BLOCK) * ROW_BLOCK
    pad_end = jnp.cumsum(padded)
    pad_start = pad_end - padded
    start = jnp.cumsum(counts) - counts
    order = jnp.argsort(e_flat)
    e_sorted = e_flat[order]
    rank = jnp.arange(TK, dtype=jnp.int32) - start[e_sorted]
    dest = pad_start[e_sorted] + rank
    n_blocks = -(-TK // ROW_BLOCK) + N_EXPERTS
    n_rows = n_blocks * ROW_BLOCK
    buf_tok = jnp.full((n_rows,), T, dtype=jnp.int32).at[dest].set((order // TOP_K).astype(jnp.int32))
    buf_w = jnp.zeros((n_rows,), jnp.float32).at[dest].set(w_flat[order])
    block_expert = jnp.clip(
        jnp.searchsorted(pad_end, jnp.arange(n_blocks, dtype=pad_end.dtype) * ROW_BLOCK, side='right'),
        0, N_EXPERTS - 1).astype(jnp.int32)
    xpad = jnp.concatenate([xt, jnp.zeros((1, d), xt.dtype)], axis=0)
    xb = xpad[buf_tok].reshape(n_blocks, ROW_BLOCK, d)

    def expert_block(args):
        xblk, e = args
        hid = jax.nn.silu(xblk @ w_gate[e]) * (xblk @ w_up[e])
        return hid @ w_down[e]

    yb = lax.map(expert_block, (xb, block_expert)).reshape(n_rows, d)
    yb = yb * buf_w.astype(yb.dtype)[:, None]
    out = jnp.zeros((T + 1, d), yb.dtype).at[buf_tok].add(yb)[:T]
    return out.reshape(bsz, seq, d)

def setup_inputs(seed: int = 0) -> dict:
    key = jax.random.key(seed)
    ks = jax.random.split(key, 24)
    nrm = jax.random.normal
    G, H, P, E = N_SSM_GROUPS, SSM_GROUP, SSM_STATE, N_EXPERTS
    x = nrm(ks[0], (BATCH, SEQ, D_MODEL), jnp.float32)
    in_g = 1.0 + 0.02 * nrm(ks[1], (D_MODEL,), jnp.float32)
    in_b = 0.02 * nrm(ks[2], (D_MODEL,), jnp.float32)
    w_in = nrm(ks[3], (DEPTH, D_MODEL, D_IN_PROJ), jnp.float32) * D_MODEL ** -0.5
    conv_w = nrm(ks[4], (DEPTH, CONV_WIDTH, D_CONV), jnp.float32) * CONV_WIDTH ** -0.5
    w_out_a = nrm(ks[5], (DEPTH, D_CONV, D_MODEL), jnp.float32) * (D_CONV ** -0.5 * BETA)
    ssm_a_re = -0.5 + 0.01 * nrm(ks[6], (DEPTH, G, P), jnp.float32)
    ssm_a_im = (jnp.pi * jnp.arange(P, dtype=jnp.float32))[None, None, :] + 0.01 * nrm(ks[7], (DEPTH, G, P), jnp.float32)
    ssm_log_dt = jax.random.uniform(ks[8], (DEPTH, G), jnp.float32, math.log(DT_MIN), math.log(DT_MAX))
    ssm_b_re = nrm(ks[9], (DEPTH, G, P, H), jnp.float32) * (2 * H) ** -0.5
    ssm_b_im = nrm(ks[10], (DEPTH, G, P, H), jnp.float32) * (2 * H) ** -0.5
    ssm_c_re = nrm(ks[11], (DEPTH, G, H, P), jnp.float32) * (2 * P) ** -0.5
    ssm_c_im = nrm(ks[12], (DEPTH, G, H, P), jnp.float32) * (2 * P) ** -0.5
    ssm_d = nrm(ks[13], (DEPTH, D_SSM), jnp.float32)
    w_glu = jnp.concatenate([
        nrm(ks[14], (DEPTH, D_SSM, D_MODEL), jnp.float32) * (D_SSM ** -0.5 * BETA),
        nrm(ks[15], (DEPTH, D_SSM, D_MODEL), jnp.float32) * D_SSM ** -0.5], axis=-1)
    w_o = nrm(ks[16], (DEPTH, D_MODEL, D_MODEL), jnp.float32) * (D_MODEL ** -0.5 * BETA)
    kl = jax.random.split(ks[17], 4)
    ln1_g = 1.0 + 0.02 * nrm(kl[0], (DEPTH, D_MODEL), jnp.float32)
    ln1_b = 0.02 * nrm(kl[1], (DEPTH, D_MODEL), jnp.float32)
    ln2_g = 1.0 + 0.02 * nrm(kl[2], (DEPTH, D_MODEL), jnp.float32)
    ln2_b = 0.02 * nrm(kl[3], (DEPTH, D_MODEL), jnp.float32)
    w_router = nrm(ks[18], (D_MODEL, E), jnp.float32) * D_MODEL ** -0.5
    b_router = 0.01 * nrm(ks[19], (E,), jnp.float32)
    w_gate = nrm(ks[20], (DEPTH, E, D_MODEL, D_FF), jnp.float32) * D_MODEL ** -0.5
    w_up = nrm(ks[21], (DEPTH, E, D_MODEL, D_FF), jnp.float32) * D_MODEL ** -0.5
    w_down = nrm(ks[22], (DEPTH, E, D_FF, D_MODEL), jnp.float32) * (D_FF ** -0.5 * BETA)
    return {"x": x, "in_g": in_g, "in_b": in_b, "w_in": w_in, "conv_w": conv_w,
            "w_out_a": w_out_a, "ssm_a_re": ssm_a_re, "ssm_a_im": ssm_a_im,
            "ssm_log_dt": ssm_log_dt, "ssm_b_re": ssm_b_re, "ssm_b_im": ssm_b_im,
            "ssm_c_re": ssm_c_re, "ssm_c_im": ssm_c_im, "ssm_d": ssm_d, "w_glu": w_glu,
            "w_o": w_o, "ln1_g": ln1_g, "ln1_b": ln1_b, "ln2_g": ln2_g, "ln2_b": ln2_b,
            "w_router": w_router, "b_router": b_router, "w_gate": w_gate, "w_up": w_up,
            "w_down": w_down}

def reference(x, in_g, in_b, w_in, conv_w, w_out_a, ssm_a_re, ssm_a_im, ssm_log_dt,
              ssm_b_re, ssm_b_im, ssm_c_re, ssm_c_im, ssm_d, w_glu, w_o,
              ln1_g, ln1_b, ln2_g, ln2_b, w_router, b_router, w_gate, w_up, w_down):
    splits = [D_CONV, 2 * D_CONV, 3 * D_CONV, 3 * D_CONV + D_SSM, 3 * D_CONV + D_SSM + D_MODEL]
    x = layer_norm(x, in_g, in_b)
    for l in range(DEPTH):
        h = x @ w_in[l]
        xin, c_gate, b_gate, u, g_a, g_b = jnp.split(h, splits, axis=-1)
        y_a = (b_gate * causal_conv3(c_gate * xin, conv_w[l])) @ w_out_a[l]
        ys = jax.nn.gelu(s5_mixer(u, ssm_a_re[l], ssm_a_im[l], ssm_log_dt[l], ssm_b_re[l],
                                  ssm_b_im[l], ssm_c_re[l], ssm_c_im[l], ssm_d[l])).astype(x.dtype)
        gv = ys @ w_glu[l]
        y_b = gv[..., :D_MODEL] * jax.nn.sigmoid(gv[..., D_MODEL:])
        mixed = jax.nn.sigmoid(g_a) * y_a + jax.nn.sigmoid(g_b) * y_b
        x = layer_norm(ALPHA * x + mixed @ w_o[l], ln1_g[l], ln1_b[l])
        x = layer_norm(ALPHA * x + moe_ffn(x, w_router, b_router, w_gate[l], w_up[l], w_down[l]),
                       ln2_g[l], ln2_b[l])
    return x


_drawn_inputs = setup_inputs


def setup_inputs(seed=0):
    import zlib

    import numpy as np

    out = dict(_drawn_inputs(seed))
    spreads = {}
    factors = {'ssm_a_re': 64.0,
     'ssm_a_im': 41.52,
     'ssm_log_dt': 64.0,
     'ssm_b_re': 44.656,
     'ssm_b_im': 42.656,
     'ssm_c_re': 41.432,
     'ssm_c_im': 64.0,
     'ln2_g': 7.75,
     'ln2_b': 8.1}
    for name, (base, spread) in spreads.items():
        noise = np.random.default_rng([zlib.crc32(name.encode()), seed]).standard_normal(out[name].shape)
        drawn = base * np.exp(spread * noise) if base else spread * noise
        out[name] = __import__('jax').numpy.asarray(drawn.astype(out[name].dtype))
    for name, factor in factors.items():
        out[name] = (out[name] * factor).astype(out[name].dtype)
    return out
```

```python
import math

import numpy as np

import concourse.bass as bass
from concourse import mybir
from contextlib import ExitStack

F32 = mybir.dt.float32
F32R = mybir.dt.float32r
I32 = mybir.dt.int32
ALU = mybir.AluOpType
ACT = mybir.ActivationFunctionType
AX = mybir.AxisListType

P = 128
T = 512
D = 2048
DC = 1024
DS = 1024
CONV_WIDTH = 3
G, H, N = 64, 16, 64
E, EG, EP = 16, 4, 4
F = 1024
EPS = 1e-5
ALPHA = 2.0 ** 0.25
TT = T // P
KD = D // P
KF = F // P
PIECE = 2048
UC = 256

STEP = 8
NCH = T // STEP
GG = G // 2
HG = GG // 2

N_U, N_CONV, N_OA, N_G, N_GLU, N_WO = 8, 24, 8, 32, 16, 16
Q_U = 0
Q_CONV = Q_U + N_U
Q_OA = Q_CONV + N_CONV
Q_G = Q_OA + N_OA
Q_GLU = Q_G + N_G
Q_WO = Q_GLU + N_GLU
Q_MOE = Q_WO + N_WO
PB = 24
NBLK = E + (2 * T - E) // P
NOVER = NBLK - E
RAW = 4
RD = 2
RM = 4

N_PRM = 10

MAGIC = 1.5 * 2.0 ** 23


def two_pi_parts():
    c1 = math.floor(2 * math.pi * 2 ** 7) / 2 ** 7
    c2 = math.floor((2 * math.pi - c1) * 2 ** 19) / 2 ** 19
    return c1, c2, 2 * math.pi - c1 - c2


class Link:

    def __init__(self, eng, sem):
        self.eng, self.sem, self.n = eng, sem, 0

    def go(self, ins):
        self.n += 1
        ins.then_inc(self.sem, 1)

    def wait(self):
        self.eng.wait_ge(self.sem, self.n)

    def link(self, ins):
        self.go(ins)
        self.wait()


def unit_of(q):
    if q < Q_OA:
        return q // 2
    return 16 + q - Q_OA if q < Q_G else 24 + (q - Q_G) // 2


def tokens_by(pe, o, x_hi, x_lo, w_hi, w_lo, first, last):
    pe.matmul(o, lhsT=x_hi, rhs=w_hi, start=first, stop=False)
    pe.matmul(o, lhsT=x_lo, rhs=w_hi, start=False, stop=False)
    return pe.matmul(o, lhsT=x_hi, rhs=w_lo, start=False, stop=last)


def build_trunk(nc, x, in_g, in_b, w_in, conv_w, w_out_a, ssm_a_re, ssm_a_im, ssm_log_dt,
                ssm_b_re, ssm_b_im, ssm_c_re, ssm_c_im, ssm_d, w_glu, w_o,
                ln1_g, ln1_b, ln2_g, ln2_b, w_router, b_router, w_gate, w_up, w_down, out):
    ctx = ExitStack()
    with ctx:
        base = nc.sbuf_base + (-nc.sbuf_base) % 64
        KB = 1024

        def at(name, shape, kb, dtype=F32):
            return nc.alloc_sbuf_tensor_at(name, shape, dtype, offset=base + int(kb * KB))


        raw = at("raw", [P, RAW, PIECE], 0)
        whi = at("whi", [P, RD, PIECE], 32, F32R)
        wlo = at("wlo", [P, RD, PIECE], 48, F32R)
        mhi = at("mhi", [P, RM, PIECE], 32, F32R)
        mlo = at("mlo", [P, RM, PIECE], 64, F32R)
        xT_hi = at("xT_hi", [P, KD, T], 64, F32R)
        xT_lo = at("xT_lo", [P, KD, T], 96, F32R)
        mx_hi = at("mx_hi", [P, KD, T], 64, F32R)
        mx_lo = at("mx_lo", [P, KD, T], 96, F32R)
        xin = at("xin", [P, TT, D], 128)
        lng = at("lng", [P, D], 160)
        lnb = at("lnb", [P, D], 168)
        pa_hi = at("pa_hi", [P, 8, T], 128, F32R)
        pa_lo = at("pa_lo", [P, 8, T], 144, F32R)
        ust = at("ust", [P, 2, T], 160)
        cx = at("cx", [P, 2, T], 164)
        cv = at("cv", [P, 2, T + 2], 168)
        ct = at("ct", [P, 2, T], 172.5)
        zrow = at("zrow", [P, 1024], 194)
        cnat = at("cnat", [P, 2, 8, 2, N], 176.5)
        prm = at("prm", [P, 30, GG], 184.5)
        nat = at("nat", [GG, 3, P], 188.25)
        braw = at("braw", [P, 2, GG, H], 189.75)
        Bb = at("Bb", [P, 2, GG, H], 194)
        Cc = at("Cc", [P, 2, GG, H], 198)
        A1 = at("A1", [P, 3, GG], 202)
        P8 = at("P8", [P, STEP, 3, GG], 202.375)
        VT = at("VT", [P, 2, HG, STEP, H], 128)
        W = at("W", [P, 2, HG, STEP + 1, H], 128)
        V = at("V", [P, 2, HG, P], 146)
        kpd = at("kpd", [2 * H, HG, 15, H], 146)
        M = at("M", [P, HG, 2, P], 146)
        U = at("U", [P, 2 * HG, NCH], 162)
        S = at("S", [P, 2, HG, NCH], 170)
        t1 = at("t1", [P, 2, HG, H], 178)
        t2 = at("t2", [P, 2, HG, H], 180)
        Bbd = at("Bbd", [P, 2, HG, 2, H], 182)
        yst = at("yst", [P, HG, 2, NCH], 178)
        sgst = at("sgst", [P, 2, T], 186)
        dgv = at("dgv", [2 * H, GG], 193.75)
        dmask = at("dmask", [2 * H, H], 193.875)
        dsk = at("dsk", [2 * H, GG, H], 190)
        ys_hi = at("ys_hi", [P, 8, T], 128, F32R)
        ys_lo = at("ys_lo", [P, 8, T], 144, F32R)
        yraw = at("yraw", [P, 8, T], 160)
        gin = at("gin", [P, 3, 2, T], 176)
        sgt = at("sgt", [P, 2, T], 188)
        gm = at("gm", [P, 2, T], 192)
        x1 = at("x1", [P, TT, D], 128)
        lng1 = at("lng1", [P, D], 160)
        lnb1 = at("lnb1", [P, D], 168)
        x1T = at("x1T", [P, 2, KD, P], 176)
        wr = at("wr", [P, KD, E], 196)
        tri = at("tri", [P, P], 197)
        ones = at("ones", [P, P], 197.5)
        brb = at("brb", [P, E], 198)
        eio = at("eio", [P, 3, E], 198.125)
        gio = at("gio", [P, EG], 198.375)
        R = at("R", [P, 24, TT, E], 198.5)
        RI = at("RI", [P, TT, E], 204.5, I32)
        ovk = at("ovk", [P, NOVER + 1, E], 194)
        ovn = at("ovn", [P, NOVER + 1], 195.5)
        xg = at("xg", [P, D], 96)
        xg_hi = at("xg_hi", [P, KD, P], 104, F32R)
        xg_lo = at("xg_lo", [P, KD, P], 112, F32R)
        sil = at("sil", [P, F], 120)
        hid = at("hid", [P, F], 124)
        h_hi = at("h_hi", [P, KF, P], 160, F32R)
        h_lo = at("h_lo", [P, KF, P], 164, F32R)
        ybl = at("ybl", [P, D], 168)
        lng2 = at("lng2", [P, D], 176)
        lnb2 = at("lnb2", [P, D], 184)
        yg = at("yg", [P, 2, 2, D], 32)
        place = [205.5]

        def small(name, shape, dtype=F32):
            t = at(name, shape, place[0], dtype)
            words = 1
            for n in shape[1:]:
                words *= n
            place[0] += math.ceil(words * 4 / 32) * 32 / KB
            return t

        ident = small("ident", [P, P])
        cwn = small("cwn", [CONV_WIDTH * 8, P])
        dnat = small("dnat", [GG, 2 * H])
        ldt = small("ldt", [GG, 2])
        cw = small("cw", [P, 8, 3])
        mv = small("mv", [P, TT, 2])
        rstd = small("rstd", [P, TT])
        nmr = small("nmr", [P, TT])
        tmp4 = small("tmp4", [P, TT])
        bst = small("bst", [P, TT, 4, 6])
        tab = small("tab", [P, 32], I32)
        dest = small("dest", [P, TT, 2], I32)
        back = small("back", [P, TT, 2], I32)
        wts = small("wts", [P, TT, 2])
        bidx = small("bidx", [P, 1], I32)
        ahead = small("ahead", [P, 4])
        zeros = small("zeros", [P, NBLK + 1], I32)
        tokid = small("tokid", [P, TT], I32)
        assert base + place[0] * KB <= nc.sbuf_usable_end, (base + place[0] * KB, nc.sbuf_usable_end)

        dn = ctx.enter_context(nc.psum_tensor("dn", [P, 4, 512], F32))
        ex = ctx.enter_context(nc.psum_tensor("ex", [P, 4, 512], F32))
        sets = (ex, dn)

        x0_d = nc.dram_tensor("x0_d", [T, D], F32).ap()
        u_d = nc.dram_tensor("u_d", [DS, STEP, NCH], F32).ap()
        ya_d = nc.dram_tensor("ya_d", [D, T], F32).ap()
        sg_d = nc.dram_tensor("sg_d", [2 * D, T], F32).ap()
        kp_d = nc.dram_tensor("kp_d", [GG, 2, H, 15 * H], F32).ap()
        y_d = nc.dram_tensor("y_d", [DS, STEP, NCH], F32).ap()
        x1_d = nc.dram_tensor("x1_d", [T, D], F32).ap()
        tok_d = nc.dram_tensor("tok_d", [(NBLK + 1) * P, 1], I32).ap()
        yb_d = nc.dram_tensor("yb_d", [NBLK * P, D], F32).ap()

        def sem(name):
            return ctx.enter_context(nc.semaphore(name))

        s_raw = [sem(f"raw_loaded{i}") for i in range(RAW)]
        s_hi = sem("hi_written")
        s_lo = sem("lo_written")
        s_used = sem("piece_used")
        s_link = sem("vector_link")
        s_plink = sem("pool_link")
        s_const = sem("constants_built")
        s_const2 = sem("router_constants_built")
        s_x = [sem(f"x_loaded{i}") for i in range(TT)]
        s_lnp = [sem("ln0_loaded"), sem("ln1_loaded"), sem("ln2_loaded")]
        s_prm = sem("parameters_loaded")
        s_ldt = sem("log_dt_loaded")
        s_nat = sem("log_dt_spread")
        s_zero = sem("token_table_cleared")
        s_ybz = sem("overflow_rows_cleared")
        s_var = sem("variance_ready")
        s_sq = sem("root_ready")
        s_rs = sem("row_scale_ready")
        s_xn = sem("rows_normalised")
        s_xm = sem("rows_scaled")
        s_rows = sem("rows_ready")
        s_tr = sem("rows_transposed")
        s_trh = sem("transposed_hi")
        s_trl = sem("transposed_lo")
        s_x0o = sem("x0_stored")
        s_cp = sem("copied_out")
        s_ust = [sem("ust_stored0"), sem("ust_stored1")]
        s_sgo = [sem("gate_stored0"), sem("gate_stored1")]
        s_cx = sem("xin_copied")
        s_pa = sem("conv_ready")
        s_pah = sem("conv_hi")
        s_pal = sem("conv_lo")
        s_ptr = sem("parameters_transposed")
        s_pcp = sem("parameters_copied")
        s_cm = sem("conv_input_ready")
        s_cz = sem("conv_padding_zeroed")
        s_bst = sem("ln1_statistics")
        s_ctr = sem("C_transposed")
        s_cc = sem("C_ready")
        s_ang = sem("angles_ready")
        s_sin = sem("sines_ready")
        s_u = sem("U_loaded")
        s_vt = sem("VT_ready")
        s_vtr = sem("VT_transposed")
        s_v = sem("V_ready")
        s_bu = sem("chunk_inputs_done")
        s_s = sem("chunk_inputs_ready")
        s_w = sem("W_ready")
        s_k = sem("K_done")
        s_kp = sem("K_padded")
        s_kps = sem("K_stored")
        s_m = sem("M_loaded")
        s_st = sem("states_ready")
        s_y = sem("y_done")
        s_yg = sem("y_gelu_ready")
        s_yo = sem("y_stored")
        s_yl = sem("y_loaded")
        s_ysh = sem("ys_hi_ready")
        s_ysl = sem("ys_lo_ready")
        s_gin = sem("glu_inputs_loaded")
        s_sgt = sem("glu_gate_ready")
        s_gm = sem("mixed_ready")
        s_mh = sem("mixed_hi")
        s_ml = sem("mixed_lo")
        s_wof = sem("w_o_banks_free")
        s_res = sem("residual_loaded")
        s_x1o = sem("x1_then_blocks_stored")
        s_x1t = sem("x1_transposed")
        s_x1c = sem("x1T_copied")
        s_log = sem("logits_done")
        s_lgc = sem("logits_copied")
        s_msk = sem("masks_ready")
        s_rnk = sem("ranks_done")
        s_dst = sem("destinations_ready")
        s_tab = sem("table_ready")
        s_sct = sem("tokens_scattered")
        s_bix = sem("block_tokens_loaded")
        s_xg = sem("block_rows_gathered")
        s_xt = sem("block_rows_transposed")
        s_xh = sem("block_hi")
        s_xl = sem("block_lo")
        s_sil = sem("silu_ready")
        s_hm = sem("hidden_ready")
        s_ht = sem("hidden_transposed")
        s_hh = sem("hidden_hi")
        s_hl = sem("hidden_lo")
        s_yb = sem("block_half_copied")
        s_yr = [sem("expert_rows_gathered0"), sem("expert_rows_gathered1")]
        s_xa = sem("residual_scaled")
        s_ygf = sem("expert_rows_used")
        s_out = sem("output_stored")

        block = ctx.enter_context(nc.Block())

        U_COL, XIN_COL, C_COL, B_COL, GA_COL = 3 * DC, 0, DC, 2 * DC, 3 * DC + DS
        w_in2, w_oa2, w_glu2, w_o2 = w_in[0], w_out_a[0], w_glu[0], w_o[0]

        def conv_col(unit):
            return (XIN_COL, C_COL, B_COL)[unit % 3] + unit // 3 * UC

        def piece_rows(w, k0, nk, c0, nc_):
            return w[k0 * P:(k0 + nk) * P, bass.ds(c0, nc_)].rearrange("(k p) n -> p k n", p=P)

        def raw_v(s, nk):
            return raw[:, s, :].rearrange("p (k n) -> p k n", k=nk)

        @block.sync
        def _(sp):
            for t in range(TT):
                sp.dma_start(xin[:, t, :], x[0, t * P:(t + 1) * P, :]).then_inc(s_x[t], 16)

            def load(q, s, nk, src):
                sp.wait_ge(s_lo, q - RAW + 1)
                sp.dma_start(raw_v(s, nk), src).then_inc(s_raw[s], 16)

            for q in range(RAW):
                sp.dma_start(raw_v(q, 8), piece_rows(w_in2, 8 * (q % 2), 8, U_COL + q // 2 * UC, UC))\
                  .then_inc(s_raw[q], 16)
            for q in range(RAW, N_U):
                load(q, q % RAW, 8, piece_rows(w_in2, 8 * (q % 2), 8, U_COL + q // 2 * UC, UC))
            for i in range(N_CONV):
                load(Q_CONV + i, i % RAW, 8, piece_rows(w_in2, 8 * (i % 2), 8, conv_col(i // 2), UC))
            for i in range(N_OA):
                load(Q_OA + i, i % RAW, 8, piece_rows(w_oa2, 0, 8, i * UC, UC))
            with sp.Fori(0, N_G // RAW) as r:
                for i in range(RAW):
                    load(Q_G + r * RAW + i, i, 8,
                         piece_rows(w_in2, 8 * (i % 2), 8, GA_COL + (r * 2 + i // 2) * UC, UC))
            for i in range(N_GLU):
                load(Q_GLU + i, i % RAW, 8, piece_rows(w_glu2, 0, 8, i % 2 * D + i // 2 * UC, UC))
            with sp.Fori(0, N_WO // RAW) as r:
                for i in range(RAW):
                    load(Q_WO + r * RAW + i, i, 4, piece_rows(w_o2, 4 * i, 4, r * 512, 512))

            def expert_piece(i, e):
                if i < 16:
                    w, k, c = (w_gate, w_up)[i // 8], 2 * (i % 8), 0
                else:
                    w, k, c = w_down, 2 * ((i - 16) % 4), (i - 16) // 4 * 1024
                rows = w[0].rearrange("e k n -> (e k) n")
                row = e * w.shape[2] + k * P
                if not isinstance(row, int):
                    row = sp.snap(row)
                return rows[bass.ds(row, 2 * P), c:c + 1024].rearrange("(k p) n -> p k n", p=P)

            def block_pieces(b, e, e_next):
                for i in range(3, PB + 3):
                    load(Q_MOE + b * PB + i, i % RAW, 2,
                         expert_piece(i % PB, e if i < PB else e_next))

            for i in range(3):
                load(Q_MOE + i, i % RAW, 2, expert_piece(i, 0))
            with sp.Fori(0, E - 1) as b:
                block_pieces(b, b, b + 1)
            sp.wait_ge(s_tab, 1)
            blocks = sp.value_load(tab[0:1, NBLK + 1:NBLK + 2], min_val=E, max_val=NBLK)
            with sp.Fori(E - 1, NBLK) as b:
                with sp.If(b < blocks):
                    e = sp.value_load(tab[0:1, bass.ds(b, 1)], min_val=0, max_val=E - 1)
                    en = sp.value_load(tab[0:1, bass.ds(b + 1, 1)], min_val=0, max_val=E - 1)
                    block_pieces(b, e, en)

        @block.gpsimd
        def _(pool):
            lk = Link(pool, s_plink)
            lk.link(pool.memset(ident[:], 0.0))
            pool.affine_select(out=ident[:], in_=ident[:], compare_op=ALU.not_equal, fill=1.0, base=0,
                               pattern=[[-1, P]], channel_multiplier=1).then_inc(s_const, 1)
            pool.memset(zeros[:], 0).then_inc(s_const, 1)
            pool.memset(zrow[:], 0.0).then_inc(s_const, 1)
            pool.iota(tokid[:], pattern=[[P, TT]], base=0, channel_multiplier=1).then_inc(s_const, 1)

            pool.wait_ge(s_ldt, 16)
            pool.tensor_copy(nat[:, 2, :].rearrange("g (r n) -> g r n", r=2),
                             ldt[:].unsqueeze(2).to_broadcast([GG, 2, N])).then_inc(s_nat, 1)

            def add_shift(buf, shift, t, n):
                pool.wait_ge(s_xm, n)
                pool.tensor_tensor(buf[:, t, :], buf[:, t, :], shift[:], ALU.add).then_inc(s_rows, 1)

            pool.wait_ge(s_lnp[0], 32)
            for t in range(TT):
                add_shift(xin, lnb, t, t + 1)
            pool.wait_ge(s_rows, TT)
            pool.memset(cv[:, :, 0:2], 0.0).then_inc(s_cz, 1)
            pool.wait_ge(s_const, 4)
            for b in range(E, NBLK):
                for c in range(2):
                    pool.dma_start(yb_d[b * P:(b + 1) * P, c * 1024:(c + 1) * 1024], zrow[:]).then_inc(s_ybz, 16)

            for half in range(2):
                if half == 0:
                    for c in range(2):
                        pool.wait_ge(s_ust[c], 16 * 12)
                else:
                    pool.wait_ge(s_y, 1)
                for j in range(STEP):
                    pool.dma_start(U[j * H:(j + 1) * H, :, :],
                                   u_d[half * DS // 2:(half + 1) * DS // 2, j, :]
                                   .rearrange("(g h) n -> h g n", h=H)).then_inc(s_u, 16)
                pool.wait_ge(s_kp, half + 1)
                for r in range(2):
                    pool.dma_start(kp_d[half * HG:(half + 1) * HG, r, :, :].rearrange("g h x -> h g x"),
                                   kpd[r * H:(r + 1) * H, :, :, :].rearrange("h g d c -> h g (d c)"))\
                        .then_inc(s_kps, 16)
                pool.wait_ge(s_kps, 32 * (half + 1))
                for i in range(STEP):
                    pool.dma_start(M[i * H:(i + 1) * H, :, :, :].rearrange("h g r x -> h (g r) x"),
                                   kp_d[half * HG:(half + 1) * HG, :, :, (7 - i) * H:(7 - i) * H + P]
                                   .rearrange("g r h x -> h (g r) x")).then_inc(s_m, 16)
                pool.wait_ge(s_yg, 4 * (half + 1))
                for j in range(STEP):
                    pool.dma_start(y_d[half * DS // 2:(half + 1) * DS // 2, j, :]
                                   .rearrange("(g h) n -> h g n", h=H),
                                   yst[j * H:(j + 1) * H, :, :, :].rearrange("h g r n -> h (g r) n"))\
                        .then_inc(s_yo, 16)
            pool.wait_ge(s_yo, 16 * 16)
            pool.dma_start(yraw[:, :, :], y_d.rearrange("(k p) j n -> p k (j n)", p=P)).then_inc(s_yl, 16)

            lk.link(pool.memset(tri[:], 1.0))
            lk.link(pool.affine_select(out=tri[:], in_=tri[:], compare_op=ALU.is_gt, fill=0.0, base=0,
                                       pattern=[[1, P]], channel_multiplier=-1))
            pool.memset(ones[:], 1.0).then_inc(s_const2, 1)
            lk.link(pool.iota(RI[:, 0, :], pattern=[[1, E]], base=0, channel_multiplier=0))
            lk.link(pool.tensor_copy(eio[:, 0, :], RI[:, 0, :]))
            lk.link(pool.iota(RI[:, 1, :], pattern=[[0, EG], [-1, EP]], base=EP, channel_multiplier=0))
            lk.link(pool.tensor_copy(eio[:, 1, :], RI[:, 1, :]))
            lk.link(pool.iota(RI[:, 2, :], pattern=[[-P, E]], base=P * (E - 1), channel_multiplier=0))
            lk.link(pool.tensor_copy(eio[:, 2, :], RI[:, 2, :]))
            lk.link(pool.iota(RI[:, 3, 0:EG], pattern=[[-1, EG]], base=EG, channel_multiplier=0))
            lk.link(pool.tensor_copy(gio[:], RI[:, 3, 0:EG]))

            for c in range(2):
                pool.wait_ge(s_sgo[c], 16 * 16)
            with pool.Fori(0, 8) as j:
                pool.wait_ge(s_gm, j + 1)
                for n, (src, row) in enumerate(((ya_d, j * UC), (sg_d, j * UC), (sg_d, j * UC + D))):
                    pool.dma_start(gin[:, n, :, :], src[bass.ds(row, UC), :]
                                   .rearrange("(c p) t -> p c t", p=P)).then_inc(s_gin, 16)

            pool.wait_ge(s_used, Q_WO)
            pool.wait_ge(s_x0o, 16 * TT)
            pool.dma_start(x1[:], x0_d.rearrange("(t p) d -> p t d", p=P)).then_inc(s_res, 16)
            pool.dma_start(lng1[:], ln1_g[0].partition_broadcast(P)).then_inc(s_lnp[1], 16)
            pool.dma_start(lnb1[:], ln1_b[0].partition_broadcast(P)).then_inc(s_lnp[1], 16)
            pool.dma_start(wr[:], w_router.rearrange("(k p) e -> p k e", p=P)).then_inc(s_lnp[1], 16)
            pool.dma_start(brb[:], b_router.partition_broadcast(P)).then_inc(s_lnp[1], 16)
            pool.wait_ge(s_gm, 9)
            pool.wait_ge(s_ml, 8)
            lk.link(pool.iota(RI[:, 0, 0:NOVER + 1], pattern=[[1, NOVER + 1]], base=0, channel_multiplier=0))
            pool.tensor_copy(ovn[:], RI[:, 0, 0:NOVER + 1]).then_inc(s_const2, 1)

            for t in range(TT):
                add_shift(x1, lnb1, t, TT + t + 1)

            pool.wait_ge(s_zero, 16)
            pool.wait_ge(s_dst, 1)
            for t in range(TT):
                for k in range(2):
                    pool.indirect_dma_start(
                        out=tok_d[:, :], out_offset=bass.IndirectOffsetOnAxis(ap=dest[:, t, k:k + 1], axis=0),
                        in_=tokid[:, t:t + 1], in_offset=None).then_inc(s_sct, 16)
            pool.wait_ge(s_sct, 16 * 2 * TT)
            pool.wait_ge(s_x1o, 16 * TT)

            def gather(b):
                pool.wait_ge(s_xt, b)
                pool.dma_start(bidx[:], tok_d[b * P:(b + 1) * P, :]).then_inc(s_bix, 16)
                pool.wait_ge(s_bix, b * 16 + 16)
                pool.indirect_dma_start(
                    out=xg[:], out_offset=None, in_=x1_d[:, :],
                    in_offset=bass.IndirectOffsetOnAxis(ap=bidx[:], axis=0)).then_inc(s_xg, 16)

            gather(0)
            pool.dma_start(lng2[:], ln2_g[0].partition_broadcast(P)).then_inc(s_lnp[2], 16)
            pool.dma_start(lnb2[:], ln2_b[0].partition_broadcast(P)).then_inc(s_lnp[2], 16)
            pool.wait_ge(s_x1t, 4 * TT)
            for t in range(TT):
                pool.tensor_scalar(x1[:, t, :], x1[:, t, :], ALPHA, None, ALU.mult).then_inc(s_xa, 1)
            for b in range(E):
                gather(b + 1)
            pool.wait_ge(s_tab, 1)
            blocks = pool.value_load(tab[0:1, NBLK + 1:NBLK + 2], min_val=E, max_val=NBLK)
            for b in range(E, NBLK):
                with pool.If(blocks > b):
                    gather(b + 1)

            pool.wait_ge(s_used, blocks * PB + (Q_MOE + 3))
            pool.wait_ge(s_x1o, blocks * 16 + 16 * TT)
            lk.link(pool.tensor_tensor(back[:].rearrange("p t k -> p (t k)"), dest[:].rearrange("p t k -> p (t k)"),
                                       zeros[:, 0:2 * TT], ALU.add))
            pool.wait_ge(s_ybz, 16 * 2 * NOVER)
            for t in range(TT):
                if t >= 2:
                    pool.wait_ge(s_ygf, t - 1)
                for k in range(2):
                    pool.indirect_dma_start(
                        out=yg[:, t % 2, k, :], out_offset=None, in_=yb_d[:, :],
                        in_offset=bass.IndirectOffsetOnAxis(ap=back[:, t, k:k + 1], axis=0)).then_inc(s_yr[t % 2], 16)
            for t in range(TT):
                add_shift(x1, lnb2, t, 2 * TT + t + 1)

        @block.scalar
        def _(act):
            act.dma_start(lng[:], in_g.partition_broadcast(P)).then_inc(s_lnp[0], 16)
            act.dma_start(lnb[:], in_b.partition_broadcast(P)).then_inc(s_lnp[0], 16)
            act.dma_start(nat[:, 0, :], ssm_a_re[0].rearrange("(g r) n -> g (r n)", r=2)).then_inc(s_prm, 16)
            act.dma_start(nat[:, 1, :], ssm_a_im[0].rearrange("(g r) n -> g (r n)", r=2)).then_inc(s_prm, 16)
            act.dma_start(ldt[:], ssm_log_dt[0].rearrange("(g r) -> g r", r=2)).then_inc(s_ldt, 16)
            for c, b_ in enumerate((ssm_b_re, ssm_b_im)):
                act.dma_start(braw[:, c, :, :], b_[0].rearrange("(g r) n h -> (r n) g h", r=2)).then_inc(s_prm, 16)
            for c, c_ in enumerate((ssm_c_re, ssm_c_im)):
                for twice in range(2):
                    act.dma_start(cnat[:, c, :, twice, :], c_[0].rearrange("(a g) h n -> (g h) a n", a=8))\
                       .then_inc(s_prm, 16)
            act.dma_start(dnat[:], ssm_d[0].rearrange("(g q) -> g q", q=2 * H)).then_inc(s_prm, 16)
            act.dma_start(cwn[:], conv_w[0].rearrange("w (a p) -> (w a) p", p=P)).then_inc(s_prm, 16)
            act.wait_ge(s_const, 4)
            act.dma_start(tok_d.rearrange("(p b) o -> p (b o)", p=P), zeros[:]).then_inc(s_zero, 16)

            def root(n):
                act.wait_ge(s_var, n + 1)

            def normalise(buf, t, n):
                act.wait_ge(s_rs, n)
                act.activation(buf[:, t, :], buf[:, t, :], ACT.Identity, bias=nmr[:, t:t + 1],
                               scale=rstd[:, t:t + 1]).then_inc(s_xn, 1)

            def rows_hi(t):
                for b in range(4):
                    act.wait_ge(s_tr, 4 * t + b + 1)
                    act.activation(xT_hi[:, 4 * b:4 * b + 4, t * P:(t + 1) * P],
                                   sets[t % 2][:, b, :].rearrange("p (k n) -> p k n", k=4), ACT.Copy)\
                       .then_inc(s_trh, 1)
                act.dma_start(x0_d[t * P:(t + 1) * P, :], xin[:, t, :]).then_inc(s_x0o, 16)

            act.wait_ge(s_const, 4)
            act.activation(ahead[:, 2:3], ident[:, 0:1], ACT.Copy).then_inc(s_yb, 1)

            for t in range(TT):
                root(t)
                act.activation(tmp4[:, t:t + 1], rstd[:, t:t + 1], ACT.Sqrt).then_inc(s_sq, 1)
                normalise(xin, t, t + 1)
                if t >= 2:
                    rows_hi(t - 2)
            rows_hi(2)
            rows_hi(3)

            def hi(q, s, whi_=whi, r=RD):
                act.wait_ge(s_raw[s], raw_count(q, s))
                if not isinstance(q, int) or q >= r:
                    act.wait_ge(s_used, q - r + 1)
                act.activation(whi_[:, s % r, :], raw[:, s, :], ACT.Copy).then_inc(s_hi, 1)

            def raw_count(q, s):
                return (q - s) * (16 // RAW) + 16

            copies = [0]

            def leave(rows, view_out, view_in, func, buf, earlier, stored):
                if earlier:
                    act.wait_ge(stored, 16 * earlier)
                copies[0] += 1
                act.activation(view_out, view_in, func).then_inc(s_cp, 1)
                act.wait_ge(s_cp, copies[0])
                act.dma_start(rows, buf).then_inc(stored, 16)

            def after(m):
                if m < 0 or (m % 2 == 0 and not Q_OA <= m < Q_G):
                    return
                n = unit_of(m)
                if m < Q_CONV:
                    act.wait_ge(s_used, m + 1)
                    for c in range(2):
                        leave(u_d[(2 * n + c) * P:(2 * n + c + 1) * P].rearrange("p j n -> p (j n)"),
                              ust[:, c, :].rearrange("p (j n) -> p j n", j=STEP),
                              dn[:, 2 * (n % 2) + c, :].rearrange("p (n j) -> p j n", j=STEP),
                              ACT.Copy, ust[:, c, :], n, s_ust[c])
                elif m < Q_OA:
                    i, part = (n - 4) // 3, (n - 4) % 3
                    if part == 0:
                        act.wait_ge(s_used, m + 1)
                        act.wait_ge(s_cm, i)
                        act.activation(cx[:], dn[:, 2 * (n % 2):2 * (n % 2) + 2, :], ACT.Copy).then_inc(s_cx, 1)
                    if part == 2:
                        if i == 0:
                            act.wait_ge(s_x0o, 16 * TT)
                        act.wait_ge(s_pa, i + 1)
                        act.activation(pa_hi[:, 2 * i:2 * i + 2, :], ct[:], ACT.Copy).then_inc(s_pah, 1)
                elif m < Q_G:
                    j = m - Q_OA
                    act.wait_ge(s_used, m + 1)
                    for c in range(2):
                        leave(ya_d[(2 * j + c) * P:(2 * j + c + 1) * P, :], ust[:, c, :],
                              dn[:, 2 * (n % 2) + c, :], ACT.Copy, ust[:, c, :], 4 + j, s_ust[c])
                else:
                    j = n - 24
                    act.wait_ge(s_used, m + 1)
                    for c in range(2):
                        leave(sg_d[(2 * j + c) * P:(2 * j + c + 1) * P, :], sgst[:, c, :],
                              dn[:, 2 * (n % 2) + c, :], ACT.Sigmoid, sgst[:, c, :], j, s_sgo[c])

            def c_ready():
                act.wait_ge(s_ctr, 1)
                for c in range(2):
                    for a in range(2):
                        for r in range(2):
                            rows = slice(r * N, (r + 1) * N)
                            last = act.activation(
                                Cc[rows, c, a * HG:(a + 1) * HG, :],
                                ex[rows, 2 * c + a, :].rearrange("p (g r h) -> p r g h", r=2, h=H)[:, r, :, :],
                                ACT.Copy)
                            last.then_inc(s_cc, 1)

            def v_ready(half, c):
                act.wait_ge(s_vtr, 2 * half + c + 1)
                if half == 0 and c == 0:
                    for tile in range(2):
                        act.wait_ge(s_ust[tile], 16 * 12)
                for b in range(4):
                    act.activation(V[:, c, 4 * b:4 * b + 4, :], ex[:, b, :], ACT.Copy).then_inc(s_v, 1)

            def chunk_inputs(half):
                act.wait_ge(s_bu, half + 1)
                for c in range(2):
                    for b in range(2):
                        act.activation(S[:, c, 8 * b:8 * b + 8, :], ex[:, 2 * c + b, :], ACT.Copy).then_inc(s_s, 1)

            def gelu_y(half):
                act.wait_ge(s_y, half + 1)
                for b in range(2):
                    for r in range(2):
                        act.activation(yst[:, 8 * b:8 * b + 8, r, :],
                                       ex[:, 2 * b + r, :].rearrange("p (g n) -> p g n", g=8),
                                       ACT.Gelu_apprx_tanh).then_inc(s_yg, 1)

            for q in range(Q_GLU):
                hi(q, q % RAW)
                after(q - 2)
                if q == 5:
                    c_ready()
                    act.wait_ge(s_ang, 1)
                    act.activation(prm[:, 10, :], prm[:, 8, :], ACT.Sin).then_inc(s_sin, 1)
                    act.activation(prm[:, 11, :], prm[:, 8, :], ACT.Sin, scale=0.5).then_inc(s_sin, 1)
                if q >= Q_G:
                    half, rel = divmod(q - Q_G, 16)
                    if rel == 6:
                        v_ready(half, 0)
                    if rel == 7:
                        v_ready(half, 1)
                    if rel == 8:
                        chunk_inputs(half)
                    if rel == 15:
                        gelu_y(half)
            hi(Q_GLU, 0)
            hi(Q_GLU + 1, 1)
            after(Q_GLU - 1)
            act.wait_ge(s_yl, 16)
            for k in range(8):
                act.activation(ys_hi[:, k, :].rearrange("p (n j) -> p j n", j=STEP),
                               yraw[:, k, :].rearrange("p (j n) -> p j n", j=STEP), ACT.Copy).then_inc(s_ysh, 1)

            for c in range(2):
                act.wait_ge(s_sgo[c], 16 * 16)
            with act.Fori(0, 4) as r:
                for i in range(2):
                    q = Q_GLU + 4 * r + 2 * i + 2
                    hi(q, (2 * i + 2) % RAW)
                    hi(q + 1, (2 * i + 3) % RAW)
                    j = r * 2 + i
                    act.wait_ge(s_used, j * 2 + (Q_GLU + 2))
                    act.wait_ge(s_gm, j + 1)
                    act.activation(sgt[:], dn[:, 2:4, :], ACT.Sigmoid).then_inc(s_sgt, 1)
                    act.wait_ge(s_gm, j + 2)
                    act.activation(mx_hi[:, bass.ds(2 * j, 2), :], gm[:], ACT.Copy).then_inc(s_mh, 1)
            with act.Fori(0, 3) as r:
                for i in range(4):
                    hi(Q_WO + 4 * r + i + 2, (i + 2) % RAW)
            hi(Q_WO + 14, 2)
            hi(Q_WO + 15, 3)

            act.wait_ge(s_used, Q_MOE)
            for i in range(3):
                hi(Q_MOE + i, i % RAW, mhi, RM)

            root(TT)
            act.activation(tmp4[:], rstd[:], ACT.Sqrt).then_inc(s_sq, 1)
            for t in range(TT):
                normalise(x1, t, TT + 1)
            for t in range(TT):
                act.wait_ge(s_rows, TT + t + 1)
                act.dma_start(x1_d[t * P:(t + 1) * P, :], x1[:, t, :]).then_inc(s_x1o, 16)
                for b in range(4):
                    act.wait_ge(s_x1t, 4 * t + b + 1)
                    if t >= 2 and b == 0:
                        act.wait_ge(s_log, t - 1)
                    act.activation(x1T[:, t % 2, 4 * b:4 * b + 4, :],
                                   sets[t % 2][:, b, :].rearrange("p (k n) -> p k n", k=4), ACT.Copy)\
                       .then_inc(s_x1c, 1)

            def block_rows_hi(n):
                for b in range(4):
                    act.wait_ge(s_xt, n + 1)
                    act.activation(xg_hi[:, 4 * b:4 * b + 4, :], ex[:, b, :].rearrange("p (k n) -> p k n", k=4),
                                   ACT.Copy).then_inc(s_xh, 1)

            def block(b):
                for i in range(3, PB + 3):
                    hi(Q_MOE + b * PB + i, i % RAW, mhi, RM)
                    if i == 10:
                        act.wait_ge(s_used, b * PB + (Q_MOE + 8))
                        act.wait_ge(s_hm, b * 2 + 1)
                        for c in range(2):
                            act.activation(sil[:, c * 512:(c + 1) * 512], dn[:, c, :], ACT.Silu)\
                               .then_inc(s_sil, 1)
                    if i == 18:
                        block_rows_hi(b + 1)
                        act.wait_ge(s_ht, b + 1)
                        for c in range(2):
                            act.activation(h_hi[:, 4 * c:4 * c + 4, :],
                                           ex[:, 2 + c, :].rearrange("p (k n) -> p k n", k=4), ACT.Copy)\
                               .then_inc(s_hh, 1)
                    if i == 22:
                        act.wait_ge(s_used, b * PB + (Q_MOE + 20))
                        act.wait_ge(s_x1o, b * 16 + 16 * TT)
                        act.activation(ybl[:, 0:1024].rearrange("p (c n) -> p c n", c=2), ex[:, 0:2, :], ACT.Copy).then_inc(s_yb, 1)
                act.wait_ge(s_used, b * PB + (Q_MOE + 24))
                act.activation(ybl[:, 1024:2048].rearrange("p (c n) -> p c n", c=2), ex[:, 2:4, :], ACT.Copy).then_inc(s_yb, 1)
                act.wait_ge(s_yb, b * 2 + 3)
                act.dma_start(yb_d[bass.ds(b * P, P), :], ybl[:]).then_inc(s_x1o, 16)

            block_rows_hi(0)
            with act.Fori(0, E) as b:
                block(b)
            act.wait_ge(s_tab, 1)
            blocks = act.value_load(tab[0:1, NBLK + 1:NBLK + 2], min_val=E, max_val=NBLK)
            with act.Fori(E, NBLK) as b:
                with act.If(b < blocks):
                    block(b)

            root(TT + 1)
            act.activation(tmp4[:], rstd[:], ACT.Sqrt).then_inc(s_sq, 1)
            for t in range(TT):
                normalise(x1, t, TT + 2)
            for t in range(TT):
                act.wait_ge(s_rows, 2 * TT + t + 1)
                act.dma_start(out[0, t * P:(t + 1) * P, :], x1[:, t, :]).then_inc(s_out, 16)
            act.wait_ge(s_out, 16 * TT)

        @block.vector
        def _(dve):
            lk = Link(dve, s_link)
            link = lk.link
            tt, ts, stt = dve.tensor_tensor, dve.tensor_scalar, dve.scalar_tensor_tensor

            def lo(q, s, whi_=whi, wlo_=wlo, r=RD):
                dve.wait_ge(s_hi, q + 1)
                tt(wlo_[:, s % r, :], raw[:, s, :], whi_[:, s % r, :].bitcast(F32), ALU.subtract).then_inc(s_lo, 1)

            def stats(buf, t):
                for c in range(4):
                    lk.go(dve.bn_stats(bst[:, t, c, :], buf[:, t, c * 512:(c + 1) * 512]))
                lk.wait()
                link(dve.bn_aggr(mv[:, t, :], bst[:, t, :, :]))

            def row_scale(sl, n):
                ts(rstd[:, sl], mv[:, sl, 1], EPS, None, ALU.add).then_inc(s_var, 1)
                dve.wait_ge(s_sq, n)
                link(dve.reciprocal(nmr[:, sl], tmp4[:, sl]))
                link(tt(tmp4[:, sl], rstd[:, sl], nmr[:, sl], ALU.mult))
                link(tt(tmp4[:, sl], tmp4[:, sl], nmr[:, sl], ALU.mult))
                link(ts(tmp4[:, sl], tmp4[:, sl], -0.5, 1.5, ALU.mult, ALU.add))
                link(tt(rstd[:, sl], nmr[:, sl], tmp4[:, sl], ALU.mult))
                stt(nmr[:, sl], mv[:, sl, 0], -1.0, rstd[:, sl], ALU.mult, ALU.mult).then_inc(s_rs, 1)

            def scale_rows(buf, gain, t, n):
                dve.wait_ge(s_xn, n)
                tt(buf[:, t, :], buf[:, t, :], gain[:], ALU.mult).then_inc(s_xm, 1)

            def rows_lo(t):
                for b in range(4):
                    dve.wait_ge(s_trh, 4 * t + b + 1)
                    tt(xT_lo[:, 4 * b:4 * b + 4, t * P:(t + 1) * P],
                       sets[t % 2][:, b, :].rearrange("p (k n) -> p k n", k=4),
                       xT_hi[:, 4 * b:4 * b + 4, t * P:(t + 1) * P].bitcast(F32), ALU.subtract)\
                        .then_inc(s_trl, 1)

            dve.memset(ahead[:, 0:1], 0.0).then_inc(s_gm, 1)
            dve.memset(ahead[:, 1:2], 0.0).then_inc(s_hm, 1)

            dve.wait_ge(s_lnp[0], 32)
            for t in range(TT + 1):
                if t < TT:
                    dve.wait_ge(s_x[t], 16)
                    stats(xin, t)
                    row_scale(slice(t, t + 1), t + 1)
                if t >= 1:
                    scale_rows(xin, lng, t - 1, t)
                if t >= 2:
                    rows_lo(t - 2)
            rows_lo(TT - 1)

            def exp_of(dst, src, xc, k, r, p):
                link(ts(xc, src, -87.0, 88.0, ALU.max, ALU.min))
                link(ts(k, xc, 1.0 / math.log(2.0), MAGIC, ALU.mult, ALU.add))
                link(ts(k, k, MAGIC, None, ALU.subtract))
                link(stt(r, k, -0.693359375, xc, ALU.mult, ALU.add))
                link(stt(r, k, 0.693359375 - math.log(2.0), r, ALU.mult, ALU.add))
                link(ts(p, r, 1.0 / math.factorial(8), None, ALU.mult))
                for d in range(7, 0, -1):
                    link(stt(p, p, 1.0 / math.factorial(d), r, ALU.add, ALU.mult))
                link(ts(p, p, 1.0, None, ALU.add))
                link(ts(xc.bitcast(I32), k, 127.0, 2.0 ** 23, ALU.add, ALU.mult))
                link(tt(p, p, xc.bitcast(F32), ALU.mult))
                link(stt(dst, src, -87.0, p, ALU.is_ge, ALU.mult))

            def v_(i):
                return prm[:, i, :]

            def cmul(o_re, o_im, a, b, x_, y_):
                link(tt(x_, a[0], b[0], ALU.mult))
                link(tt(y_, a[1], b[1], ALU.mult))
                link(tt(x_, x_, y_, ALU.subtract))
                link(tt(y_, a[0], b[1], ALU.mult))
                link(tt(o_im, a[1], b[0], ALU.mult))
                link(tt(o_im, o_im, y_, ALU.add))
                link(dve.tensor_copy(o_re, x_))

            def parameters_1():
                dve.wait_ge(s_ptr, 1)
                dve.tensor_copy(prm[:, 0:3, :], ex[:, 0, 0:3 * GG].rearrange("p (i g) -> p i g", i=3))\
                    .then_inc(s_pcp, 1)
                dve.tensor_copy(dgv[:], ex[0:2 * H, 0, 3 * GG:4 * GG]).then_inc(s_pcp, 1)
                dve.tensor_copy(cw[:], ex[:, 0, 4 * GG:4 * GG + 24].rearrange("p (w a) -> p a w", w=3)).then_inc(s_pcp, 1)
                dve.wait_ge(s_pcp, 3)
                exp_of(v_(3), v_(2), v_(21), v_(22), v_(23), v_(24))
                link(ts(v_(4), v_(0), -1e-4, None, ALU.min))
                link(tt(v_(19), v_(4), v_(3), ALU.mult))
                exp_of(v_(5), v_(19), v_(21), v_(22), v_(23), v_(24))
                link(tt(v_(6), v_(1), v_(3), ALU.mult))
                c1, c2, c3 = two_pi_parts()
                link(ts(v_(7), v_(6), 1.0 / (2 * math.pi), MAGIC, ALU.mult, ALU.add))
                link(ts(v_(7), v_(7), MAGIC, None, ALU.subtract))
                link(stt(v_(8), v_(7), -c1, v_(6), ALU.mult, ALU.add))
                link(stt(v_(8), v_(7), -c2, v_(8), ALU.mult, ALU.add))
                link(stt(v_(8), v_(7), -c3, v_(8), ALU.mult, ALU.add))
                ts(v_(8), v_(8), -3.1415925, 3.1415925, ALU.max, ALU.min).then_inc(s_ang, 1)

            def parameters_2():
                dve.wait_ge(s_sin, 2)
                link(tt(v_(12), v_(11), v_(11), ALU.mult))
                link(ts(v_(12), v_(12), -2.0, 1.0, ALU.mult, ALU.add))
                link(tt(A1[:, 0, :], v_(5), v_(12), ALU.mult))
                link(tt(A1[:, 2, :], v_(5), v_(10), ALU.mult))
                link(ts(A1[:, 1, :], A1[:, 2, :], -1.0, None, ALU.mult))
                link(tt(v_(15), v_(4), v_(4), ALU.mult))
                link(tt(v_(19), v_(1), v_(1), ALU.mult))
                link(tt(v_(15), v_(15), v_(19), ALU.add))
                link(dve.reciprocal(v_(15), v_(15)))
                link(ts(v_(16), A1[:, 0, :], -1.0, None, ALU.add))
                link(tt(v_(17), v_(16), v_(4), ALU.mult))
                link(tt(v_(19), A1[:, 2, :], v_(1), ALU.mult))
                link(tt(v_(17), v_(17), v_(19), ALU.add))
                link(tt(v_(17), v_(17), v_(15), ALU.mult))
                link(tt(v_(18), A1[:, 2, :], v_(4), ALU.mult))
                link(tt(v_(19), v_(16), v_(1), ALU.mult))
                link(tt(v_(18), v_(18), v_(19), ALU.subtract))
                link(tt(v_(18), v_(18), v_(15), ALU.mult))
                a = (A1[:, 0, :], A1[:, 2, :])
                cmul(v_(25), v_(26), a, a, v_(19), v_(20))
                b = (v_(25), v_(26))
                cmul(v_(27), v_(28), b, b, v_(19), v_(20))
                b = (v_(27), v_(28))
                cmul(P8[:, 0, 0, :], P8[:, 0, 2, :], b, b, v_(19), v_(20))

            def parameters_3():
                a8 = (P8[:, 0, 0, :], P8[:, 0, 2, :])
                for i in range(1, STEP):
                    cmul(P8[:, i, 0, :], P8[:, i, 2, :], (P8[:, i - 1, 0, :], P8[:, i - 1, 2, :]), a8,
                         v_(19), v_(20))
                link(ts(P8[:, :, 1, :], P8[:, :, 2, :], -1.0, None, ALU.mult))
                co_re = v_(17).unsqueeze(2).to_broadcast([P, GG, H])
                co_im = v_(18).unsqueeze(2).to_broadcast([P, GG, H])
                link(tt(Bb[:, 0, :, :], braw[:, 0, :, :], co_re, ALU.mult))
                link(tt(Bb[:, 1, :, :], braw[:, 1, :, :], co_im, ALU.mult))
                link(tt(Bb[:, 0, :, :], Bb[:, 0, :, :], Bb[:, 1, :, :], ALU.subtract))
                link(tt(braw[:, 0, :, :], braw[:, 0, :, :], co_im, ALU.mult))
                link(tt(Bb[:, 1, :, :], braw[:, 1, :, :], co_re, ALU.mult))
                link(tt(Bb[:, 1, :, :], Bb[:, 1, :, :], braw[:, 0, :, :], ALU.add))
                link(tt(dmask[:], ident[0:2 * H, 0:H], ident[0:2 * H, H:2 * H], ALU.add))
                link(tt(dsk[:], dgv[:].unsqueeze(2).to_broadcast([2 * H, GG, H]),
                        dmask[:].unsqueeze(1).to_broadcast([2 * H, GG, H]), ALU.mult))

            def times_a(dst, src, half, op, done=None):
                g = slice(half * HG, (half + 1) * HG)
                ar = A1[:, 0, g].unsqueeze(1).to_broadcast([P, 2, HG]).unsqueeze(3).to_broadcast([P, 2, HG, H])
                ai = A1[:, 1:3, g].unsqueeze(3).to_broadcast([P, 2, HG, H])
                lk.go(tt(t1[:], src, ar, ALU.mult))
                lk.go(tt(t2[:], src[:, ::-1], ai, ALU.mult))
                lk.wait()
                if done is None:
                    link(tt(dst, t1[:], t2[:], op))
                else:
                    tt(dst, t1[:], t2[:], op).then_inc(done, 1)

            def vt_steps(half, steps):
                for i in steps:
                    if i == STEP - 1:
                        g = slice(half * HG, (half + 1) * HG)
                        link(dve.tensor_copy(VT[:, :, :, i, :], Bb[:, :, g, :]))
                    else:
                        times_a(VT[:, :, :, i, :], VT[:, :, :, i + 1, :], half, ALU.add)

            def w_steps(half, steps, done=None):
                for d in steps:
                    if d == 0:
                        g = slice(half * HG, (half + 1) * HG)
                        lk.go(dve.tensor_copy(W[:, 0, :, 0, :], Cc[:, 0, g, :]))
                        lk.go(ts(W[:, 1, :, 0, :], Cc[:, 1, g, :], -1.0, None, ALU.mult))
                        lk.wait()
                    else:
                        times_a(W[:, :, :, d, :], W[:, :, :, d - 1, :], half, ALU.subtract, done)

            def block_diagonal(half):
                g = slice(half * HG, (half + 1) * HG)
                link(dve.memset(Bbd[:], 0.0))
                lk.go(dve.tensor_copy(Bbd[0:N, :, :, 0, :], Bb[0:N, :, g, :]))
                dve.tensor_copy(Bbd[N:P, :, :, 1, :], Bb[N:P, :, g, :]).then_inc(s_vt, 1)
                lk.wait()

            Sb = S[:].rearrange("p c g (b i) -> p c g b i", i=STEP)
            u1 = t1[:].rearrange("p c g h -> p (c g h)")
            u2 = t2[:].rearrange("p c g h -> p (c g h)")

            def advance(half, power, dst, src, nb, done=None):
                g = slice(half * HG, (half + 1) * HG)
                shape = [P, 2, HG, nb]
                ar = P8[:, power - 1, 0, g].unsqueeze(1).to_broadcast([P, 2, HG]).unsqueeze(3).to_broadcast(shape)
                ai = P8[:, power - 1, 1:3, g].unsqueeze(3).to_broadcast(shape)
                x_ = u1[:, 0:2 * HG * nb].rearrange("p (c g b) -> p c g b", c=2, g=HG)
                y_ = u2[:, 0:2 * HG * nb].rearrange("p (c g b) -> p c g b", c=2, g=HG)
                lk.go(tt(x_, src, ar, ALU.mult))
                lk.go(tt(y_, src[:, ::-1], ai, ALU.mult))
                lk.wait()
                link(tt(dst, dst, x_, ALU.add))
                if done is None:
                    link(tt(dst, dst, y_, ALU.add))
                else:
                    tt(dst, dst, y_, ALU.add).then_inc(done, 1)

            def scan_inside(half, steps):
                for i in steps:
                    advance(half, 1, Sb[:, :, :, :, i], Sb[:, :, :, :, i - 1], STEP)

            def scan_over(half):
                for b in range(1, STEP):
                    advance(half, STEP, Sb[:, :, :, b:b + 1, STEP - 1], Sb[:, :, :, b - 1:b, STEP - 1], 1)

            def scan_back(half, places, done=None):
                for i in places:
                    advance(half, i + 1, Sb[:, :, :, 1:STEP, i], Sb[:, :, :, 0:STEP - 1, STEP - 1], STEP - 1, done)

            def pad_k(half):
                dve.wait_ge(s_k, half + 1)
                lk.go(dve.memset(kpd[:, :, 0:7, :], 0.0))
                for b in range(4):
                    lk.go(dve.tensor_copy(kpd[:, 4 * b:4 * b + 4, 7:15, :],
                                          ex[0:2 * H, b, :].rearrange("p (g d h) -> p g d h", g=4, h=H)))
                lk.wait()
                tt(kpd[:, :, 7, :], kpd[:, :, 7, :], dsk[:, half * HG:(half + 1) * HG, :], ALU.add)\
                    .then_inc(s_kp, 1)

            def conv_after(m):
                n = unit_of(m)
                i, part = (n - 4) // 3, (n - 4) % 3
                b2 = dn[:, 2 * (n % 2):2 * (n % 2) + 2, :]
                if part == 1:
                    dve.wait_ge(s_cx, i + 1)
                    dve.wait_ge(s_used, m + 1)
                    tt(cv[:, :, 2:], b2, cx[:], ALU.mult).then_inc(s_cm, 1)
                    dve.wait_ge(s_cm, i + 1)
                    for k in range(CONV_WIDTH):
                        for c in range(2):
                            w_ = cw[:, 2 * i + c, k:k + 1]
                            v = cv[:, c, k:k + T]
                            lk.go(ts(ct[:, c, :], v, w_, None, ALU.mult) if k == 0 else
                                  stt(ct[:, c, :], v, w_, ct[:, c, :], ALU.mult, ALU.add))
                        lk.wait()
                if part == 2:
                    dve.wait_ge(s_used, m + 1)
                    tt(ct[:], ct[:], b2, ALU.mult).then_inc(s_pa, 1)
                    dve.wait_ge(s_pah, i + 1)
                    tt(pa_lo[:, 2 * i:2 * i + 2, :], ct[:], pa_hi[:, 2 * i:2 * i + 2, :].bitcast(F32),
                       ALU.subtract).then_inc(s_pal, 1)
                    dve.wait_ge(s_pal, i + 1)

            for q in range(Q_GLU):
                lo(q, q % RAW)
                m = q - 2
                if Q_CONV <= m < Q_OA and m % 2 == 1:
                    if m == Q_CONV + 3:
                        dve.wait_ge(s_cz, 1)
                        dve.wait_ge(s_prm, 16 * N_PRM)
                    conv_after(m)
                if q == 3:
                    parameters_1()
                if q == 6:
                    parameters_2()
                if q == 8:
                    dve.wait_ge(s_ybz, 16 * 2 * NOVER)
                    parameters_3()
                if q >= Q_G:
                    half, rel = divmod(q - Q_G, 16)
                    if rel == 1:
                        if half == 1:
                            dve.wait_ge(s_y, 1)
                            dve.wait_ge(s_yo, 16 * 8)
                        else:
                            dve.wait_ge(s_used, Q_G)
                        vt_steps(half, (7, 6, 5))
                    if rel == 2:
                        vt_steps(half, (4, 3, 2))
                    if rel == 3:
                        vt_steps(half, (1, 0))
                        block_diagonal(half)
                    if rel == 7:
                        dve.wait_ge(s_vtr, 2 * half + 2)
                        w_steps(half, (0, 1, 2, 3))
                    if rel == 8:
                        w_steps(half, (4, 5, 6))
                    if rel == 9:
                        w_steps(half, (7,))
                        w_steps(half, (8,), s_w)
                        dve.wait_ge(s_w, half + 1)
                        dve.wait_ge(s_s, 4 * (half + 1))
                        scan_inside(half, (1, 2, 3, 4))
                    if rel == 10:
                        scan_inside(half, (5, 6, 7))
                        scan_over(half)
                    if rel == 11:
                        pad_k(half)
                        scan_back(half, (0, 1, 2))
                    if rel == 12:
                        scan_back(half, (3, 4, 5))
                        scan_back(half, (6,), s_st)
                        dve.wait_ge(s_st, half + 1)
            lo(Q_GLU, 0)
            lo(Q_GLU + 1, 1)
            for k in range(8):
                dve.wait_ge(s_ysh, k + 1)
                tt(ys_lo[:, k, :].rearrange("p (n j) -> p j n", j=STEP),
                   yraw[:, k, :].rearrange("p (j n) -> p j n", j=STEP),
                   ys_hi[:, k, :].rearrange("p (n j) -> p j n", j=STEP).bitcast(F32), ALU.subtract)\
                    .then_inc(s_ysl, 1)

            base_n = lk.n
            with dve.Fori(0, 4) as r:
                for i in range(2):
                    q = Q_GLU + 4 * r + 2 * i + 2
                    lo(q, (2 * i + 2) % RAW)
                    lo(q + 1, (2 * i + 3) % RAW)
                    j = r * 2 + i
                    n = base_n + j * 3
                    dve.wait_ge(s_gin, j * 48 + 48)
                    dve.wait_ge(s_sgt, j + 1)
                    tt(gm[:], dn[:, 0:2, :], sgt[:], ALU.mult).then_inc(s_link, 1)
                    tt(gin[:, 0, :, :], gin[:, 0, :, :], gin[:, 1, :, :], ALU.mult).then_inc(s_link, 1)
                    dve.wait_ge(s_link, n + 1)
                    tt(gm[:], gm[:], gin[:, 2, :, :], ALU.mult).then_inc(s_link, 1)
                    dve.wait_ge(s_link, n + 3)
                    tt(gm[:], gm[:], gin[:, 0, :, :], ALU.add).then_inc(s_gm, 1)
                    dve.wait_ge(s_mh, j + 1)
                    tt(mx_lo[:, bass.ds(2 * j, 2), :], gm[:], mx_hi[:, bass.ds(2 * j, 2), :].bitcast(F32),
                       ALU.subtract).then_inc(s_ml, 1)
                    dve.wait_ge(s_ml, j + 1)
            lk.n = base_n + 24

            def residual(c, banks):
                for t in range(TT):
                    stt(x1[:, t, bass.ds(c * 512, 512)], x1[:, t, bass.ds(c * 512, 512)], ALPHA,
                        banks[:, t, :], ALU.mult, ALU.add).then_inc(s_wof, 1)
                dve.wait_ge(s_wof, c * 4 + 4)
                for t in range(TT):
                    dve.bn_stats(bst[:, t, bass.ds(c, 1), :].rearrange("p o s -> p (o s)"),
                                 x1[:, t, bass.ds(c * 512, 512)]).then_inc(s_bst, 1)

            def wo_chunk(c, banks):
                dve.wait_ge(s_used, Q_WO + 4 * c + 4)
                residual(c, banks)

            dve.wait_ge(s_res, 16)
            for c in range(3):
                for i in range(4):
                    lo(Q_WO + 4 * c + i + 2, (i + 2) % RAW)
                wo_chunk(c, (dn, ex)[c % 2])
            lo(Q_WO + 14, 2)
            lo(Q_WO + 15, 3)
            wo_chunk(3, ex)
            dve.wait_ge(s_bst, 16)
            for t in range(TT):
                lk.go(dve.bn_aggr(mv[:, t, :], bst[:, t, :, :]))
            lk.wait()
            row_scale(slice(0, TT), TT + 1)
            dve.wait_ge(s_lnp[1], 64)
            for t in range(TT):
                scale_rows(x1, lng1, t, TT + t + 1)
            for i in range(3):
                lo(Q_MOE + i, i % RAW, mhi, mlo, RM)

            def rv(i):
                return R[:, i, :, :]

            def rg(i):
                return R[:, i, :, :].rearrange("p t (g e) -> p t g e", e=EP)

            def rs(i):
                return R[:, i, :, 0:EG]

            def over_e(ap):
                return ap.unsqueeze(3).to_broadcast([P, TT, EG, EP])

            def over_16(ap):
                return ap.unsqueeze(2).to_broadcast([P, TT, E])

            dve.wait_ge(s_const2, 2)
            for t in range(TT):
                dve.wait_ge(s_log, t + 1)
                tt(R[:, 0, t, :], sets[t % 2][:, 0, 0:E], brb[:], ALU.add).then_inc(s_lgc, 1)
            dve.wait_ge(s_lgc, TT)
            one = R[:, 1, :, 0]
            link(dve.tensor_reduce(one, rv(0), AX.X, ALU.max))
            link(tt(rv(0), rv(0), over_16(one), ALU.subtract))
            exp_of(rv(2), rv(0), rv(3), rv(4), rv(5), rv(6))
            link(dve.tensor_reduce(one, rv(2), AX.X, ALU.add))
            link(dve.reciprocal(one, one))
            link(tt(rv(2), rv(2), over_16(one), ALU.mult))
            place_e = eio[:, 1, :].rearrange("p (g e) -> p g e", e=EP).unsqueeze(1).to_broadcast([P, TT, EG, EP])

            def first_max(p_, m, oh, w_):
                link(dve.tensor_reduce(rs(m), rg(p_), AX.X, ALU.max))
                link(tt(rg(w_), rg(p_), over_e(rs(m)), ALU.is_equal))
                link(tt(rg(w_), rg(w_), place_e, ALU.mult))
                link(dve.tensor_reduce(rs(23), rg(w_), AX.X, ALU.max))
                link(tt(rg(oh), rg(w_), over_e(rs(23)), ALU.is_equal))

            first_max(2, 7, 8, 9)
            link(stt(rv(10), rv(8), -2.0, rv(2), ALU.mult, ALU.add))
            first_max(10, 11, 12, 9)
            link(tt(rs(13), rs(7), rs(11), ALU.add))
            link(dve.tensor_reduce(one, rs(13), AX.X, ALU.max))
            link(tt(rs(14), rs(13), one.unsqueeze(2).to_broadcast([P, TT, EG]), ALU.is_equal))
            link(tt(rs(14), rs(14), gio[:].unsqueeze(1).to_broadcast([P, TT, EG]), ALU.mult))
            link(dve.tensor_reduce(one, rs(14), AX.X, ALU.max))
            link(tt(rs(15), rs(14), one.unsqueeze(2).to_broadcast([P, TT, EG]), ALU.is_equal))
            lk.go(tt(rg(16), rg(8), over_e(rs(15)), ALU.mult))
            lk.go(tt(rg(17), rg(12), over_e(rs(15)), ALU.mult))
            lk.wait()
            tt(rv(18), rv(16), rv(17), ALU.add).then_inc(s_msk, 1)
            link(tt(rs(13), rs(13), rs(15), ALU.mult))
            link(tt(rs(7), rs(7), rs(15), ALU.mult))
            link(tt(rs(11), rs(11), rs(15), ALU.mult))
            link(dve.tensor_reduce(one, rs(13), AX.X, ALU.add))
            link(dve.reciprocal(one, one))
            for k, i in enumerate((7, 11)):
                link(dve.tensor_reduce(R[:, 19, :, 0], rs(i), AX.X, ALU.add))
                link(tt(wts[:, :, k], R[:, 19, :, 0], one, ALU.mult))
            dve.wait_ge(s_rnk, 1)
            link(dve.tensor_copy(R[:, 20, :, :], dn[:, 3, 0:TT * E].rearrange("p (t e) -> p t e", t=TT)))
            cnt, ov, inc, kk = R[:, 21, 0, :], R[:, 21, 1, :], R[:, 21, 2, :], R[:, 21, 3, :]
            link(dve.tensor_copy(cnt, dn[:, 3, TT * E:(TT + 1) * E]))
            link(ts(ov, cnt, float(P), None, ALU.is_gt))
            for m in (2, 3):
                link(stt(ov, cnt, float(m * P), ov, ALU.is_gt, ALU.add))
            link(dve.tensor_tensor_scan(inc, ones[:, 0:E], ov, 0.0, ALU.mult, ALU.add))
            link(tt(kk, inc, ov, ALU.subtract))
            link(stt(kk, kk, float(P), eio[:, 2, :], ALU.mult, ALU.add))
            link(ts(rv(22), rv(20), float(P), None, ALU.is_ge))
            link(tt(rv(22), rv(22), kk.unsqueeze(1).to_broadcast([P, TT, E]), ALU.mult))
            link(tt(rv(22), rv(22), rv(20), ALU.add))
            link(stt(rv(22), eio[:, 0, :].unsqueeze(1).to_broadcast([P, TT, E]), float(P), rv(22),
                     ALU.mult, ALU.add))
            for k, i in enumerate((16, 17)):
                link(tt(rv(9), rv(i), rv(22), ALU.mult))
                link(dve.tensor_reduce(R[:, 19, :, k], rv(9), AX.X, ALU.add))
            dve.tensor_copy(dest[:], R[:, 19, :, 0:2]).then_inc(s_dst, 1)
            link(tt(ovk[:], inc.unsqueeze(1).to_broadcast([P, NOVER + 1, E]),
                    ovn[:].unsqueeze(2).to_broadcast([P, NOVER + 1, E]), ALU.is_le))
            link(dve.tensor_reduce(R[:, 23, 0, 0:NOVER + 1], ovk[:], AX.X, ALU.add))
            link(ts(R[:, 23, 0, 0:NOVER + 1], R[:, 23, 0, 0:NOVER + 1], float(E - 1), None, ALU.min))
            lk.go(dve.tensor_copy(tab[:, 0:E], eio[:, 0, :]))
            lk.go(dve.tensor_copy(tab[:, E:NBLK + 1], R[:, 23, 0, 0:NOVER + 1]))
            lk.wait()
            ts(tab[:, NBLK + 1:NBLK + 2], inc[:, E - 1:E], float(E), None, ALU.add).then_inc(s_tab, 1)

            def block_rows_lo(n):
                for b in range(4):
                    dve.wait_ge(s_xh, n * 4 + b + 1)
                    tt(xg_lo[:, 4 * b:4 * b + 4, :], ex[:, b, :].rearrange("p (k n) -> p k n", k=4),
                       xg_hi[:, 4 * b:4 * b + 4, :].bitcast(F32), ALU.subtract).then_inc(s_xl, 1)

            def block(b):
                for i in range(3, PB + 3):
                    lo(Q_MOE + b * PB + i, i % RAW, mhi, mlo, RM)
                    if i == 18:
                        dve.wait_ge(s_used, b * PB + (Q_MOE + 16))
                        for c in range(2):
                            dve.wait_ge(s_sil, b * 2 + c + 1)
                            tt(hid[:, c * 512:(c + 1) * 512], sil[:, c * 512:(c + 1) * 512], dn[:, 2 + c, :],
                               ALU.mult).then_inc(s_hm, 1)
                        block_rows_lo(b + 1)
                        for c in range(2):
                            dve.wait_ge(s_hh, b * 2 + c + 1)
                            tt(h_lo[:, 4 * c:4 * c + 4, :], ex[:, 2 + c, :].rearrange("p (k n) -> p k n", k=4),
                               h_hi[:, 4 * c:4 * c + 4, :].bitcast(F32), ALU.subtract).then_inc(s_hl, 1)

            block_rows_lo(0)
            with dve.Fori(0, E) as b:
                block(b)
            blocks = dve.value_load(tab[0:1, NBLK + 1:NBLK + 2], min_val=E, max_val=NBLK)
            with dve.Fori(E, NBLK) as b:
                with dve.If(b < blocks):
                    block(b)

            dve.wait_ge(s_xa, TT)
            for t in range(TT):
                dve.wait_ge(s_yr[t % 2], 32 * (t // 2 + 1))
                link(stt(x1[:, t, :], yg[:, t % 2, 0, :], wts[:, t, 0:1], x1[:, t, :], ALU.mult, ALU.add))
                stt(x1[:, t, :], yg[:, t % 2, 1, :], wts[:, t, 1:2], x1[:, t, :], ALU.mult, ALU.add).then_inc(s_ygf, 1)
                dve.wait_ge(s_ygf, t + 1)
                stats(x1, t)
            row_scale(slice(0, TT), TT + 2)
            dve.wait_ge(s_lnp[2], 32)
            for t in range(TT):
                scale_rows(x1, lng2, t, 2 * TT + t + 1)

        @block.tensor
        def _(pe):
            pe.wait_ge(s_const, 4)
            for t in range(TT):
                pe.wait_ge(s_rows, t + 1)
                for b in range(4):
                    if t >= 2:
                        pe.wait_ge(s_trl, 4 * (t - 2) + b + 1)
                    for k in range(4):
                        mm = pe.transpose(sets[t % 2][:, b, k * P:(k + 1) * P],
                                          xin[:, t, (4 * b + k) * P:(4 * b + k + 1) * P], ident[:])
                    mm.then_inc(s_tr, 1)

            def three(o, w, wl, r_, rl, first, last):
                pe.matmul(o, lhsT=w, rhs=r_, start=first, stop=False)
                pe.matmul(o, lhsT=w, rhs=rl, start=False, stop=False)
                return pe.matmul(o, lhsT=wl, rhs=r_, start=False, stop=last)

            def unit_piece(q, s, par, rhs, k0, first, last):
                hi_, lo_ = rhs
                h = whi[:, s % RD, :].rearrange("p (k n) -> p k n", k=8)
                l = wlo[:, s % RD, :].rearrange("p (k n) -> p k n", k=8)
                pe.wait_ge(s_lo, q + 1)
                for k in range(8):
                    for c in range(2):
                        cs = slice(c * P, (c + 1) * P)
                        mm = three(dn[:, 2 * par + c, :], h[:, k, cs], l[:, k, cs],
                                   hi_[:, k0 + k, :], lo_[:, k0 + k, :], first and k == 0, last and k == 7)
                mm.then_inc(s_used, 1)

            def banks_free(n):
                if n < 2:
                    return
                m = n - 2
                if m < 4:
                    pe.wait_ge(s_cp, 2 * (m + 1))
                elif m < 16:
                    pe.wait_ge((s_cx, s_cm, s_pa)[(m - 4) % 3], (m - 4) // 3 + 1)
                elif m < 40:
                    pe.wait_ge(s_cp, 8 + 2 * (m - 15))

            def parameter_transposes():
                pe.wait_ge(s_prm, 16 * N_PRM)
                pe.wait_ge(s_trl, 16)
                pe.wait_ge(s_nat, 1)
                for i in range(3):
                    pe.transpose(ex[:, 0, i * GG:(i + 1) * GG], nat[:, i, :], ident[0:GG, 0:GG])
                pe.transpose(ex[0:2 * H, 0, 3 * GG:4 * GG], dnat[:], ident[0:GG, 0:GG])
                mm = pe.transpose(ex[:, 0, 4 * GG:4 * GG + 24], cwn[:], ident[0:24, 0:24])
                mm.then_inc(s_ptr, 1)

            def c_transposes():
                pe.wait_ge(s_pcp, 3)
                for c in range(2):
                    for a in range(8):
                        mm = pe.transpose(ex[:, 2 * c + a // 4, (a % 4) * P:(a % 4 + 1) * P],
                                          cnat[:, c, a, :, :].rearrange("p o n -> p (o n)"), ident[:])
                mm.then_inc(s_ctr, 1)

            def vt_transposes(half, c):
                if c == 0:
                    pe.wait_ge(s_vt, half + 1)
                    if half == 0:
                        pe.wait_ge(s_cc, 8)
                    else:
                        pe.wait_ge(s_yg, 4)
                else:
                    pe.wait_ge(s_v, 8 * half + 4)
                for g in range(HG):
                    mm = pe.transpose(ex[:, g // 4, (g % 4) * P:(g % 4 + 1) * P],
                                      VT[:, c, g, :, :].rearrange("p i h -> p (i h)"), ident[:])
                mm.then_inc(s_vtr, 1)

            def chunk_inputs(half):
                pe.wait_ge(s_u, 16 * 8 * (half + 1))
                pe.wait_ge(s_v, 8 * (half + 1))
                for c in range(2):
                    for g in range(HG):
                        for r in range(2):
                            slot = c * HG + g
                            mm = pe.matmul(ex[r * N:(r + 1) * N, slot // 8, (slot % 8) * NCH:(slot % 8 + 1) * NCH],
                                           lhsT=V[:, c, g, r * N:(r + 1) * N], rhs=U[:, 2 * g + r, :],
                                           start=True, stop=True)
                mm.then_inc(s_bu, 1)

            def kernels(half):
                pe.wait_ge(s_w, half + 1)
                pe.wait_ge(s_s, 4 * (half + 1))
                for g in range(HG):
                    for c in range(2):
                        mm = pe.matmul(ex[0:2 * H, g // 4, (g % 4) * P:(g % 4 + 1) * P],
                                       lhsT=Bbd[:, c, g, :, :].rearrange("p r h -> p (r h)"),
                                       rhs=W[:, c, g, 0:STEP, :].rearrange("p d h -> p (d h)"),
                                       start=(c == 0), stop=(c == 1))
                mm.then_inc(s_k, 1)

            def outputs(half):
                pe.wait_ge(s_st, half + 1)
                pe.wait_ge(s_m, 16 * 8 * (half + 1))
                pe.wait_ge(s_kp, half + 1)
                for g in range(HG):
                    for r in range(2):
                        o = ex[:, 2 * (g // 8) + r, (g % 8) * NCH:(g % 8 + 1) * NCH]
                        rows = slice(r * N, (r + 1) * N)
                        pe.matmul(o, lhsT=M[:, g, r, :], rhs=U[:, 2 * g + r, :], start=True, stop=False)
                        for c in range(2):
                            mm = pe.matmul(o[:, 1:], lhsT=W[rows, c, g, 1:, :].rearrange("p d h -> p (d h)"),
                                           rhs=S[rows, c, g, 0:NCH - 1], start=False, stop=(c == 1))
                mm.then_inc(s_y, 1)

            pe.wait_ge(s_trl, 16)
            for q in range(Q_GLU):
                n = unit_of(q)
                if q < Q_OA or q >= Q_G:
                    if q % 2 == 0:
                        banks_free(n)
                    unit_piece(q, q % RAW, n % 2, (xT_hi, xT_lo), 8 * (q % 2), q % 2 == 0, q % 2 == 1)
                else:
                    banks_free(n)
                    if q == Q_OA:
                        pe.wait_ge(s_pal, 4)
                    unit_piece(q, q % RAW, n % 2, (pa_hi, pa_lo), 0, True, True)
                if q == 1:
                    parameter_transposes()
                if q == 3:
                    c_transposes()
                if q >= Q_G:
                    half, rel = divmod(q - Q_G, 16)
                    if rel == 4:
                        vt_transposes(half, 0)
                    if rel == 5:
                        vt_transposes(half, 1)
                    if rel == 6:
                        chunk_inputs(half)
                    if rel == 9:
                        kernels(half)
                    if rel == 13:
                        outputs(half)
            pe.wait_ge(s_ysl, 8)
            with pe.Fori(0, 4) as r:
                for i in range(2):
                    j = r * 2 + i
                    q = j * 2 + Q_GLU
                    if i == 0:
                        pe.wait_ge(s_cp, 56)
                    pe.wait_ge(s_gm, j + 1)
                    unit_piece(q, (2 * i) % RAW, 0, (ys_hi, ys_lo), 0, True, True)
                    unit_piece(q + 1, (2 * i + 1) % RAW, 1, (ys_hi, ys_lo), 0, True, True)

            pe.wait_ge(s_ml, 8)
            pe.wait_ge(s_yg, 8)
            for c in range(4):
                banks = (dn, ex)[c % 2]
                if c >= 2:
                    pe.wait_ge(s_wof, 4 * (c - 1))
                for i in range(4):
                    q = Q_WO + 4 * c + i
                    h = whi[:, q % RD, :].rearrange("p (k n) -> p k n", k=4)
                    l = wlo[:, q % RD, :].rearrange("p (k n) -> p k n", k=4)
                    pe.wait_ge(s_lo, q + 1)
                    for k in range(4):
                        kk = 4 * i + k
                        for t in range(TT):
                            ts_ = slice(t * P, (t + 1) * P)
                            mm = tokens_by(pe, banks[:, t, :], mx_hi[:, kk, ts_], mx_lo[:, kk, ts_],
                                           h[:, k, :], l[:, k, :], kk == 0, kk == KD - 1)
                    mm.then_inc(s_used, 1)

            def router(t):
                pe.wait_ge(s_x1c, 4 * t + 4)
                for k in range(KD):
                    mm = pe.matmul(sets[t % 2][:, 0, 0:E], lhsT=x1T[:, t % 2, k, :], rhs=wr[:, k, :],
                                   start=(k == 0), stop=(k == KD - 1))
                mm.then_inc(s_log, 1)

            pe.wait_ge(s_wof, 16)
            pe.wait_ge(s_lnp[1], 64)
            for t in range(TT):
                pe.wait_ge(s_rows, TT + t + 1)
                if t >= 2:
                    pe.wait_ge(s_lgc, t - 1)
                for b in range(4):
                    for k in range(4):
                        mm = pe.transpose(sets[t % 2][:, b, k * P:(k + 1) * P],
                                          x1[:, t, (4 * b + k) * P:(4 * b + k + 1) * P], ident[:])
                    mm.then_inc(s_x1t, 1)
                if t >= 1:
                    router(t - 1)
            router(TT - 1)
            pe.wait_ge(s_const2, 2)
            pe.wait_ge(s_msk, 1)
            for t in range(TT + 1):
                o = dn[:, 3, t * E:(t + 1) * E]
                for t_ in range(t):
                    mm = pe.matmul(o, lhsT=ones[:], rhs=R[:, 18, t_, :], start=(t_ == 0), stop=(t_ == t - 1 and t == TT))
                if t < TT:
                    mm = pe.matmul(o, lhsT=tri[:], rhs=R[:, 18, t, :], start=(t == 0), stop=True)
            mm.then_inc(s_rnk, 1)

            def rows_transpose(n):
                pe.wait_ge(s_xg, n * 16 + 16)
                for k in range(KD):
                    mm = pe.transpose(ex[:, k // 4, (k % 4) * P:(k % 4 + 1) * P], xg[:, k * P:(k + 1) * P], ident[:])
                mm.then_inc(s_xt, 1)

            def expert_matmuls(q, s, banks, xh, xl, k0, first, last):
                h = mhi[:, s % RM, :].rearrange("p (k n) -> p k n", k=2)
                l = mlo[:, s % RM, :].rearrange("p (k n) -> p k n", k=2)
                pe.wait_ge(s_lo, q + 1)
                for k in range(2):
                    for c in range(2):
                        cs = slice(c * 512, (c + 1) * 512)
                        mm = tokens_by(pe, banks[c], xh[:, k0 + k, :], xl[:, k0 + k, :], h[:, k, cs], l[:, k, cs],
                                       first and k == 0, last and k == 1)
                mm.then_inc(s_used, 1)

            def expert_piece(b, i):
                q = Q_MOE + b * PB + i
                i = i % PB
                if i < 16:
                    banks = [dn[:, 2 * (i // 8) + c, :] for c in range(2)]
                    expert_matmuls(q, i % RAW, banks, xg_hi, xg_lo, 2 * (i % 8), i % 8 == 0, i % 8 == 7)
                else:
                    banks = [ex[:, 2 * ((i - 16) // 4) + c, :] for c in range(2)]
                    expert_matmuls(q, i % RAW, banks, h_hi, h_lo, 2 * (i % 4), i % 4 == 0, i % 4 == 3)

            def block(b):
                for i in range(3, 16):
                    expert_piece(b, i)
                pe.wait_ge(s_yb, b * 2 + 1)
                rows_transpose(b + 1)
                pe.wait_ge(s_hm, b * 2 + 3)
                pe.wait_ge(s_xl, b * 4 + 8)
                for k in range(KF):
                    mm = pe.transpose(ex[:, 2 + k // 4, (k % 4) * P:(k % 4 + 1) * P],
                                      hid[:, k * P:(k + 1) * P], ident[:])
                mm.then_inc(s_ht, 1)
                pe.wait_ge(s_hl, b * 2 + 2)
                for i in range(16, PB + 3):
                    expert_piece(b, i)

            pe.wait_ge(s_dst, 1)
            rows_transpose(0)
            pe.wait_ge(s_xl, 4)
            for i in range(3):
                expert_piece(0, i)
            with pe.Fori(0, E) as b:
                block(b)
            pe.wait_ge(s_tab, 1)
            blocks = pe.value_load(tab[0:1, NBLK + 1:NBLK + 2], min_val=E, max_val=NBLK)
            with pe.Fori(E, NBLK) as b:
                with pe.If(b < blocks):
                    block(b)


_INS = ["x", "in_g", "in_b", "w_in", "conv_w", "w_out_a", "ssm_a_re", "ssm_a_im", "ssm_log_dt",
        "ssm_b_re", "ssm_b_im", "ssm_c_re", "ssm_c_im", "ssm_d", "w_glu", "w_o",
        "ln1_g", "ln1_b", "ln2_g", "ln2_b", "w_router", "b_router", "w_gate", "w_up", "w_down"]


def kernel(**inputs):
    import numpy as _np
    import concourse.bacc as _bacc
    from concourse import mybir as _mybir
    from concourse.bass_utils import run_bass_kernel_spmd as _run

    nc = _bacc.Bacc("TRN2", target_bir_lowering=False, num_devices=1)
    arrays, args = {}, []
    for name in _INS:
        a = _np.ascontiguousarray(inputs[name])
        arrays[f"in_{name}"] = a
        args.append(nc.dram_tensor(f"in_{name}", a.shape, _mybir.dt.from_np(a.dtype), kind="ExternalInput").ap())
    out = nc.dram_tensor("out", (1, T, D), _mybir.dt.float32, kind="ExternalOutput").ap()
    build_trunk(nc, *args, out)
    r = _run(nc, [arrays], core_ids=[0])
    return r.results[0]["out"]
```

```python
import math

import numpy as np

import concourse.bass as bass
from concourse import mybir
from contextlib import ExitStack

F32 = mybir.dt.float32
F32R = mybir.dt.float32r
I32 = mybir.dt.int32
BF16 = mybir.dt.bfloat16
ALU = mybir.AluOpType
ACT = mybir.ActivationFunctionType
AX = mybir.AxisListType

P = 128
T = 512
D = 2048
DC = 1024
DS = 1024
CONV_WIDTH = 3
G, H, N = 64, 16, 64
E, EG, EP = 16, 4, 4
F = 1024
EPS = 1e-5
ALPHA = 2.0 ** 0.25
TT = T // P
KD = D // P
KF = F // P
PIECE = 2048
UC = 256

STEP = 8
NCH = T // STEP
GG = G // 2
HG = GG // 2

N_U, N_CONV, N_OA, N_G, N_GLU, N_WO = 8, 24, 8, 32, 16, 16
Q_CONV = 0
Q_U = Q_CONV + N_CONV
Q_OA = Q_U + N_U
Q_G = Q_OA + N_OA
Q_GLU = Q_G + N_G
Q_WO = Q_GLU + N_GLU
Q_MOE = Q_WO + N_WO
PB = 24
NBLK = E + (2 * T - E) // P
NOVER = NBLK - E
RAW = 4
RD = 2
RM = 4
RAWM = 8

N_PRM = 10

MAGIC = 1.5 * 2.0 ** 23


def two_pi_parts():
    c1 = math.floor(2 * math.pi * 2 ** 7) / 2 ** 7
    c2 = math.floor((2 * math.pi - c1) * 2 ** 19) / 2 ** 19
    return c1, c2, 2 * math.pi - c1 - c2


class Link:

    def __init__(self, eng, sem):
        self.eng, self.sem, self.n = eng, sem, 0

    def go(self, ins):
        self.n += 1
        ins.then_inc(self.sem, 1)

    def wait(self):
        self.eng.wait_ge(self.sem, self.n)

    def link(self, ins):
        self.go(ins)
        self.wait()


def unit_of(q):
    if q < Q_OA:
        return q // 2
    return 16 + q - Q_OA if q < Q_G else 24 + (q - Q_G) // 2


def tokens_by(pe, o, x_hi, x_lo, w_hi, w_lo, first, last):
    pe.matmul(o, lhsT=x_hi, rhs=w_hi, start=first, stop=False)
    pe.matmul(o, lhsT=x_lo, rhs=w_hi, start=False, stop=False)
    return pe.matmul(o, lhsT=x_hi, rhs=w_lo, start=False, stop=last)


def build_trunk(nc, x, in_g, in_b, w_in, conv_w, w_out_a, ssm_a_re, ssm_a_im, ssm_log_dt,
                ssm_b_re, ssm_b_im, ssm_c_re, ssm_c_im, ssm_d, w_glu, w_o,
                ln1_g, ln1_b, ln2_g, ln2_b, w_router, b_router, w_gate, w_up, w_down, out):
    ctx = ExitStack()
    with ctx:
        base = nc.sbuf_base + (-nc.sbuf_base) % 64
        KB = 1024

        def at(name, shape, kb, dtype=F32):
            return nc.alloc_sbuf_tensor_at(name, shape, dtype, offset=base + int(kb * KB))


        raw = at("raw", [P, RAW, PIECE], 0)
        whi = at("whi", [P, RD, PIECE], 32, F32R)
        wlo = at("wlo", [P, RD, PIECE], 48, F32R)
        mhi = at("mhi", [P, RM, PIECE], 32, F32R)
        mlo = at("mlo", [P, RM, PIECE], 64, F32R)
        xT_hi = at("xT_hi", [P, KD, T], 64, F32R)
        xT_lo = at("xT_lo", [P, KD, T], 96, F32R)
        mx_hi = at("mx_hi", [P, KD, T], 64, F32R)
        mx_lo = at("mx_lo", [P, KD, T], 96, F32R)
        xin = at("xin", [P, TT, D], 128)
        lng = at("lng", [P, D], 160)
        lnb = at("lnb", [P, D], 168)
        pa_hi = at("pa_hi", [P, 8, T], 128, F32R)
        pa_lo = at("pa_lo", [P, 8, T], 144, F32R)
        ust = at("ust", [P, 2, T], 160)
        cx = at("cx", [P, 2, T], 164)
        cv = at("cv", [P, 2, T + 2], 168)
        ct = at("ct", [P, 2, T], 172.5)
        zrow = at("zrow", [P, 1024], 194)
        cnat = at("cnat", [P, 2, 8, 2, N], 176.5)
        prm = at("prm", [P, 30, GG], 184.5)
        nat = at("nat", [GG, 3, P], 188.25)
        braw = at("braw", [P, 2, GG, H], 189.75)
        Bb = at("Bb", [P, 2, GG, H], 194)
        Cc = at("Cc", [P, 2, GG, H], 198)
        A1 = at("A1", [P, 3, GG], 202)
        P8 = at("P8", [P, STEP, 3, GG], 202.375)
        VT = at("VT", [P, 2, HG, STEP, H], 128)
        W = at("W", [P, 2, HG, STEP + 1, H], 128)
        V = at("V", [P, 2, HG, P], 146)
        kpd = at("kpd", [2 * H, HG, 15, H], 146)
        M = at("M", [P, HG, 2, P], 146)
        U = at("U", [P, 2 * HG, NCH], 162)
        S = at("S", [P, 2, HG, NCH], 170)
        t1 = at("t1", [P, 2, HG, H], 178)
        t2 = at("t2", [P, 2, HG, H], 180)
        Bbd = at("Bbd", [P, 2, HG, 2, H], 182)
        yst = at("yst", [P, HG, 2, NCH], 178)
        sgst = at("sgst", [P, 2, T], 186)
        dgv = at("dgv", [2 * H, GG], 193.75)
        dmask = at("dmask", [2 * H, H], 193.875)
        dsk = at("dsk", [2 * H, GG, H], 190)
        ys_hi = at("ys_hi", [P, 8, T], 128, F32R)
        ys_lo = at("ys_lo", [P, 8, T], 144, F32R)
        yraw = at("yraw", [P, 8, T], 160)
        gin = at("gin", [P, 3, 2, T], 176)
        sgt = at("sgt", [P, 2, T], 188)
        gm = at("gm", [P, 2, T], 192)
        x1 = at("x1", [P, TT, D], 128)
        lng1 = at("lng1", [P, D], 160)
        lnb1 = at("lnb1", [P, D], 168)
        x1T = at("x1T", [P, 2, KD, P], 176)
        wr = at("wr", [P, KD, E], 196)
        tri = at("tri", [P, P], 197, BF16)
        onesb = at("onesb", [P, P], 197.25, BF16)
        mask = at("mask", [P, TT, E], 197.5, BF16)
        ones = at("ones", [P, E], 197.75)
        square = at("square", [P, P], 198.5)
        brb = at("brb", [P, E], 198)
        eio = at("eio", [P, 3, E], 198.125)
        gio = at("gio", [P, EG], 198.375)
        R = at("R", [P, 24, TT, E], 198.5)
        RI = at("RI", [P, TT, E], 204.5, I32)
        ovk = at("ovk", [P, NOVER + 1, E], 194)
        ovn = at("ovn", [P, NOVER + 1], 195.5)
        xg_hi = at("xg_hi", [P, KD, P], 104, F32R)
        xg_lo = at("xg_lo", [P, KD, P], 112, F32R)
        sil = at("sil", [P, F], 120)
        hid = at("hid", [P, F], 124)
        raw2 = at("raw2", [P, RAWM - RAW, PIECE], 128)
        h_hi = at("h_hi", [P, KF, P], 160, F32R)
        h_lo = at("h_lo", [P, KF, P], 164, F32R)
        ybl = at("ybl", [P, D], 168)
        xg = at("xg", [P, D], 176)
        xr = at("xr", [P, TT, D], 0)
        lng2 = at("lng2", [P, D], 128)
        lnb2 = at("lnb2", [P, D], 136)
        yg = at("yg", [P, TT, 2, D], 32)
        place = [205.5]

        def small(name, shape, dtype=F32):
            t = at(name, shape, place[0], dtype)
            words = 1
            for n in shape[1:]:
                words *= n
            place[0] += math.ceil(words * 4 / 32) * 32 / KB
            return t

        ident = small("ident", [P, P])
        cwn = small("cwn", [CONV_WIDTH * 8, P])
        dnat = small("dnat", [GG, 2 * H])
        ldt = small("ldt", [GG, 2])
        cw = small("cw", [P, 8, 3])
        mv = small("mv", [P, TT, 2])
        rstd = small("rstd", [P, TT])
        nmr = small("nmr", [P, TT])
        tmp4 = small("tmp4", [P, TT])
        bst = small("bst", [P, TT, 4, 6])
        tab = small("tab", [P, 32], I32)
        dest = small("dest", [P, TT, 2], I32)
        back = small("back", [P, TT, 2], I32)
        wts = small("wts", [P, TT, 2])
        bidx = small("bidx", [P, 1], I32)
        ahead = small("ahead", [P, 4])
        zeros = small("zeros", [P, NBLK + 1], I32)
        tokid = small("tokid", [P, TT], I32)
        assert base + place[0] * KB <= nc.sbuf_usable_end, (base + place[0] * KB, nc.sbuf_usable_end)

        dn = ctx.enter_context(nc.psum_tensor("dn", [P, 4, 512], F32))
        ex = ctx.enter_context(nc.psum_tensor("ex", [P, 4, 512], F32))
        sets = (ex, dn)

        x0_d = nc.dram_tensor("x0_d", [T, D], F32).ap()
        u_d = nc.dram_tensor("u_d", [DS, STEP, NCH], F32).ap()
        ya_d = nc.dram_tensor("ya_d", [D, T], F32).ap()
        sg_d = nc.dram_tensor("sg_d", [2 * D, T], F32).ap()
        kp_d = nc.dram_tensor("kp_d", [GG, 2, H, 15 * H], F32).ap()
        y_d = nc.dram_tensor("y_d", [DS, STEP, NCH], F32).ap()
        x1_d = nc.dram_tensor("x1_d", [T, D], F32).ap()
        tok_d = nc.dram_tensor("tok_d", [(NBLK + 1) * P, 1], I32).ap()
        yb_d = nc.dram_tensor("yb_d", [NBLK * P, D], F32).ap()

        def sem(name):
            return ctx.enter_context(nc.semaphore(name))

        s_raw = [sem(f"raw_loaded{i}") for i in range(RAW)]
        s_rawm = [sem(f"expert_piece_loaded{i}") for i in range(RAWM)]
        s_hi = sem("hi_written")
        s_lo = sem("lo_written")
        s_used = sem("piece_used")
        s_link = sem("vector_link")
        s_plink = sem("pool_link")
        s_const = sem("constants_built")
        s_const2 = sem("router_constants_built")
        s_x = [sem(f"x_loaded{i}") for i in range(TT)]
        s_lnp = [sem("ln0_loaded"), sem("ln1_loaded"), sem("ln2_loaded")]
        s_prm = sem("parameters_loaded")
        s_ldt = sem("log_dt_loaded")
        s_nat = sem("log_dt_spread")
        s_zero = sem("token_table_cleared")
        s_ybz = sem("overflow_rows_cleared")
        s_var = sem("variance_ready")
        s_sq = sem("root_ready")
        s_rs = sem("row_scale_ready")
        s_xn = sem("rows_normalised")
        s_xm = sem("rows_scaled")
        s_rows = [sem(f"rows_ready{i}") for i in range(TT)]
        s_tr = sem("rows_transposed")
        s_trh = sem("transposed_hi")
        s_trl = sem("transposed_lo")
        s_x0o = sem("x0_stored")
        s_cp = sem("copied_out")
        s_ust = [sem("ust_stored0"), sem("ust_stored1")]
        s_sgo = [sem("gate_stored0"), sem("gate_stored1")]
        s_cx = sem("xin_copied")
        s_pa = sem("conv_ready")
        s_pah = sem("conv_hi")
        s_pal = sem("conv_lo")
        s_ptr = sem("parameters_transposed")
        s_pcp = sem("parameters_copied")
        s_cm = sem("conv_input_ready")
        s_cz = sem("conv_padding_zeroed")
        s_bst = sem("ln1_statistics")
        s_ctr = sem("C_transposed")
        s_cc = sem("C_ready")
        s_ang = sem("angles_ready")
        s_sin = sem("sines_ready")
        s_u = sem("U_loaded")
        s_vt = sem("VT_ready")
        s_vtr = sem("VT_transposed")
        s_v = sem("V_ready")
        s_bu = sem("chunk_inputs_done")
        s_s = sem("chunk_inputs_ready")
        s_w = sem("W_ready")
        s_k = sem("K_done")
        s_kp = sem("K_padded")
        s_kps = sem("K_stored")
        s_m = sem("M_loaded")
        s_st = sem("states_ready")
        s_y = sem("y_done")
        s_yg = sem("y_gelu_ready")
        s_yo = sem("y_stored")
        s_yl = sem("y_loaded")
        s_ysh = sem("ys_hi_ready")
        s_ysl = sem("ys_lo_ready")
        s_gin = sem("glu_inputs_loaded")
        s_sgt = sem("glu_gate_ready")
        s_gm = sem("mixed_ready")
        s_mh = sem("mixed_hi")
        s_ml = sem("mixed_lo")
        s_wof = sem("w_o_banks_free")
        s_res = sem("residual_loaded")
        s_x1o = sem("x1_then_blocks_stored")
        s_x1t = sem("x1_transposed")
        s_x1c = sem("x1T_copied")
        s_log = sem("logits_done")
        s_lgc = sem("logits_copied")
        s_msk = sem("masks_ready")
        s_rnk = sem("ranks_done")
        s_dst = sem("destinations_ready")
        s_tab = sem("table_ready")
        s_sct = sem("tokens_scattered")
        s_bix = sem("block_tokens_loaded")
        s_xg = sem("block_rows_gathered")
        s_xt = sem("block_rows_transposed")
        s_xh = sem("block_hi")
        s_xl = sem("block_lo")
        s_sil = sem("silu_ready")
        s_hm = sem("hidden_ready")
        s_ht = sem("hidden_transposed")
        s_hh = sem("hidden_hi")
        s_hl = sem("hidden_lo")
        s_yb = sem("block_half_copied")
        s_yr = [sem(f"expert_rows_gathered{i}") for i in range(TT)]
        s_xr = [sem(f"residual_loaded{i}") for i in range(TT)]
        s_xa = sem("residual_scaled")
        s_out = sem("output_stored")

        block = ctx.enter_context(nc.Block())

        U_COL, XIN_COL, C_COL, B_COL, GA_COL = 3 * DC, 0, DC, 2 * DC, 3 * DC + DS
        w_in2, w_oa2, w_glu2, w_o2 = w_in[0], w_out_a[0], w_glu[0], w_o[0]

        def conv_col(unit):
            return (XIN_COL, C_COL, B_COL)[unit % 3] + unit // 3 * UC

        def piece_rows(w, k0, nk, c0, nc_):
            return w[k0 * P:(k0 + nk) * P, bass.ds(c0, nc_)].rearrange("(k p) n -> p k n", p=P)

        def raw_v(s, nk):
            return raw[:, s, :].rearrange("p (k n) -> p k n", k=nk)

        def expert_raw(s):
            return raw[:, s, :] if s < RAW else raw2[:, s - RAW, :]

        @block.sync
        def _(sp):
            for t in range(TT):
                sp.dma_start(xin[:, t, :], x[0, t * P:(t + 1) * P, :]).then_inc(s_x[t], 16)

            def load(q, s, nk, src):
                sp.wait_ge(s_lo, q - RAW + 1)
                sp.dma_start(raw_v(s, nk), src).then_inc(s_raw[s], 16)

            for i in range(RAW):
                sp.dma_start(raw_v(i, 8), piece_rows(w_in2, 8 * (i % 2), 8, conv_col(i // 2), UC))\
                  .then_inc(s_raw[i], 16)
            for i in range(RAW, N_CONV):
                load(Q_CONV + i, i % RAW, 8, piece_rows(w_in2, 8 * (i % 2), 8, conv_col(i // 2), UC))
            for i in range(N_U):
                load(Q_U + i, i % RAW, 8, piece_rows(w_in2, 8 * (i % 2), 8, U_COL + i // 2 * UC, UC))
            for i in range(N_OA):
                load(Q_OA + i, i % RAW, 8, piece_rows(w_oa2, 0, 8, i * UC, UC))
            with sp.Fori(0, N_G // RAW) as r:
                for i in range(RAW):
                    load(Q_G + r * RAW + i, i, 8,
                         piece_rows(w_in2, 8 * (i % 2), 8, GA_COL + (r * 2 + i // 2) * UC, UC))
            for i in range(N_GLU):
                load(Q_GLU + i, i % RAW, 8, piece_rows(w_glu2, 0, 8, i % 2 * D + i // 2 * UC, UC))
            with sp.Fori(0, N_WO // RAW) as r:
                for i in range(RAW):
                    load(Q_WO + r * RAW + i, i, 4, piece_rows(w_o2, 4 * i, 4, r * 512, 512))

            def expert_piece(i, e):
                if i < 16:
                    w, k, c = (w_gate, w_up)[i // 8], 2 * (i % 8), 0
                else:
                    w, k, c = w_down, 2 * ((i - 16) % 4), (i - 16) // 4 * 1024
                rows = w[0].rearrange("e k n -> (e k) n")
                row = e * w.shape[2] + k * P
                if not isinstance(row, int):
                    row = sp.snap(row)
                return rows[bass.ds(row, 2 * P), c:c + 1024].rearrange("(k p) n -> p k n", p=P)

            def load_expert(q, i, e):
                s = i % RAWM
                if q is not None:
                    sp.wait_ge(s_lo, q - RAWM + 1)
                sp.dma_start(expert_raw(s).rearrange("p (k n) -> p k n", k=2), expert_piece(i % PB, e))\
                  .then_inc(s_rawm[s], 16)

            for i in range(RAW):
                load_expert(Q_MOE + i + RAWM - RAW, i, 0)
            sp.wait_ge(s_x1t, 4 * TT)
            sp.wait_ge(s_x1o, 16 * TT)
            for i in range(RAW, RAWM):
                load_expert(None, i, 0)

            def this_block(b, e):
                for i in range(RAWM, PB):
                    load_expert(Q_MOE + b * PB + i, i, e)

            def next_block(b, e):
                for i in range(PB, PB + RAWM):
                    load_expert(Q_MOE + b * PB + i, i, e)

            with sp.Fori(0, E - 1) as b:
                this_block(b, b)
                next_block(b, b + 1)
            sp.wait_ge(s_tab, 1)
            blocks = sp.value_load(tab[0:1, NBLK + 1:NBLK + 2], min_val=E, max_val=NBLK)
            with sp.Fori(E - 1, NBLK) as b:
                with sp.If(b < blocks):
                    this_block(b, sp.value_load(tab[0:1, bass.ds(b, 1)], min_val=0, max_val=E - 1))
                with sp.If(b < blocks - 1):
                    next_block(b, sp.value_load(tab[0:1, bass.ds(b + 1, 1)], min_val=0, max_val=E - 1))
            for i in range(TT + 2):
                sp.wait_ge(s_lo, blocks * PB + (Q_MOE - RAWM + i + 1))
                if i < TT:
                    sp.dma_start(xr[:, i, :], x1_d[i * P:(i + 1) * P, :]).then_inc(s_xr[i], 16)
                else:
                    sp.dma_start((lng2, lnb2)[i - TT][:], (ln2_g, ln2_b)[i - TT][0].partition_broadcast(P))\
                      .then_inc(s_lnp[2], 16)

        @block.gpsimd
        def _(pool):
            lk = Link(pool, s_plink)
            lk.link(pool.memset(ident[:], 0.0))
            pool.affine_select(out=ident[:], in_=ident[:], compare_op=ALU.not_equal, fill=1.0, base=0,
                               pattern=[[-1, P]], channel_multiplier=1).then_inc(s_const, 1)
            pool.memset(zeros[:], 0).then_inc(s_const, 1)
            pool.memset(zrow[:], 0.0).then_inc(s_const, 1)
            pool.iota(tokid[:], pattern=[[P, TT]], base=0, channel_multiplier=1).then_inc(s_const, 1)

            pool.wait_ge(s_ldt, 16)
            pool.tensor_copy(nat[:, 2, :].rearrange("g (r n) -> g r n", r=2),
                             ldt[:].unsqueeze(2).to_broadcast([GG, 2, N])).then_inc(s_nat, 1)

            def add_shift(buf, shift, t, n):
                pool.wait_ge(s_xm, n)
                pool.tensor_tensor(buf[:, t, :], buf[:, t, :], shift[:], ALU.add).then_inc(s_rows[t], 1)

            pool.wait_ge(s_lnp[0], 32)
            for t in range(2):
                add_shift(xin, lnb, t, t + 1)
            for t in range(TT):
                pool.wait_ge(s_rows[t], 1)
            pool.memset(cv[:, :, 0:2], 0.0).then_inc(s_cz, 1)
            pool.wait_ge(s_const, 4)
            for b in range(E, NBLK):
                for c in range(2):
                    pool.dma_start(yb_d[b * P:(b + 1) * P, c * 1024:(c + 1) * 1024], zrow[:]).then_inc(s_ybz, 16)

            for half in range(2):
                if half == 0:
                    for c in range(2):
                        pool.wait_ge(s_ust[c], 16 * 12)
                else:
                    pool.wait_ge(s_y, 1)
                for j in range(STEP):
                    pool.dma_start(U[j * H:(j + 1) * H, :, :],
                                   u_d[half * DS // 2:(half + 1) * DS // 2, j, :]
                                   .rearrange("(g h) n -> h g n", h=H)).then_inc(s_u, 16)
                pool.wait_ge(s_kp, half + 1)
                for r in range(2):
                    pool.dma_start(kp_d[half * HG:(half + 1) * HG, r, :, :].rearrange("g h x -> h g x"),
                                   kpd[r * H:(r + 1) * H, :, :, :].rearrange("h g d c -> h g (d c)"))\
                        .then_inc(s_kps, 16)
                pool.wait_ge(s_kps, 32 * (half + 1))
                for i in range(STEP):
                    pool.dma_start(M[i * H:(i + 1) * H, :, :, :].rearrange("h g r x -> h (g r) x"),
                                   kp_d[half * HG:(half + 1) * HG, :, :, (7 - i) * H:(7 - i) * H + P]
                                   .rearrange("g r h x -> h (g r) x")).then_inc(s_m, 16)
                pool.wait_ge(s_yg, 4 * (half + 1))
                for j in range(STEP):
                    pool.dma_start(y_d[half * DS // 2:(half + 1) * DS // 2, j, :]
                                   .rearrange("(g h) n -> h g n", h=H),
                                   yst[j * H:(j + 1) * H, :, :, :].rearrange("h g r n -> h (g r) n"))\
                        .then_inc(s_yo, 16)
            pool.wait_ge(s_yo, 16 * 16)
            pool.dma_start(yraw[:, :, :], y_d.rearrange("(k p) j n -> p k (j n)", p=P)).then_inc(s_yl, 16)

            lk.link(pool.memset(square[:], 1.0))
            lk.link(pool.tensor_copy(onesb[:], square[:]))
            lk.link(pool.affine_select(out=square[:], in_=square[:], compare_op=ALU.is_gt, fill=0.0, base=0,
                                       pattern=[[1, P]], channel_multiplier=-1))
            lk.link(pool.tensor_copy(tri[:], square[:]))
            pool.memset(ones[:], 1.0).then_inc(s_const2, 1)
            lk.link(pool.iota(RI[:, 0, :], pattern=[[1, E]], base=0, channel_multiplier=0))
            lk.link(pool.tensor_copy(eio[:, 0, :], RI[:, 0, :]))
            lk.link(pool.iota(RI[:, 1, :], pattern=[[0, EG], [-1, EP]], base=EP, channel_multiplier=0))
            lk.link(pool.tensor_copy(eio[:, 1, :], RI[:, 1, :]))
            lk.link(pool.iota(RI[:, 2, :], pattern=[[-P, E]], base=P * (E - 1), channel_multiplier=0))
            lk.link(pool.tensor_copy(eio[:, 2, :], RI[:, 2, :]))
            lk.link(pool.iota(RI[:, 3, 0:EG], pattern=[[-1, EG]], base=EG, channel_multiplier=0))
            lk.link(pool.tensor_copy(gio[:], RI[:, 3, 0:EG]))

            for c in range(2):
                pool.wait_ge(s_sgo[c], 16 * 16)
            with pool.Fori(0, 8) as j:
                pool.wait_ge(s_gm, j + 2)
                for n, (src, row) in enumerate(((ya_d, j * UC), (sg_d, j * UC), (sg_d, j * UC + D))):
                    pool.dma_start(gin[:, n, :, :], src[bass.ds(row, UC), :]
                                   .rearrange("(c p) t -> p c t", p=P)).then_inc(s_gin, 16)

            pool.wait_ge(s_used, Q_WO)
            pool.wait_ge(s_x0o, 16 * TT)
            pool.dma_start(x1[:], x0_d.rearrange("(t p) d -> p t d", p=P)).then_inc(s_res, 16)
            pool.dma_start(lng1[:], ln1_g[0].partition_broadcast(P)).then_inc(s_lnp[1], 16)
            pool.dma_start(lnb1[:], ln1_b[0].partition_broadcast(P)).then_inc(s_lnp[1], 16)
            pool.dma_start(wr[:], w_router.rearrange("(k p) e -> p k e", p=P)).then_inc(s_lnp[1], 16)
            pool.dma_start(brb[:], b_router.partition_broadcast(P)).then_inc(s_lnp[1], 16)
            pool.wait_ge(s_gm, 10)
            pool.wait_ge(s_ml, 8)
            lk.link(pool.iota(RI[:, 0, 0:NOVER + 1], pattern=[[1, NOVER + 1]], base=0, channel_multiplier=0))
            pool.tensor_copy(ovn[:], RI[:, 0, 0:NOVER + 1]).then_inc(s_const2, 1)

            pool.wait_ge(s_lnp[1], 64)
            for t in (1, 3):
                add_shift(x1, lnb1, t, TT + t + 1)

            pool.wait_ge(s_zero, 16)
            pool.wait_ge(s_dst, 1)
            for t in range(TT):
                for k in range(2):
                    pool.indirect_dma_start(
                        out=tok_d[:, :], out_offset=bass.IndirectOffsetOnAxis(ap=dest[:, t, k:k + 1], axis=0),
                        in_=tokid[:, t:t + 1], in_offset=None).then_inc(s_sct, 16)
            pool.wait_ge(s_sct, 16 * 2 * TT)
            pool.wait_ge(s_x1o, 16 * TT)

            def gather(b):
                if b:
                    pool.wait_ge(s_xt, 2 * b)
                pool.dma_start(bidx[:], tok_d[b * P:(b + 1) * P, :]).then_inc(s_bix, 16)
                pool.wait_ge(s_bix, b * 16 + 16)
                pool.indirect_dma_start(
                    out=xg[:], out_offset=None, in_=x1_d[:, :],
                    in_offset=bass.IndirectOffsetOnAxis(ap=bidx[:], axis=0)).then_inc(s_xg, 16)

            gather(0)
            for b in range(E):
                gather(b + 1)
            pool.wait_ge(s_tab, 1)
            blocks = pool.value_load(tab[0:1, NBLK + 1:NBLK + 2], min_val=E, max_val=NBLK)
            for b in range(E, NBLK):
                with pool.If(blocks > b):
                    gather(b + 1)

            pool.wait_ge(s_used, blocks * PB + Q_MOE)
            pool.wait_ge(s_x1o, blocks * 32 + 16 * TT)
            lk.link(pool.tensor_tensor(back[:].rearrange("p t k -> p (t k)"), dest[:].rearrange("p t k -> p (t k)"),
                                       zeros[:, 0:2 * TT], ALU.add))
            pool.wait_ge(s_ybz, 16 * 2 * NOVER)
            for t in range(TT):
                for k in range(2):
                    pool.indirect_dma_start(
                        out=yg[:, t, k, :], out_offset=None, in_=yb_d[:, :],
                        in_offset=bass.IndirectOffsetOnAxis(ap=back[:, t, k:k + 1], axis=0)).then_inc(s_yr[t], 16)
            pool.wait_ge(s_lnp[2], 32)
            for t in range(3):
                pool.wait_ge(s_xn, 2 * TT + t + 1)
                lk.link(pool.tensor_tensor(xr[:, t, :], xr[:, t, :], lng2[:], ALU.mult))
                pool.tensor_tensor(xr[:, t, :], xr[:, t, :], lnb2[:], ALU.add).then_inc(s_rows[t], 1)

        @block.scalar
        def _(act):
            act.dma_start(lng[:], in_g.partition_broadcast(P)).then_inc(s_lnp[0], 16)
            act.dma_start(lnb[:], in_b.partition_broadcast(P)).then_inc(s_lnp[0], 16)
            act.dma_start(nat[:, 0, :], ssm_a_re[0].rearrange("(g r) n -> g (r n)", r=2)).then_inc(s_prm, 16)
            act.dma_start(nat[:, 1, :], ssm_a_im[0].rearrange("(g r) n -> g (r n)", r=2)).then_inc(s_prm, 16)
            act.dma_start(ldt[:], ssm_log_dt[0].rearrange("(g r) -> g r", r=2)).then_inc(s_ldt, 16)
            for c, b_ in enumerate((ssm_b_re, ssm_b_im)):
                act.dma_start(braw[:, c, :, :], b_[0].rearrange("(g r) n h -> (r n) g h", r=2)).then_inc(s_prm, 16)
            for c, c_ in enumerate((ssm_c_re, ssm_c_im)):
                for twice in range(2):
                    act.dma_start(cnat[:, c, :, twice, :], c_[0].rearrange("(a g) h n -> (g h) a n", a=8))\
                       .then_inc(s_prm, 16)
            act.dma_start(dnat[:], ssm_d[0].rearrange("(g q) -> g q", q=2 * H)).then_inc(s_prm, 16)
            act.dma_start(cwn[:], conv_w[0].rearrange("w (a p) -> (w a) p", p=P)).then_inc(s_prm, 16)
            act.wait_ge(s_const, 4)
            act.dma_start(tok_d.rearrange("(p b) o -> p (b o)", p=P), zeros[:]).then_inc(s_zero, 16)

            def root(n):
                act.wait_ge(s_var, n + 1)

            def normalise(buf, t, n):
                act.wait_ge(s_rs, n)
                act.activation(buf[:, t, :], buf[:, t, :], ACT.Identity, bias=nmr[:, t:t + 1],
                               scale=rstd[:, t:t + 1]).then_inc(s_xn, 1)

            def rows_hi(t):
                for b in range(4):
                    act.wait_ge(s_tr, 4 * t + b + 1)
                    act.activation(xT_hi[:, 4 * b:4 * b + 4, t * P:(t + 1) * P],
                                   sets[t % 2][:, b, :].rearrange("p (k n) -> p k n", k=4), ACT.Copy)\
                       .then_inc(s_trh, 1)
                act.dma_start(x0_d[t * P:(t + 1) * P, :], xin[:, t, :]).then_inc(s_x0o, 16)

            act.wait_ge(s_const, 4)
            act.activation(ahead[:, 2:3], ident[:, 0:1], ACT.Copy).then_inc(s_yb, 1)

            for t in range(TT):
                root(t)
                act.activation(tmp4[:, t:t + 1], rstd[:, t:t + 1], ACT.Sqrt).then_inc(s_sq, 1)
                normalise(xin, t, t + 1)
                if t >= 2:
                    rows_hi(t - 2)
            rows_hi(2)
            rows_hi(3)

            def hi(q, s, whi_=whi, r=RD):
                act.wait_ge(s_raw[s], raw_count(q, s))
                if not isinstance(q, int) or q >= r:
                    act.wait_ge(s_used, q - r + 1)
                act.activation(whi_[:, s % r, :], raw[:, s, :], ACT.Copy).then_inc(s_hi, 1)

            def hi_expert(b, i):
                act.wait_ge(s_rawm[i % RAWM], b * (16 * PB // RAWM) + 16 * (i // RAWM + 1))
                act.wait_ge(s_used, b * PB + (Q_MOE + i - RM + 1))
                act.activation(mhi[:, i % RM, :], expert_raw(i % RAWM), ACT.Copy).then_inc(s_hi, 1)

            def raw_count(q, s):
                return (q - s) * (16 // RAW) + 16

            copies = [0]

            def leave(rows, view_out, view_in, func, buf, earlier, stored):
                if earlier:
                    act.wait_ge(stored, 16 * earlier)
                copies[0] += 1
                act.activation(view_out, view_in, func).then_inc(s_cp, 1)
                act.wait_ge(s_cp, copies[0])
                act.dma_start(rows, buf).then_inc(stored, 16)

            def after(m):
                if m < 0 or (m % 2 == 0 and not Q_OA <= m < Q_G):
                    return
                n = unit_of(m)
                if m < Q_U:
                    i, part = divmod(n, 3)
                    if part == 0:
                        act.wait_ge(s_used, m + 1)
                        act.wait_ge(s_cm, i)
                        act.activation(cx[:], dn[:, 2 * (n % 2):2 * (n % 2) + 2, :], ACT.Copy).then_inc(s_cx, 1)
                    if part == 2:
                        if i == 0:
                            act.wait_ge(s_x0o, 16 * TT)
                        act.wait_ge(s_pa, i + 1)
                        act.activation(pa_hi[:, 2 * i:2 * i + 2, :], ct[:], ACT.Copy).then_inc(s_pah, 1)
                elif m < Q_OA:
                    i = n - 12
                    act.wait_ge(s_used, m + 1)
                    for c in range(2):
                        leave(u_d[(2 * i + c) * P:(2 * i + c + 1) * P].rearrange("p j n -> p (j n)"),
                              ust[:, c, :].rearrange("p (j n) -> p j n", j=STEP),
                              dn[:, 2 * (n % 2) + c, :].rearrange("p (n j) -> p j n", j=STEP),
                              ACT.Copy, ust[:, c, :], i, s_ust[c])
                elif m < Q_G:
                    j = m - Q_OA
                    act.wait_ge(s_used, m + 1)
                    for c in range(2):
                        leave(ya_d[(2 * j + c) * P:(2 * j + c + 1) * P, :], ust[:, c, :],
                              dn[:, 2 * (n % 2) + c, :], ACT.Copy, ust[:, c, :], 4 + j, s_ust[c])
                else:
                    j = n - 24
                    act.wait_ge(s_used, m + 1)
                    for c in range(2):
                        leave(sg_d[(2 * j + c) * P:(2 * j + c + 1) * P, :], sgst[:, c, :],
                              dn[:, 2 * (n % 2) + c, :], ACT.Sigmoid, sgst[:, c, :], j, s_sgo[c])

            def c_ready():
                act.wait_ge(s_ctr, 1)
                for c in range(2):
                    for a in range(2):
                        for r in range(2):
                            rows = slice(r * N, (r + 1) * N)
                            last = act.activation(
                                Cc[rows, c, a * HG:(a + 1) * HG, :],
                                ex[rows, 2 * c + a, :].rearrange("p (g r h) -> p r g h", r=2, h=H)[:, r, :, :],
                                ACT.Copy)
                            last.then_inc(s_cc, 1)

            def v_ready(half, c):
                act.wait_ge(s_vtr, 2 * half + c + 1)
                if half == 0 and c == 0:
                    for tile in range(2):
                        act.wait_ge(s_ust[tile], 16 * 12)
                for b in range(4):
                    act.activation(V[:, c, 4 * b:4 * b + 4, :], ex[:, b, :], ACT.Copy).then_inc(s_v, 1)

            def chunk_inputs(half):
                act.wait_ge(s_bu, half + 1)
                for c in range(2):
                    for b in range(2):
                        act.activation(S[:, c, 8 * b:8 * b + 8, :], ex[:, 2 * c + b, :], ACT.Copy).then_inc(s_s, 1)

            def gelu_y(half):
                act.wait_ge(s_y, half + 1)
                for b in range(2):
                    for r in range(2):
                        act.activation(yst[:, 8 * b:8 * b + 8, r, :],
                                       ex[:, 2 * b + r, :].rearrange("p (g n) -> p g n", g=8),
                                       ACT.Gelu_apprx_tanh).then_inc(s_yg, 1)

            for q in range(Q_GLU):
                hi(q, q % RAW)
                after(q - 2)
                if q == 5:
                    c_ready()
                    act.wait_ge(s_ang, 1)
                    act.activation(prm[:, 10, :], prm[:, 8, :], ACT.Sin).then_inc(s_sin, 1)
                    act.activation(prm[:, 11, :], prm[:, 8, :], ACT.Sin, scale=0.5).then_inc(s_sin, 1)
                if q >= Q_G:
                    half, rel = divmod(q - Q_G, 16)
                    if rel == 6:
                        v_ready(half, 0)
                    if rel == 7:
                        v_ready(half, 1)
                    if rel == 8:
                        chunk_inputs(half)
                    if rel == 13:
                        gelu_y(half)
            hi(Q_GLU, 0)
            act.wait_ge(s_yl, 16)
            for k in range(8):
                act.activation(ys_hi[:, k, :].rearrange("p (n j) -> p j n", j=STEP),
                               yraw[:, k, :].rearrange("p (j n) -> p j n", j=STEP), ACT.Copy).then_inc(s_ysh, 1)
            hi(Q_GLU + 1, 1)
            after(Q_GLU - 1)

            for c in range(2):
                act.wait_ge(s_sgo[c], 16 * 16)
            with act.Fori(0, 4) as r:
                for i in range(2):
                    q = Q_GLU + 4 * r + 2 * i + 2
                    hi(q, (2 * i + 2) % RAW)
                    hi(q + 1, (2 * i + 3) % RAW)
                    j = r * 2 + i
                    act.wait_ge(s_used, j * 2 + (Q_GLU + 2))
                    act.wait_ge(s_gm, j + 2)
                    act.activation(sgt[:], (dn, ex)[i][:, 2:4, :], ACT.Sigmoid).then_inc(s_sgt, 1)
                    act.wait_ge(s_gm, j + 3)
                    act.activation(mx_hi[:, bass.ds(2 * j, 2), :], gm[:], ACT.Copy).then_inc(s_mh, 1)
            with act.Fori(0, 3) as r:
                for i in range(4):
                    hi(Q_WO + 4 * r + i + 2, (i + 2) % RAW)
            hi(Q_WO + 14, 2)
            hi(Q_WO + 15, 3)

            act.wait_ge(s_used, Q_MOE)
            for i in range(3):
                hi_expert(0, i)

            root(TT)
            act.activation(tmp4[:], rstd[:], ACT.Sqrt).then_inc(s_sq, 1)
            for t in range(TT):
                normalise(x1, t, TT + 1)
            for t in range(TT):
                act.wait_ge(s_rows[t], 2)
                act.dma_start(x1_d[t * P:(t + 1) * P, :], x1[:, t, :]).then_inc(s_x1o, 16)
                for b in range(4):
                    act.wait_ge(s_x1t, 4 * t + b + 1)
                    if t >= 2 and b == 0:
                        act.wait_ge(s_log, t - 1)
                    act.activation(x1T[:, t % 2, 4 * b:4 * b + 4, :],
                                   sets[t % 2][:, b, :].rearrange("p (k n) -> p k n", k=4), ACT.Copy)\
                       .then_inc(s_x1c, 1)

            def block_rows_hi(n, half):
                act.wait_ge(s_xt, n * 2 + half + 1)
                for c in range(2):
                    k = 8 * half + 4 * c
                    act.activation(xg_hi[:, k:k + 4, :], dn[:, c, :].rearrange("p (k n) -> p k n", k=4),
                                   ACT.Copy).then_inc(s_xh, 1)

            def block_half_out(b, half):
                cols = slice(1024 * half, 1024 * (half + 1))
                act.activation(ybl[:, cols].rearrange("p (c n) -> p c n", c=2), ex[:, 2 * half:2 * half + 2, :],
                               ACT.Copy).then_inc(s_yb, 1)
                act.wait_ge(s_yb, b * 2 + 2 + half)
                act.dma_start(yb_d[bass.ds(b * P, P), cols], ybl[:, cols]).then_inc(s_x1o, 16)

            def this_block(b):
                for i in range(3, PB):
                    hi_expert(b, i)
                    if i == 11:
                        act.wait_ge(s_used, b * PB + (Q_MOE + 8))
                        act.wait_ge(s_hm, b * 2 + 1)
                        for c in range(2):
                            act.activation(sil[:, c * 512:(c + 1) * 512], dn[:, c, :], ACT.Silu)\
                               .then_inc(s_sil, 1)
                    if i == 19:
                        for c in range(2):
                            act.wait_ge(s_ht, b * 2 + c + 1)
                            act.activation(h_hi[:, 4 * c:4 * c + 4, :],
                                           dn[:, 2 + c, :].rearrange("p (k n) -> p k n", k=4), ACT.Copy)\
                               .then_inc(s_hh, 1)
                        block_rows_hi(b + 1, 0)
                    if i == 22:
                        block_rows_hi(b + 1, 1)
                act.wait_ge(s_used, b * PB + (Q_MOE + 20))
                act.wait_ge(s_x1o, b * 32 + 16 * TT)
                block_half_out(b, 0)

            def next_block(b):
                for i in range(PB, PB + 3):
                    hi_expert(b, i)

            def block_out(b):
                act.wait_ge(s_used, b * PB + (Q_MOE + 24))
                block_half_out(b, 1)

            block_rows_hi(0, 0)
            block_rows_hi(0, 1)
            with act.Fori(0, E - 1) as b:
                this_block(b)
                next_block(b)
                block_out(b)
            act.wait_ge(s_tab, 1)
            blocks = act.value_load(tab[0:1, NBLK + 1:NBLK + 2], min_val=E, max_val=NBLK)
            with act.Fori(E - 1, NBLK) as b:
                with act.If(b < blocks):
                    this_block(b)
                with act.If(b < blocks - 1):
                    next_block(b)
                with act.If(b < blocks):
                    block_out(b)

            for t in range(TT):
                act.wait_ge(s_xr[t], 16)
                act.activation(xr[:, t, :], xr[:, t, :], ACT.Copy, scale=ALPHA).then_inc(s_xa, 1)
            for t in range(TT):
                root(TT + 1 + t)
                act.activation(tmp4[:, t:t + 1], rstd[:, t:t + 1], ACT.Sqrt).then_inc(s_sq, 1)
                normalise(xr, t, TT + 2 + t)
            for t in range(TT):
                act.wait_ge(s_rows[t], 3)
                act.dma_start(out[0, t * P:(t + 1) * P, :], xr[:, t, :]).then_inc(s_out, 16)
            act.wait_ge(s_out, 16 * TT)

        @block.vector
        def _(dve):
            lk = Link(dve, s_link)
            link = lk.link
            tt, ts, stt = dve.tensor_tensor, dve.tensor_scalar, dve.scalar_tensor_tensor

            def lo(q, s, whi_=whi, wlo_=wlo, r=RD):
                dve.wait_ge(s_hi, q + 1)
                tt(wlo_[:, s % r, :], raw[:, s, :], whi_[:, s % r, :].bitcast(F32), ALU.subtract).then_inc(s_lo, 1)

            def lo_expert(b, i):
                dve.wait_ge(s_hi, b * PB + (Q_MOE + i + 1))
                tt(mlo[:, i % RM, :], expert_raw(i % RAWM), mhi[:, i % RM, :].bitcast(F32), ALU.subtract)\
                    .then_inc(s_lo, 1)

            def stats(buf, t):
                for c in range(4):
                    lk.go(dve.bn_stats(bst[:, t, c, :], buf[:, t, c * 512:(c + 1) * 512]))
                lk.wait()
                link(dve.bn_aggr(mv[:, t, :], bst[:, t, :, :]))

            def row_scale(sl, n):
                ts(rstd[:, sl], mv[:, sl, 1], EPS, None, ALU.add).then_inc(s_var, 1)
                dve.wait_ge(s_sq, n)
                link(dve.reciprocal(nmr[:, sl], tmp4[:, sl]))
                link(tt(tmp4[:, sl], rstd[:, sl], nmr[:, sl], ALU.mult))
                link(tt(tmp4[:, sl], tmp4[:, sl], nmr[:, sl], ALU.mult))
                link(ts(tmp4[:, sl], tmp4[:, sl], -0.5, 1.5, ALU.mult, ALU.add))
                link(tt(rstd[:, sl], nmr[:, sl], tmp4[:, sl], ALU.mult))
                stt(nmr[:, sl], mv[:, sl, 0], -1.0, rstd[:, sl], ALU.mult, ALU.mult).then_inc(s_rs, 1)

            def scale_rows(buf, gain, t, n):
                dve.wait_ge(s_xn, n)
                tt(buf[:, t, :], buf[:, t, :], gain[:], ALU.mult).then_inc(s_xm, 1)

            def shift_rows(buf, shift, t, n):
                dve.wait_ge(s_xm, n)
                tt(buf[:, t, :], buf[:, t, :], shift[:], ALU.add).then_inc(s_rows[t], 1)

            def rows_lo(t):
                for b in range(4):
                    dve.wait_ge(s_trh, 4 * t + b + 1)
                    tt(xT_lo[:, 4 * b:4 * b + 4, t * P:(t + 1) * P],
                       sets[t % 2][:, b, :].rearrange("p (k n) -> p k n", k=4),
                       xT_hi[:, 4 * b:4 * b + 4, t * P:(t + 1) * P].bitcast(F32), ALU.subtract)\
                        .then_inc(s_trl, 1)

            dve.memset(ahead[:, 0:1], 0.0).then_inc(s_gm, 1)
            dve.memset(ahead[:, 3:4], 0.0).then_inc(s_gm, 1)
            dve.memset(ahead[:, 1:2], 0.0).then_inc(s_hm, 1)

            for t in range(TT):
                dve.wait_ge(s_x[t], 16)
                stats(xin, t)
                row_scale(slice(t, t + 1), t + 1)
                if t == 1:
                    dve.wait_ge(s_lnp[0], 32)
                if t >= 1:
                    scale_rows(xin, lng, t - 1, t)
            shift_rows(xin, lnb, 2, 3)
            rows_lo(0)
            rows_lo(1)
            scale_rows(xin, lng, 3, 4)
            shift_rows(xin, lnb, 3, 4)
            rows_lo(2)
            rows_lo(3)

            def exp_of(dst, src, xc, k, r, p):
                link(ts(xc, src, -87.0, 88.0, ALU.max, ALU.min))
                link(ts(k, xc, 1.0 / math.log(2.0), MAGIC, ALU.mult, ALU.add))
                link(ts(k, k, MAGIC, None, ALU.subtract))
                link(stt(r, k, -0.693359375, xc, ALU.mult, ALU.add))
                link(stt(r, k, 0.693359375 - math.log(2.0), r, ALU.mult, ALU.add))
                link(ts(p, r, 1.0 / math.factorial(8), None, ALU.mult))
                for d in range(7, 0, -1):
                    link(stt(p, p, 1.0 / math.factorial(d), r, ALU.add, ALU.mult))
                link(ts(p, p, 1.0, None, ALU.add))
                link(ts(xc.bitcast(I32), k, 127.0, 2.0 ** 23, ALU.add, ALU.mult))
                link(tt(p, p, xc.bitcast(F32), ALU.mult))
                link(stt(dst, src, -87.0, p, ALU.is_ge, ALU.mult))

            def v_(i):
                return prm[:, i, :]

            def cmul(o_re, o_im, a, b, x_, y_):
                link(tt(x_, a[0], b[0], ALU.mult))
                link(tt(y_, a[1], b[1], ALU.mult))
                link(tt(x_, x_, y_, ALU.subtract))
                link(tt(y_, a[0], b[1], ALU.mult))
                link(tt(o_im, a[1], b[0], ALU.mult))
                link(tt(o_im, o_im, y_, ALU.add))
                link(dve.tensor_copy(o_re, x_))

            def parameters_1():
                dve.wait_ge(s_ptr, 1)
                dve.tensor_copy(prm[:, 0:3, :], ex[:, 0, 0:3 * GG].rearrange("p (i g) -> p i g", i=3))\
                    .then_inc(s_pcp, 1)
                dve.tensor_copy(dgv[:], ex[0:2 * H, 0, 3 * GG:4 * GG]).then_inc(s_pcp, 1)
                dve.tensor_copy(cw[:], ex[:, 0, 4 * GG:4 * GG + 24].rearrange("p (w a) -> p a w", w=3)).then_inc(s_pcp, 1)
                dve.wait_ge(s_pcp, 3)
                exp_of(v_(3), v_(2), v_(21), v_(22), v_(23), v_(24))
                link(ts(v_(4), v_(0), -1e-4, None, ALU.min))
                link(tt(v_(19), v_(4), v_(3), ALU.mult))
                exp_of(v_(5), v_(19), v_(21), v_(22), v_(23), v_(24))
                link(tt(v_(6), v_(1), v_(3), ALU.mult))
                c1, c2, c3 = two_pi_parts()
                link(ts(v_(7), v_(6), 1.0 / (2 * math.pi), MAGIC, ALU.mult, ALU.add))
                link(ts(v_(7), v_(7), MAGIC, None, ALU.subtract))
                link(stt(v_(8), v_(7), -c1, v_(6), ALU.mult, ALU.add))
                link(stt(v_(8), v_(7), -c2, v_(8), ALU.mult, ALU.add))
                link(stt(v_(8), v_(7), -c3, v_(8), ALU.mult, ALU.add))
                ts(v_(8), v_(8), -3.1415925, 3.1415925, ALU.max, ALU.min).then_inc(s_ang, 1)

            def parameters_2():
                dve.wait_ge(s_sin, 2)
                link(tt(v_(12), v_(11), v_(11), ALU.mult))
                link(ts(v_(12), v_(12), -2.0, 1.0, ALU.mult, ALU.add))
                link(tt(A1[:, 0, :], v_(5), v_(12), ALU.mult))
                link(tt(A1[:, 2, :], v_(5), v_(10), ALU.mult))
                link(ts(A1[:, 1, :], A1[:, 2, :], -1.0, None, ALU.mult))
                link(tt(v_(15), v_(4), v_(4), ALU.mult))
                link(tt(v_(19), v_(1), v_(1), ALU.mult))
                link(tt(v_(15), v_(15), v_(19), ALU.add))
                link(dve.reciprocal(v_(15), v_(15)))
                link(ts(v_(16), A1[:, 0, :], -1.0, None, ALU.add))
                link(tt(v_(17), v_(16), v_(4), ALU.mult))
                link(tt(v_(19), A1[:, 2, :], v_(1), ALU.mult))
                link(tt(v_(17), v_(17), v_(19), ALU.add))
                link(tt(v_(17), v_(17), v_(15), ALU.mult))
                link(tt(v_(18), A1[:, 2, :], v_(4), ALU.mult))
                link(tt(v_(19), v_(16), v_(1), ALU.mult))
                link(tt(v_(18), v_(18), v_(19), ALU.subtract))
                link(tt(v_(18), v_(18), v_(15), ALU.mult))
                a = (A1[:, 0, :], A1[:, 2, :])
                cmul(v_(25), v_(26), a, a, v_(19), v_(20))
                b = (v_(25), v_(26))
                cmul(v_(27), v_(28), b, b, v_(19), v_(20))
                b = (v_(27), v_(28))
                cmul(P8[:, 0, 0, :], P8[:, 0, 2, :], b, b, v_(19), v_(20))

            def parameters_3():
                a8 = (P8[:, 0, 0, :], P8[:, 0, 2, :])
                for i in range(1, STEP):
                    cmul(P8[:, i, 0, :], P8[:, i, 2, :], (P8[:, i - 1, 0, :], P8[:, i - 1, 2, :]), a8,
                         v_(19), v_(20))
                link(ts(P8[:, :, 1, :], P8[:, :, 2, :], -1.0, None, ALU.mult))
                co_re = v_(17).unsqueeze(2).to_broadcast([P, GG, H])
                co_im = v_(18).unsqueeze(2).to_broadcast([P, GG, H])
                link(tt(Bb[:, 0, :, :], braw[:, 0, :, :], co_re, ALU.mult))
                link(tt(Bb[:, 1, :, :], braw[:, 1, :, :], co_im, ALU.mult))
                link(tt(Bb[:, 0, :, :], Bb[:, 0, :, :], Bb[:, 1, :, :], ALU.subtract))
                link(tt(braw[:, 0, :, :], braw[:, 0, :, :], co_im, ALU.mult))
                link(tt(Bb[:, 1, :, :], braw[:, 1, :, :], co_re, ALU.mult))
                link(tt(Bb[:, 1, :, :], Bb[:, 1, :, :], braw[:, 0, :, :], ALU.add))
                link(tt(dmask[:], ident[0:2 * H, 0:H], ident[0:2 * H, H:2 * H], ALU.add))
                link(tt(dsk[:], dgv[:].unsqueeze(2).to_broadcast([2 * H, GG, H]),
                        dmask[:].unsqueeze(1).to_broadcast([2 * H, GG, H]), ALU.mult))

            def times_a(dst, src, half, op, done=None):
                g = slice(half * HG, (half + 1) * HG)
                ar = A1[:, 0, g].unsqueeze(1).to_broadcast([P, 2, HG]).unsqueeze(3).to_broadcast([P, 2, HG, H])
                ai = A1[:, 1:3, g].unsqueeze(3).to_broadcast([P, 2, HG, H])
                lk.go(tt(t1[:], src, ar, ALU.mult))
                lk.go(tt(t2[:], src[:, ::-1], ai, ALU.mult))
                lk.wait()
                if done is None:
                    link(tt(dst, t1[:], t2[:], op))
                else:
                    tt(dst, t1[:], t2[:], op).then_inc(done, 1)

            def vt_steps(half, steps):
                for i in steps:
                    if i == STEP - 1:
                        g = slice(half * HG, (half + 1) * HG)
                        link(dve.tensor_copy(VT[:, :, :, i, :], Bb[:, :, g, :]))
                    else:
                        times_a(VT[:, :, :, i, :], VT[:, :, :, i + 1, :], half, ALU.add)

            def w_steps(half, steps, done=None):
                for d in steps:
                    if d == 0:
                        g = slice(half * HG, (half + 1) * HG)
                        lk.go(dve.tensor_copy(W[:, 0, :, 0, :], Cc[:, 0, g, :]))
                        lk.go(ts(W[:, 1, :, 0, :], Cc[:, 1, g, :], -1.0, None, ALU.mult))
                        lk.wait()
                    else:
                        times_a(W[:, :, :, d, :], W[:, :, :, d - 1, :], half, ALU.subtract, done)

            def block_diagonal(half):
                g = slice(half * HG, (half + 1) * HG)
                link(dve.memset(Bbd[:], 0.0))
                lk.go(dve.tensor_copy(Bbd[0:N, :, :, 0, :], Bb[0:N, :, g, :]))
                dve.tensor_copy(Bbd[N:P, :, :, 1, :], Bb[N:P, :, g, :]).then_inc(s_vt, 1)
                lk.wait()

            Sb = S[:].rearrange("p c g (b i) -> p c g b i", i=STEP)
            u1 = t1[:].rearrange("p c g h -> p (c g h)")
            u2 = t2[:].rearrange("p c g h -> p (c g h)")

            def advance(half, power, dst, src, nb, done=None):
                g = slice(half * HG, (half + 1) * HG)
                shape = [P, 2, HG, nb]
                ar = P8[:, power - 1, 0, g].unsqueeze(1).to_broadcast([P, 2, HG]).unsqueeze(3).to_broadcast(shape)
                ai = P8[:, power - 1, 1:3, g].unsqueeze(3).to_broadcast(shape)
                x_ = u1[:, 0:2 * HG * nb].rearrange("p (c g b) -> p c g b", c=2, g=HG)
                y_ = u2[:, 0:2 * HG * nb].rearrange("p (c g b) -> p c g b", c=2, g=HG)
                lk.go(tt(x_, src, ar, ALU.mult))
                lk.go(tt(y_, src[:, ::-1], ai, ALU.mult))
                lk.wait()
                link(tt(dst, dst, x_, ALU.add))
                if done is None:
                    link(tt(dst, dst, y_, ALU.add))
                else:
                    tt(dst, dst, y_, ALU.add).then_inc(done, 1)

            def scan_inside(half, steps):
                for i in steps:
                    advance(half, 1, Sb[:, :, :, :, i], Sb[:, :, :, :, i - 1], STEP)

            def scan_over(half):
                for b in range(1, STEP):
                    advance(half, STEP, Sb[:, :, :, b:b + 1, STEP - 1], Sb[:, :, :, b - 1:b, STEP - 1], 1)

            def scan_back(half, places, done=None):
                for i in places:
                    advance(half, i + 1, Sb[:, :, :, 1:STEP, i], Sb[:, :, :, 0:STEP - 1, STEP - 1], STEP - 1, done)

            def pad_k(half):
                dve.wait_ge(s_k, half + 1)
                lk.go(dve.memset(kpd[:, :, 0:7, :], 0.0))
                for b in range(4):
                    lk.go(dve.tensor_copy(kpd[:, 4 * b:4 * b + 4, 7:15, :],
                                          ex[0:2 * H, b, :].rearrange("p (g d h) -> p g d h", g=4, h=H)))
                lk.wait()
                tt(kpd[:, :, 7, :], kpd[:, :, 7, :], dsk[:, half * HG:(half + 1) * HG, :], ALU.add)\
                    .then_inc(s_kp, 1)

            def conv_after(m):
                n = unit_of(m)
                i, part = divmod(n, 3)
                b2 = dn[:, 2 * (n % 2):2 * (n % 2) + 2, :]
                if part == 1:
                    dve.wait_ge(s_cx, i + 1)
                    dve.wait_ge(s_used, m + 1)
                    tt(cv[:, :, 2:], b2, cx[:], ALU.mult).then_inc(s_cm, 1)
                    dve.wait_ge(s_cm, i + 1)
                    for k in range(CONV_WIDTH):
                        for c in range(2):
                            w_ = cw[:, 2 * i + c, k:k + 1]
                            v = cv[:, c, k:k + T]
                            lk.go(ts(ct[:, c, :], v, w_, None, ALU.mult) if k == 0 else
                                  stt(ct[:, c, :], v, w_, ct[:, c, :], ALU.mult, ALU.add))
                        lk.wait()
                if part == 2:
                    dve.wait_ge(s_used, m + 1)
                    tt(ct[:], ct[:], b2, ALU.mult).then_inc(s_pa, 1)
                    dve.wait_ge(s_pah, i + 1)
                    tt(pa_lo[:, 2 * i:2 * i + 2, :], ct[:], pa_hi[:, 2 * i:2 * i + 2, :].bitcast(F32),
                       ALU.subtract).then_inc(s_pal, 1)
                    dve.wait_ge(s_pal, i + 1)

            for q in range(Q_GLU):
                lo(q, q % RAW)
                m = q - 2
                if 0 <= m < Q_U and m % 2 == 1:
                    if m == 3:
                        dve.wait_ge(s_cz, 1)
                        dve.wait_ge(s_prm, 16 * N_PRM)
                    conv_after(m)
                if q == 3:
                    parameters_1()
                if q == 6:
                    parameters_2()
                if q == 8:
                    dve.wait_ge(s_ybz, 16 * 2 * NOVER)
                    parameters_3()
                if q >= Q_G:
                    half, rel = divmod(q - Q_G, 16)
                    if rel == 1:
                        if half == 1:
                            dve.wait_ge(s_y, 1)
                            dve.wait_ge(s_yo, 16 * 8)
                        else:
                            dve.wait_ge(s_used, Q_G)
                        vt_steps(half, (7, 6, 5))
                    if rel == 2:
                        vt_steps(half, (4, 3, 2))
                    if rel == 3:
                        vt_steps(half, (1, 0))
                        block_diagonal(half)
                    if rel == 7:
                        dve.wait_ge(s_vtr, 2 * half + 2)
                        w_steps(half, (0, 1, 2, 3))
                    if rel == 8:
                        w_steps(half, (4, 5, 6))
                    if rel == 9:
                        w_steps(half, (7,))
                        w_steps(half, (8,), s_w)
                        dve.wait_ge(s_w, half + 1)
                        dve.wait_ge(s_s, 4 * (half + 1))
                        scan_inside(half, (1, 2, 3, 4))
                    if rel == 10:
                        scan_inside(half, (5, 6, 7))
                        scan_over(half)
                    if rel == 11:
                        pad_k(half)
                        scan_back(half, (0, 1, 2))
                    if rel == 12:
                        scan_back(half, (3, 4, 5))
                        scan_back(half, (6,), s_st)
                        dve.wait_ge(s_st, half + 1)
            lo(Q_GLU, 0)
            for k in range(8):
                dve.wait_ge(s_ysh, k + 1)
                tt(ys_lo[:, k, :].rearrange("p (n j) -> p j n", j=STEP),
                   yraw[:, k, :].rearrange("p (j n) -> p j n", j=STEP),
                   ys_hi[:, k, :].rearrange("p (n j) -> p j n", j=STEP).bitcast(F32), ALU.subtract)\
                    .then_inc(s_ysl, 1)
            lo(Q_GLU + 1, 1)

            base_n = lk.n
            with dve.Fori(0, 4) as r:
                for i in range(2):
                    q = Q_GLU + 4 * r + 2 * i + 2
                    lo(q, (2 * i + 2) % RAW)
                    lo(q + 1, (2 * i + 3) % RAW)
                    j = r * 2 + i
                    n = base_n + j * 3
                    dve.wait_ge(s_gin, j * 48 + 48)
                    dve.wait_ge(s_sgt, j + 1)
                    tt(gm[:], (dn, ex)[i][:, 0:2, :], sgt[:], ALU.mult).then_inc(s_link, 1)
                    tt(gin[:, 0, :, :], gin[:, 0, :, :], gin[:, 1, :, :], ALU.mult).then_inc(s_link, 1)
                    dve.wait_ge(s_link, n + 1)
                    tt(gm[:], gm[:], gin[:, 2, :, :], ALU.mult).then_inc(s_link, 1)
                    dve.wait_ge(s_link, n + 3)
                    tt(gm[:], gm[:], gin[:, 0, :, :], ALU.add).then_inc(s_gm, 1)
                    dve.wait_ge(s_mh, j + 1)
                    tt(mx_lo[:, bass.ds(2 * j, 2), :], gm[:], mx_hi[:, bass.ds(2 * j, 2), :].bitcast(F32),
                       ALU.subtract).then_inc(s_ml, 1)
                    dve.wait_ge(s_ml, j + 1)
            lk.n = base_n + 24

            def residual(c, banks):
                for t in range(TT):
                    stt(x1[:, t, bass.ds(c * 512, 512)], x1[:, t, bass.ds(c * 512, 512)], ALPHA,
                        banks[:, t, :], ALU.mult, ALU.add).then_inc(s_wof, 1)
                dve.wait_ge(s_wof, c * 4 + 4)
                for t in range(TT):
                    dve.bn_stats(bst[:, t, bass.ds(c, 1), :].rearrange("p o s -> p (o s)"),
                                 x1[:, t, bass.ds(c * 512, 512)]).then_inc(s_bst, 1)

            def wo_chunk(c, banks):
                dve.wait_ge(s_used, Q_WO + 4 * c + 4)
                residual(c, banks)

            dve.wait_ge(s_res, 16)
            for c in range(3):
                for i in range(4):
                    lo(Q_WO + 4 * c + i + 2, (i + 2) % RAW)
                wo_chunk(c, (dn, ex)[c % 2])
            lo(Q_WO + 14, 2)
            lo(Q_WO + 15, 3)
            wo_chunk(3, ex)
            dve.wait_ge(s_bst, 16)
            for t in range(TT):
                lk.go(dve.bn_aggr(mv[:, t, :], bst[:, t, :, :]))
            lk.wait()
            row_scale(slice(0, TT), TT + 1)
            dve.wait_ge(s_lnp[1], 64)
            for t in range(TT):
                scale_rows(x1, lng1, t, TT + t + 1)
                if t % 2 == 0:
                    shift_rows(x1, lnb1, t, TT + t + 1)
            for i in range(3):
                lo_expert(0, i)

            def rv(i):
                return R[:, i, :, :]

            def rg(i):
                return R[:, i, :, :].rearrange("p t (g e) -> p t g e", e=EP)

            def rs(i):
                return R[:, i, :, 0:EG]

            def over_e(ap):
                return ap.unsqueeze(3).to_broadcast([P, TT, EG, EP])

            def over_16(ap):
                return ap.unsqueeze(2).to_broadcast([P, TT, E])

            dve.wait_ge(s_const2, 2)
            for t in range(TT):
                dve.wait_ge(s_log, t + 1)
                tt(R[:, 0, t, :], sets[t % 2][:, 0, 0:E], brb[:], ALU.add).then_inc(s_lgc, 1)
            dve.wait_ge(s_lgc, TT)
            one = R[:, 1, :, 0]
            link(dve.tensor_reduce(one, rv(0), AX.X, ALU.max))
            link(tt(rv(0), rv(0), over_16(one), ALU.subtract))
            exp_of(rv(2), rv(0), rv(3), rv(4), rv(5), rv(6))
            link(dve.tensor_reduce(one, rv(2), AX.X, ALU.add))
            link(dve.reciprocal(one, one))
            link(tt(rv(2), rv(2), over_16(one), ALU.mult))
            place_e = eio[:, 1, :].rearrange("p (g e) -> p g e", e=EP).unsqueeze(1).to_broadcast([P, TT, EG, EP])

            def first_max(p_, m, oh, w_):
                link(dve.tensor_reduce(rs(m), rg(p_), AX.X, ALU.max))
                link(tt(rg(w_), rg(p_), over_e(rs(m)), ALU.is_equal))
                link(tt(rg(w_), rg(w_), place_e, ALU.mult))
                link(dve.tensor_reduce(rs(23), rg(w_), AX.X, ALU.max))
                link(tt(rg(oh), rg(w_), over_e(rs(23)), ALU.is_equal))

            first_max(2, 7, 8, 9)
            link(stt(rv(10), rv(8), -2.0, rv(2), ALU.mult, ALU.add))
            first_max(10, 11, 12, 9)
            link(tt(rs(13), rs(7), rs(11), ALU.add))
            link(dve.tensor_reduce(one, rs(13), AX.X, ALU.max))
            link(tt(rs(14), rs(13), one.unsqueeze(2).to_broadcast([P, TT, EG]), ALU.is_equal))
            link(tt(rs(14), rs(14), gio[:].unsqueeze(1).to_broadcast([P, TT, EG]), ALU.mult))
            link(dve.tensor_reduce(one, rs(14), AX.X, ALU.max))
            link(tt(rs(15), rs(14), one.unsqueeze(2).to_broadcast([P, TT, EG]), ALU.is_equal))
            lk.go(tt(rg(16), rg(8), over_e(rs(15)), ALU.mult))
            lk.go(tt(rg(17), rg(12), over_e(rs(15)), ALU.mult))
            lk.wait()
            tt(mask[:], rv(16), rv(17), ALU.add).then_inc(s_msk, 1)
            link(tt(rs(13), rs(13), rs(15), ALU.mult))
            link(tt(rs(7), rs(7), rs(15), ALU.mult))
            link(tt(rs(11), rs(11), rs(15), ALU.mult))
            link(dve.tensor_reduce(one, rs(13), AX.X, ALU.add))
            link(dve.reciprocal(one, one))
            for k, i in enumerate((7, 11)):
                link(dve.tensor_reduce(R[:, 19, :, 0], rs(i), AX.X, ALU.add))
                link(tt(wts[:, :, k], R[:, 19, :, 0], one, ALU.mult))
            dve.wait_ge(s_rnk, 1)
            link(dve.tensor_copy(R[:, 20, :, :], dn[:, 3, 0:TT * E].rearrange("p (t e) -> p t e", t=TT)))
            cnt, ov, inc, kk = R[:, 21, 0, :], R[:, 21, 1, :], R[:, 21, 2, :], R[:, 21, 3, :]
            link(dve.tensor_copy(cnt, dn[:, 3, TT * E:(TT + 1) * E]))
            link(ts(ov, cnt, float(P), None, ALU.is_gt))
            for m in (2, 3):
                link(stt(ov, cnt, float(m * P), ov, ALU.is_gt, ALU.add))
            link(dve.tensor_tensor_scan(inc, ones[:], ov, 0.0, ALU.mult, ALU.add))
            link(tt(kk, inc, ov, ALU.subtract))
            link(stt(kk, kk, float(P), eio[:, 2, :], ALU.mult, ALU.add))
            link(ts(rv(22), rv(20), float(P), None, ALU.is_ge))
            link(tt(rv(22), rv(22), kk.unsqueeze(1).to_broadcast([P, TT, E]), ALU.mult))
            link(tt(rv(22), rv(22), rv(20), ALU.add))
            link(stt(rv(22), eio[:, 0, :].unsqueeze(1).to_broadcast([P, TT, E]), float(P), rv(22),
                     ALU.mult, ALU.add))
            for k, i in enumerate((16, 17)):
                link(tt(rv(9), rv(i), rv(22), ALU.mult))
                link(dve.tensor_reduce(R[:, 19, :, k], rv(9), AX.X, ALU.add))
            dve.tensor_copy(dest[:], R[:, 19, :, 0:2]).then_inc(s_dst, 1)
            link(tt(ovk[:], inc.unsqueeze(1).to_broadcast([P, NOVER + 1, E]),
                    ovn[:].unsqueeze(2).to_broadcast([P, NOVER + 1, E]), ALU.is_le))
            link(dve.tensor_reduce(R[:, 23, 0, 0:NOVER + 1], ovk[:], AX.X, ALU.add))
            link(ts(R[:, 23, 0, 0:NOVER + 1], R[:, 23, 0, 0:NOVER + 1], float(E - 1), None, ALU.min))
            lk.go(dve.tensor_copy(tab[:, 0:E], eio[:, 0, :]))
            lk.go(dve.tensor_copy(tab[:, E:NBLK + 1], R[:, 23, 0, 0:NOVER + 1]))
            lk.wait()
            ts(tab[:, NBLK + 1:NBLK + 2], inc[:, E - 1:E], float(E), None, ALU.add).then_inc(s_tab, 1)

            def block_rows_lo(n, half):
                for c in range(2):
                    dve.wait_ge(s_xh, n * 4 + 2 * half + c + 1)
                    k = 8 * half + 4 * c
                    tt(xg_lo[:, k:k + 4, :], dn[:, c, :].rearrange("p (k n) -> p k n", k=4),
                       xg_hi[:, k:k + 4, :].bitcast(F32), ALU.subtract).then_inc(s_xl, 1)

            def this_block(b):
                for i in range(3, PB):
                    lo_expert(b, i)
                    if i == 18:
                        dve.wait_ge(s_used, b * PB + (Q_MOE + 16))
                        for c in range(2):
                            dve.wait_ge(s_sil, b * 2 + c + 1)
                            tt(hid[:, c * 512:(c + 1) * 512], sil[:, c * 512:(c + 1) * 512], dn[:, 2 + c, :],
                               ALU.mult).then_inc(s_hm, 1)
                    if i == 19:
                        for c in range(2):
                            dve.wait_ge(s_hh, b * 2 + c + 1)
                            tt(h_lo[:, 4 * c:4 * c + 4, :], dn[:, 2 + c, :].rearrange("p (k n) -> p k n", k=4),
                               h_hi[:, 4 * c:4 * c + 4, :].bitcast(F32), ALU.subtract).then_inc(s_hl, 1)
                        block_rows_lo(b + 1, 0)
                    if i == 22:
                        block_rows_lo(b + 1, 1)

            def next_block(b):
                for i in range(PB, PB + 3):
                    lo_expert(b, i)

            block_rows_lo(0, 0)
            block_rows_lo(0, 1)
            with dve.Fori(0, E - 1) as b:
                this_block(b)
                next_block(b)
            blocks = dve.value_load(tab[0:1, NBLK + 1:NBLK + 2], min_val=E, max_val=NBLK)
            with dve.Fori(E - 1, NBLK) as b:
                with dve.If(b < blocks):
                    this_block(b)
                with dve.If(b < blocks - 1):
                    next_block(b)

            for t in range(TT):
                dve.wait_ge(s_xa, t + 1)
                dve.wait_ge(s_yr[t], 32)
                link(stt(xr[:, t, :], yg[:, t, 0, :], wts[:, t, 0:1], xr[:, t, :], ALU.mult, ALU.add))
                link(stt(xr[:, t, :], yg[:, t, 1, :], wts[:, t, 1:2], xr[:, t, :], ALU.mult, ALU.add))
                stats(xr, t)
                row_scale(slice(t, t + 1), TT + 2 + t)
            dve.wait_ge(s_lnp[2], 32)
            scale_rows(xr, lng2, TT - 1, 3 * TT)
            shift_rows(xr, lnb2, TT - 1, 2 * TT + 1)

        @block.tensor
        def _(pe):
            pe.wait_ge(s_const, 4)
            for t in range(TT):
                pe.wait_ge(s_rows[t], 1)
                for b in range(4):
                    if t >= 2:
                        pe.wait_ge(s_trl, 4 * (t - 2) + b + 1)
                    for k in range(4):
                        mm = pe.transpose(sets[t % 2][:, b, k * P:(k + 1) * P],
                                          xin[:, t, (4 * b + k) * P:(4 * b + k + 1) * P], ident[:])
                    mm.then_inc(s_tr, 1)

            def three(o, w, wl, r_, rl, first, last):
                pe.matmul(o, lhsT=w, rhs=r_, start=first, stop=False)
                pe.matmul(o, lhsT=w, rhs=rl, start=False, stop=False)
                return pe.matmul(o, lhsT=wl, rhs=r_, start=False, stop=last)

            def unit_piece(q, s, par, rhs, k0, first, last, banks=dn):
                hi_, lo_ = rhs
                h = whi[:, s % RD, :].rearrange("p (k n) -> p k n", k=8)
                l = wlo[:, s % RD, :].rearrange("p (k n) -> p k n", k=8)
                pe.wait_ge(s_lo, q + 1)
                for k in range(8):
                    for c in range(2):
                        cs = slice(c * P, (c + 1) * P)
                        mm = three(banks[:, 2 * par + c, :], h[:, k, cs], l[:, k, cs],
                                   hi_[:, k0 + k, :], lo_[:, k0 + k, :], first and k == 0, last and k == 7)
                mm.then_inc(s_used, 1)

            def banks_free(n):
                if n < 2:
                    return
                m = n - 2
                if m < 12:
                    pe.wait_ge((s_cx, s_cm, s_pa)[m % 3], m // 3 + 1)
                elif m < 16:
                    pe.wait_ge(s_cp, 2 * (m - 11))
                elif m < 40:
                    pe.wait_ge(s_cp, 8 + 2 * (m - 15))

            def parameter_transposes():
                pe.wait_ge(s_prm, 16 * N_PRM)
                pe.wait_ge(s_trl, 16)
                pe.wait_ge(s_nat, 1)
                for i in range(3):
                    pe.transpose(ex[:, 0, i * GG:(i + 1) * GG], nat[:, i, :], ident[0:GG, 0:GG])
                pe.transpose(ex[0:2 * H, 0, 3 * GG:4 * GG], dnat[:], ident[0:GG, 0:GG])
                mm = pe.transpose(ex[:, 0, 4 * GG:4 * GG + 24], cwn[:], ident[0:24, 0:24])
                mm.then_inc(s_ptr, 1)

            def c_transposes():
                pe.wait_ge(s_pcp, 3)
                for c in range(2):
                    for a in range(8):
                        mm = pe.transpose(ex[:, 2 * c + a // 4, (a % 4) * P:(a % 4 + 1) * P],
                                          cnat[:, c, a, :, :].rearrange("p o n -> p (o n)"), ident[:])
                mm.then_inc(s_ctr, 1)

            def vt_transposes(half, c):
                if c == 0:
                    pe.wait_ge(s_vt, half + 1)
                    if half == 0:
                        pe.wait_ge(s_cc, 8)
                    else:
                        pe.wait_ge(s_yg, 4)
                else:
                    pe.wait_ge(s_v, 8 * half + 4)
                for g in range(HG):
                    mm = pe.transpose(ex[:, g // 4, (g % 4) * P:(g % 4 + 1) * P],
                                      VT[:, c, g, :, :].rearrange("p i h -> p (i h)"), ident[:])
                mm.then_inc(s_vtr, 1)

            def chunk_inputs(half):
                pe.wait_ge(s_u, 16 * 8 * (half + 1))
                pe.wait_ge(s_v, 8 * (half + 1))
                for c in range(2):
                    for g in range(HG):
                        for r in range(2):
                            slot = c * HG + g
                            mm = pe.matmul(ex[r * N:(r + 1) * N, slot // 8, (slot % 8) * NCH:(slot % 8 + 1) * NCH],
                                           lhsT=V[:, c, g, r * N:(r + 1) * N], rhs=U[:, 2 * g + r, :],
                                           start=True, stop=True)
                mm.then_inc(s_bu, 1)

            def kernels(half):
                pe.wait_ge(s_w, half + 1)
                pe.wait_ge(s_s, 4 * (half + 1))
                for g in range(HG):
                    for c in range(2):
                        mm = pe.matmul(ex[0:2 * H, g // 4, (g % 4) * P:(g % 4 + 1) * P],
                                       lhsT=Bbd[:, c, g, :, :].rearrange("p r h -> p (r h)"),
                                       rhs=W[:, c, g, 0:STEP, :].rearrange("p d h -> p (d h)"),
                                       start=(c == 0), stop=(c == 1))
                mm.then_inc(s_k, 1)

            def outputs(half):
                pe.wait_ge(s_st, half + 1)
                pe.wait_ge(s_m, 16 * 8 * (half + 1))
                pe.wait_ge(s_kp, half + 1)
                for g in range(HG):
                    for r in range(2):
                        o = ex[:, 2 * (g // 8) + r, (g % 8) * NCH:(g % 8 + 1) * NCH]
                        rows = slice(r * N, (r + 1) * N)
                        pe.matmul(o, lhsT=M[:, g, r, :], rhs=U[:, 2 * g + r, :], start=True, stop=False)
                        for c in range(2):
                            mm = pe.matmul(o[:, 1:], lhsT=W[rows, c, g, 1:, :].rearrange("p d h -> p (d h)"),
                                           rhs=S[rows, c, g, 0:NCH - 1], start=False, stop=(c == 1))
                mm.then_inc(s_y, 1)

            pe.wait_ge(s_trl, 16)
            for q in range(Q_GLU):
                n = unit_of(q)
                if q < Q_OA or q >= Q_G:
                    if q % 2 == 0:
                        banks_free(n)
                    unit_piece(q, q % RAW, n % 2, (xT_hi, xT_lo), 8 * (q % 2), q % 2 == 0, q % 2 == 1)
                else:
                    banks_free(n)
                    if q == Q_OA:
                        pe.wait_ge(s_pal, 4)
                    unit_piece(q, q % RAW, n % 2, (pa_hi, pa_lo), 0, True, True)
                if q == 1:
                    parameter_transposes()
                if q == 3:
                    c_transposes()
                if q >= Q_G:
                    half, rel = divmod(q - Q_G, 16)
                    if rel == 4:
                        vt_transposes(half, 0)
                    if rel == 5:
                        vt_transposes(half, 1)
                    if rel == 6:
                        chunk_inputs(half)
                    if rel == 9:
                        kernels(half)
                    if rel == 11:
                        outputs(half)
            pe.wait_ge(s_ysl, 8)
            pe.wait_ge(s_yg, 8)
            with pe.Fori(0, 4) as r:
                for i in range(2):
                    j = r * 2 + i
                    q = j * 2 + Q_GLU
                    if i == 0:
                        pe.wait_ge(s_cp, 56)
                    pe.wait_ge(s_gm, j + 1)
                    unit_piece(q, (2 * i) % RAW, 0, (ys_hi, ys_lo), 0, True, True, (dn, ex)[i])
                    unit_piece(q + 1, (2 * i + 1) % RAW, 1, (ys_hi, ys_lo), 0, True, True, (dn, ex)[i])

            pe.wait_ge(s_ml, 7)
            for c in range(4):
                banks = (dn, ex)[c % 2]
                if c == 1:
                    pe.wait_ge(s_gm, 10)
                if c >= 2:
                    pe.wait_ge(s_wof, 4 * (c - 1))
                for i in range(4):
                    q = Q_WO + 4 * c + i
                    h = whi[:, q % RD, :].rearrange("p (k n) -> p k n", k=4)
                    l = wlo[:, q % RD, :].rearrange("p (k n) -> p k n", k=4)
                    pe.wait_ge(s_lo, q + 1)
                    if c == 0 and i == 3:
                        pe.wait_ge(s_ml, 8)
                    for k in range(4):
                        kk = 4 * i + k
                        for t in range(TT):
                            ts_ = slice(t * P, (t + 1) * P)
                            mm = tokens_by(pe, banks[:, t, :], mx_hi[:, kk, ts_], mx_lo[:, kk, ts_],
                                           h[:, k, :], l[:, k, :], kk == 0, kk == KD - 1)
                    mm.then_inc(s_used, 1)

            def router(t):
                pe.wait_ge(s_x1c, 4 * t + 4)
                for k in range(KD):
                    mm = pe.matmul(sets[t % 2][:, 0, 0:E], lhsT=x1T[:, t % 2, k, :], rhs=wr[:, k, :],
                                   start=(k == 0), stop=(k == KD - 1))
                mm.then_inc(s_log, 1)

            pe.wait_ge(s_wof, 16)
            pe.wait_ge(s_lnp[1], 64)
            for t in range(TT):
                pe.wait_ge(s_rows[t], 2)
                if t >= 2:
                    pe.wait_ge(s_lgc, t - 1)
                for b in range(4):
                    for k in range(4):
                        mm = pe.transpose(sets[t % 2][:, b, k * P:(k + 1) * P],
                                          x1[:, t, (4 * b + k) * P:(4 * b + k + 1) * P], ident[:])
                    mm.then_inc(s_x1t, 1)
                if t >= 1:
                    router(t - 1)
            router(TT - 1)
            pe.wait_ge(s_const2, 2)
            pe.wait_ge(s_msk, 1)
            for t in range(TT + 1):
                o = dn[:, 3, t * E:(t + 1) * E]
                for t_ in range(t):
                    mm = pe.matmul(o, lhsT=onesb[:], rhs=mask[:, t_, :], start=(t_ == 0), stop=(t_ == t - 1 and t == TT))
                if t < TT:
                    mm = pe.matmul(o, lhsT=tri[:], rhs=mask[:, t, :], start=(t == 0), stop=True)
            mm.then_inc(s_rnk, 1)

            def rows_transpose(n, half):
                if half == 0:
                    pe.wait_ge(s_xg, n * 16 + 16)
                else:
                    pe.wait_ge(s_xl, n * 4 + 2)
                for k in range(8):
                    mm = pe.transpose(dn[:, k // 4, (k % 4) * P:(k % 4 + 1) * P],
                                      xg[:, (8 * half + k) * P:(8 * half + k + 1) * P], ident[:])
                mm.then_inc(s_xt, 1)

            def expert_matmuls(q, s, banks, xh, xl, k0, first, last):
                h = mhi[:, s % RM, :].rearrange("p (k n) -> p k n", k=2)
                l = mlo[:, s % RM, :].rearrange("p (k n) -> p k n", k=2)
                pe.wait_ge(s_lo, q + 1)
                for k in range(2):
                    for c in range(2):
                        cs = slice(c * 512, (c + 1) * 512)
                        mm = tokens_by(pe, banks[c], xh[:, k0 + k, :], xl[:, k0 + k, :], h[:, k, cs], l[:, k, cs],
                                       first and k == 0, last and k == 1)
                mm.then_inc(s_used, 1)

            def expert_piece(b, i):
                q = Q_MOE + b * PB + i
                i = i % PB
                if i < 16:
                    banks = [dn[:, 2 * (i // 8) + c, :] for c in range(2)]
                    expert_matmuls(q, i % RM, banks, xg_hi, xg_lo, 2 * (i % 8), i % 8 == 0, i % 8 == 7)
                else:
                    banks = [ex[:, 2 * ((i - 16) // 4) + c, :] for c in range(2)]
                    expert_matmuls(q, i % RM, banks, h_hi, h_lo, 2 * (i % 4), i % 4 == 0, i % 4 == 3)

            def this_block(b):
                for i in range(3, 16):
                    expert_piece(b, i)
                pe.wait_ge(s_sil, b * 2 + 2)
                rows_transpose(b + 1, 0)
                for c in range(2):
                    pe.wait_ge(s_hm, b * 2 + c + 2)
                    for k in range(4):
                        mm = pe.transpose(dn[:, 2 + c, k * P:(k + 1) * P],
                                          hid[:, (4 * c + k) * P:(4 * c + k + 1) * P], ident[:])
                    mm.then_inc(s_ht, 1)
                pe.wait_ge(s_hl, b * 2 + 2)
                pe.wait_ge(s_yb, b * 2 + 1)
                for i in range(16, 19):
                    expert_piece(b, i)
                rows_transpose(b + 1, 1)
                for i in range(19, PB):
                    expert_piece(b, i)

            def next_block(b):
                pe.wait_ge(s_xl, b * 4 + 8)
                for i in range(PB, PB + 3):
                    expert_piece(b, i)

            pe.wait_ge(s_dst, 1)
            rows_transpose(0, 0)
            rows_transpose(0, 1)
            pe.wait_ge(s_xl, 4)
            for i in range(3):
                expert_piece(0, i)
            with pe.Fori(0, E - 1) as b:
                this_block(b)
                next_block(b)
            pe.wait_ge(s_tab, 1)
            blocks = pe.value_load(tab[0:1, NBLK + 1:NBLK + 2], min_val=E, max_val=NBLK)
            with pe.Fori(E - 1, NBLK) as b:
                with pe.If(b < blocks):
                    this_block(b)
                with pe.If(b < blocks - 1):
                    next_block(b)


_INS = ["x", "in_g", "in_b", "w_in", "conv_w", "w_out_a", "ssm_a_re", "ssm_a_im", "ssm_log_dt",
        "ssm_b_re", "ssm_b_im", "ssm_c_re", "ssm_c_im", "ssm_d", "w_glu", "w_o",
        "ln1_g", "ln1_b", "ln2_g", "ln2_b", "w_router", "b_router", "w_gate", "w_up", "w_down"]


def kernel(**inputs):
    import numpy as _np
    import concourse.bacc as _bacc
    from concourse import mybir as _mybir
    from concourse.bass_utils import run_bass_kernel_spmd as _run

    nc = _bacc.Bacc("TRN2", target_bir_lowering=False, num_devices=1)
    arrays, args = {}, []
    for name in _INS:
        a = _np.ascontiguousarray(inputs[name])
        arrays[f"in_{name}"] = a
        args.append(nc.dram_tensor(f"in_{name}", a.shape, _mybir.dt.from_np(a.dtype), kind="ExternalInput").ap())
    out = nc.dram_tensor("out", (1, T, D), _mybir.dt.float32, kind="ExternalOutput").ap()
    build_trunk(nc, *args, out)
    r = _run(nc, [arrays], core_ids=[0])
    return r.results[0]["out"]
```

```python
import math

import numpy as np

import concourse.bass as bass
from concourse import mybir
from contextlib import ExitStack

F32 = mybir.dt.float32
F32R = mybir.dt.float32r
I32 = mybir.dt.int32
BF16 = mybir.dt.bfloat16
ALU = mybir.AluOpType
ACT = mybir.ActivationFunctionType
AX = mybir.AxisListType

P = 128
T = 512
D = 2048
DC = 1024
DS = 1024
CONV_WIDTH = 3
G, H, N = 64, 16, 64
E, EG, EP = 16, 4, 4
F = 1024
EPS = 1e-5
ALPHA = 2.0 ** 0.25
TT = T // P
KD = D // P
KF = F // P
PIECE = 2048
UC = 256

STEP = 8
NCH = T // STEP
GG = G // 2
HG = GG // 2

N_U, N_CONV, N_OA, N_G, N_GLU, N_WO = 8, 24, 8, 32, 16, 16
Q_CONV = 0
Q_U = Q_CONV + N_CONV
Q_OA = Q_U + N_U
Q_G = Q_OA + N_OA
Q_GLU = Q_G + N_G
Q_WO = Q_GLU + N_GLU
Q_MOE = Q_WO + N_WO
PB = 24
NBLK = E + (2 * T - E) // P
NOVER = NBLK - E
COUNTS = NBLK + 2
RAW = 4
RD = 2
RM = 4
RAWM = 12
AHEAD = RM + RAWM

N_ZERO = 2 * (NOVER + 1)
N_PRM = 10

MAGIC = 1.5 * 2.0 ** 23


def two_pi_parts():
    c1 = math.floor(2 * math.pi * 2 ** 7) / 2 ** 7
    c2 = math.floor((2 * math.pi - c1) * 2 ** 19) / 2 ** 19
    return c1, c2, 2 * math.pi - c1 - c2


class Link:

    def __init__(self, eng, sem):
        self.eng, self.sem, self.n = eng, sem, 0

    def go(self, ins):
        self.n += 1
        ins.then_inc(self.sem, 1)

    def wait(self):
        self.eng.wait_ge(self.sem, self.n)

    def link(self, ins):
        self.go(ins)
        self.wait()


def unit_of(q):
    if q < Q_OA:
        return q // 2
    return 16 + q - Q_OA if q < Q_G else 24 + (q - Q_G) // 2


def tokens_by(pe, o, x_hi, x_lo, w_hi, w_lo, first, last):
    pe.matmul(o, lhsT=x_hi, rhs=w_hi, start=first, stop=False)
    pe.matmul(o, lhsT=x_lo, rhs=w_hi, start=False, stop=False)
    return pe.matmul(o, lhsT=x_hi, rhs=w_lo, start=False, stop=last)


def build_trunk(nc, x, in_g, in_b, w_in, conv_w, w_out_a, ssm_a_re, ssm_a_im, ssm_log_dt,
                ssm_b_re, ssm_b_im, ssm_c_re, ssm_c_im, ssm_d, w_glu, w_o,
                ln1_g, ln1_b, ln2_g, ln2_b, w_router, b_router, w_gate, w_up, w_down, out):
    ctx = ExitStack()
    with ctx:
        base = nc.sbuf_base + (-nc.sbuf_base) % 64
        KB = 1024

        def at(name, shape, kb, dtype=F32):
            return nc.alloc_sbuf_tensor_at(name, shape, dtype, offset=base + int(kb * KB))

        raw = at("raw", [P, RAW, PIECE], 0)
        whi = at("whi", [P, RD, PIECE], 32, F32R)
        wlo = at("wlo", [P, RD, PIECE], 48, F32R)
        mhi = at("mhi", [P, RM, PIECE], 32, F32R)
        mlo = at("mlo", [P, RM, PIECE], 64, F32R)
        xT_hi = at("xT_hi", [P, KD, T], 64, F32R)
        xT_lo = at("xT_lo", [P, KD, T], 96, F32R)
        mx_hi = at("mx_hi", [P, KD, T], 64, F32R)
        mx_lo = at("mx_lo", [P, KD, T], 96, F32R)
        xin = at("xin", [P, TT, D], 128)
        lng = at("lng", [P, D], 160)
        lnb = at("lnb", [P, D], 168)
        pa_hi = at("pa_hi", [P, 8, T], 128, F32R)
        pa_lo = at("pa_lo", [P, 8, T], 144, F32R)
        ust = at("ust", [P, 2, T], 160)
        cx = at("cx", [P, 2, T], 164)
        cv = at("cv", [P, 2, T + 2], 168)
        ct = at("ct", [P, 2, T], 172.5)
        zrow = at("zrow", [P, 1024], 194)
        cnat = at("cnat", [P, 2, 8, 2, N], 176.5)
        prm = at("prm", [P, 30, GG], 184.5)
        nat = at("nat", [GG, 3, P], 188.25)
        braw = at("braw", [P, 2, GG, H], 189.75)
        Bb = at("Bb", [P, 2, GG, H], 194)
        Cc = at("Cc", [P, 2, GG, H], 198)
        A1 = at("A1", [P, 3, GG], 202)
        P8 = at("P8", [P, STEP, 3, GG], 202.375)
        VT = at("VT", [P, 2, HG, STEP, H], 128)
        W = at("W", [P, 2, HG, STEP + 1, H], 128)
        V = at("V", [P, 2, HG, P], 146)
        kpd = at("kpd", [2 * H, HG, 15, H], 146)
        M = at("M", [P, HG, 2, P], 146)
        U = at("U", [P, 2 * HG, NCH], 162)
        S = at("S", [P, 2, HG, NCH], 170)
        t1 = at("t1", [P, 2, HG, H], 178)
        t2 = at("t2", [P, 2, HG, H], 180)
        Bbd = at("Bbd", [P, 2, HG, 2, H], 182)
        yst = at("yst", [P, HG, 2, NCH], 178)
        sgst = at("sgst", [P, 2, T], 186)
        dgv = at("dgv", [2 * H, GG], 193.75)
        dmask = at("dmask", [2 * H, H], 193.875)
        dsk = at("dsk", [2 * H, GG, H], 190)
        ys_hi = at("ys_hi", [P, 8, T], 128, F32R)
        ys_lo = at("ys_lo", [P, 8, T], 144, F32R)
        yraw = at("yraw", [P, 8, T], 160)
        gin = at("gin", [P, 3, 2, T], 176)
        sgt = at("sgt", [P, 2, T], 188)
        gm = at("gm", [P, 2, T], 192)
        x1 = at("x1", [P, TT, D], 128)
        lng1 = at("lng1", [P, D], 160)
        lnb1 = at("lnb1", [P, D], 168)
        x1T = at("x1T", [P, 2, KD, P], 176)
        lgT = at("lgT", [E, TT, P], 192)
        wr = at("wr", [P, KD, E], 196)
        tri = at("tri", [P, P], 197, BF16)
        onesb = at("onesb", [P, P], 197.25, BF16)
        mask = at("mask", [P, TT, E], 197.5, BF16)
        ones = at("ones", [P, E], 197.75)
        square = at("square", [P, P], 198.5)
        brb = at("brb", [P, E], 198)
        eio = at("eio", [P, 3, E], 198.125)
        gio = at("gio", [P, EG], 198.375)
        R = at("R", [P, 24, TT, E], 198.5)
        RI = at("RI", [P, TT, E], 204.5, I32)
        ovk = at("ovk", [P, NOVER + 1, E], 194)
        ovn = at("ovn", [P, NOVER + 1], 195.5)
        xg_hi = at("xg_hi", [P, KD, P], 104, F32R)
        xg_lo = at("xg_lo", [P, KD, P], 112, F32R)
        hid = at("hid", [P, F], 120)
        h_hi = at("h_hi", [P, KF, P], 124, F32R)
        h_lo = at("h_lo", [P, KF, P], 160, F32R)
        ybl = at("ybl", [P, D], 164)
        xg = at("xg", [P, D], 172)
        raw2 = at("raw2", [P, 4, PIECE], 128)
        raw3 = at("raw3", [P, 1, PIECE], 96)
        raw4 = at("raw4", [P, 3, PIECE], 180)
        xr = at("xr", [P, TT, D], 0)
        lng2 = at("lng2", [P, D], 128)
        lnb2 = at("lnb2", [P, D], 136)
        yg = at("yg", [P, TT, 2, D], 32)
        place = [205.5]

        def small(name, shape, dtype=F32):
            t = at(name, shape, place[0], dtype)
            words = 1
            for n in shape[1:]:
                words *= n
            place[0] += math.ceil(words * 4 / 32) * 32 / KB
            return t

        ident = small("ident", [P, P])
        cwn = small("cwn", [CONV_WIDTH * 8, P])
        dnat = small("dnat", [GG, 2 * H])
        ldt = small("ldt", [GG, 2])
        cw = small("cw", [P, 8, 3])
        mv = small("mv", [P, TT, 2])
        rstd = small("rstd", [P, TT])
        nmr = small("nmr", [P, TT])
        tmp4 = small("tmp4", [P, TT])
        bst = small("bst", [P, TT, 4, 6])
        tab = small("tab", [P, COUNTS + NBLK], I32)
        dest = small("dest", [P, TT, 2], I32)
        back = small("back", [P, TT, 2], I32)
        wts = small("wts", [P, TT, 2])
        bidx = small("bidx", [P, 1], I32)
        ahead = small("ahead", [P, 4])
        zeros = small("zeros", [P, NBLK + 1], I32)
        tokid = small("tokid", [P, TT], I32)
        assert base + place[0] * KB <= nc.sbuf_usable_end, (base + place[0] * KB, nc.sbuf_usable_end)

        dn = ctx.enter_context(nc.psum_tensor("dn", [P, 4, 512], F32))
        ex = ctx.enter_context(nc.psum_tensor("ex", [P, 4, 512], F32))
        sets = (ex, dn)
        sets1 = (dn, ex)

        x0_d = nc.dram_tensor("x0_d", [T, D], F32).ap()
        u_d = nc.dram_tensor("u_d", [DS, STEP, NCH], F32).ap()
        ya_d = nc.dram_tensor("ya_d", [D, T], F32).ap()
        sg_d = nc.dram_tensor("sg_d", [2 * D, T], F32).ap()
        kp_d = nc.dram_tensor("kp_d", [GG, 2, H, 15 * H], F32).ap()
        y_d = nc.dram_tensor("y_d", [DS, STEP, NCH], F32).ap()
        x1_d = nc.dram_tensor("x1_d", [T, D], F32).ap()
        tok_d = nc.dram_tensor("tok_d", [(NBLK + 1) * P, 1], I32).ap()
        yb_d = nc.dram_tensor("yb_d", [NBLK * P, D], F32).ap()

        def sem(name):
            return ctx.enter_context(nc.semaphore(name))

        s_raw = [sem(f"raw_loaded{i}") for i in range(RAW)]
        s_rawm = [sem(f"expert_piece_loaded{i}") for i in range(RAWM)]
        s_hi = sem("hi_written")
        s_lo = sem("lo_written")
        s_lop = sem("first_lo_written")
        s_used = sem("piece_used")
        s_link = sem("vector_link")
        s_plink = sem("pool_link")
        s_const = sem("constants_built")
        s_const2 = sem("router_constants_built")
        s_x = [sem(f"x_loaded{i}") for i in range(TT)]
        s_lnp = [sem("ln0_loaded"), sem("ln1_loaded"), sem("ln2_loaded")]
        s_prm = sem("parameters_loaded")
        s_ldt = sem("log_dt_loaded")
        s_nat = sem("log_dt_spread")
        s_zero = sem("token_table_cleared")
        s_ybz = sem("unused_rows_cleared")
        s_var = sem("variance_ready")
        s_sq = sem("root_ready")
        s_rs = sem("row_scale_ready")
        s_xn = sem("rows_normalised")
        s_xm = sem("rows_scaled")
        s_rows = [sem(f"rows_ready{i}") for i in range(TT)]
        s_tr = sem("rows_transposed")
        s_trh = sem("transposed_hi")
        s_trl = sem("transposed_lo")
        s_x0o = sem("x0_stored")
        s_cp = sem("copied_out")
        s_ust = [sem("ust_stored0"), sem("ust_stored1")]
        s_sgo = [sem("gate_stored0"), sem("gate_stored1")]
        s_cx = sem("xin_copied")
        s_pa = sem("conv_ready")
        s_pah = sem("conv_hi")
        s_pal = sem("conv_lo")
        s_ptr = sem("parameters_transposed")
        s_pcp = sem("parameters_copied")
        s_cm = sem("conv_input_ready")
        s_cz = sem("conv_padding_zeroed")
        s_bst = sem("ln1_statistics")
        s_ctr = sem("C_transposed")
        s_cc = sem("C_ready")
        s_ang = sem("angles_ready")
        s_sin = sem("sines_ready")
        s_u = sem("U_loaded")
        s_vt = sem("VT_ready")
        s_vtr = sem("VT_transposed")
        s_v = sem("V_ready")
        s_bu = sem("chunk_inputs_done")
        s_s = sem("chunk_inputs_ready")
        s_w = sem("W_ready")
        s_k = sem("K_done")
        s_kp = sem("K_padded")
        s_kps = sem("K_stored")
        s_m = sem("M_loaded")
        s_st = sem("states_ready")
        s_y = sem("y_done")
        s_yg = sem("y_gelu_ready")
        s_yo = sem("y_stored")
        s_yl = sem("y_loaded")
        s_ysh = sem("ys_hi_ready")
        s_ysl = sem("ys_lo_ready")
        s_gin = sem("glu_inputs_loaded")
        s_sgt = sem("glu_gate_ready")
        s_gm = sem("mixed_ready")
        s_mh = sem("mixed_hi")
        s_ml = sem("mixed_lo")
        s_wof = sem("w_o_banks_free")
        s_wt = sem("w_o_tile_done")
        s_res = sem("residual_loaded")
        s_x1o = sem("x1_then_blocks_stored")
        s_x1t = sem("x1_transposed")
        s_x1c = sem("x1T_copied")
        s_log = sem("logits_done")
        s_lgt = sem("logits_copied")
        s_lgx = sem("logits_transposed")
        s_lgc = sem("logits_taken")
        s_msk = sem("masks_ready")
        s_rnk = sem("ranks_done")
        s_dst = sem("destinations_ready")
        s_tab = sem("table_ready")
        s_sct = sem("tokens_scattered")
        s_bix = sem("block_tokens_loaded")
        s_xg = sem("block_rows_gathered")
        s_xt = sem("block_rows_transposed")
        s_xh = sem("block_hi")
        s_xl = sem("block_lo")
        s_sil = sem("silu_ready")
        s_hm = sem("hidden_ready")
        s_ht = sem("hidden_transposed")
        s_hh = sem("hidden_hi")
        s_hl = sem("hidden_lo")
        s_yb = sem("block_half_copied")
        s_yr = [sem(f"expert_rows_gathered{i}") for i in range(TT)]
        s_xr = [sem(f"residual_loaded{i}") for i in range(TT)]
        s_xa = sem("residual_scaled")
        s_out = sem("output_stored")

        block = ctx.enter_context(nc.Block())

        U_COL, XIN_COL, C_COL, B_COL, GA_COL = 3 * DC, 0, DC, 2 * DC, 3 * DC + DS
        w_in2, w_oa2, w_glu2, w_o2 = w_in[0], w_out_a[0], w_glu[0], w_o[0]

        def conv_col(unit):
            return (XIN_COL, C_COL, B_COL)[unit % 3] + unit // 3 * UC

        def piece_rows(w, k0, nk, c0, nc_):
            return w[k0 * P:(k0 + nk) * P, bass.ds(c0, nc_)].rearrange("(k p) n -> p k n", p=P)

        def raw_v(s, nk):
            return raw[:, s, :].rearrange("p (k n) -> p k n", k=nk)

        def expert_raw(s):
            for ring, first in ((raw4, 9), (raw3, 8), (raw2, 4), (raw, 0)):
                if s >= first:
                    return ring[:, s - first, :]

        halves = (slice(0, D // 2), slice(D // 2, D))

        def lo_count(b, i):
            return b * PB + (Q_MOE + i - RM + 1)

        @block.sync
        def _(sp):
            for t in range(TT):
                sp.dma_start(xin[:, t, :], x[0, t * P:(t + 1) * P, :]).then_inc(s_x[t], 16)

            def load(q, s, nk, src):
                sp.wait_ge(s_lo, q - RAW + 1)
                sp.dma_start(raw_v(s, nk), src).then_inc(s_raw[s], 16)

            for i in range(RAW):
                sp.dma_start(raw_v(i, 8), piece_rows(w_in2, 8 * (i % 2), 8, conv_col(i // 2), UC))\
                  .then_inc(s_raw[i], 16)
            sp.dma_start(nat[:, 0, :], ssm_a_re[0].rearrange("(g r) n -> g (r n)", r=2)).then_inc(s_prm, 16)
            sp.dma_start(nat[:, 1, :], ssm_a_im[0].rearrange("(g r) n -> g (r n)", r=2)).then_inc(s_prm, 16)
            sp.dma_start(ldt[:], ssm_log_dt[0].rearrange("(g r) -> g r", r=2)).then_inc(s_ldt, 16)
            for c, b_ in enumerate((ssm_b_re, ssm_b_im)):
                sp.dma_start(braw[:, c, :, :], b_[0].rearrange("(g r) n h -> (r n) g h", r=2)).then_inc(s_prm, 16)
            for c, c_ in enumerate((ssm_c_re, ssm_c_im)):
                for twice in range(2):
                    sp.dma_start(cnat[:, c, :, twice, :], c_[0].rearrange("(a g) h n -> (g h) a n", a=8))\
                      .then_inc(s_prm, 16)
            sp.dma_start(dnat[:], ssm_d[0].rearrange("(g q) -> g q", q=2 * H)).then_inc(s_prm, 16)
            sp.dma_start(cwn[:], conv_w[0].rearrange("w (a p) -> (w a) p", p=P)).then_inc(s_prm, 16)
            sp.wait_ge(s_const, 4)
            sp.dma_start(tok_d.rearrange("(p b) o -> p (b o)", p=P), zeros[:]).then_inc(s_zero, 16)

            for i in range(RAW, N_CONV):
                load(Q_CONV + i, i % RAW, 8, piece_rows(w_in2, 8 * (i % 2), 8, conv_col(i // 2), UC))
            for i in range(N_U):
                load(Q_U + i, i % RAW, 8, piece_rows(w_in2, 8 * (i % 2), 8, U_COL + i // 2 * UC, UC))
            for i in range(N_OA):
                load(Q_OA + i, i % RAW, 8, piece_rows(w_oa2, 0, 8, i * UC, UC))
            with sp.Fori(0, N_G // RAW) as r:
                for i in range(RAW):
                    load(Q_G + r * RAW + i, i, 8,
                         piece_rows(w_in2, 8 * (i % 2), 8, GA_COL + (r * 2 + i // 2) * UC, UC))
            for i in range(N_GLU):
                load(Q_GLU + i, i % RAW, 8, piece_rows(w_glu2, 0, 8, i % 2 * D + i // 2 * UC, UC))
            with sp.Fori(0, N_WO // RAW) as r:
                for i in range(RAW):
                    load(Q_WO + r * RAW + i, i, 4, piece_rows(w_o2, 4 * i, 4, r * 512, 512))

            def expert_piece(i, e):
                if i < 16:
                    w, k, c = (w_gate, w_up)[i // 8], 2 * (i % 8), 0
                else:
                    w, k, c = w_down, 2 * ((i - 16) % 4), (i - 16) // 4 * 1024
                rows = w[0].rearrange("e k n -> (e k) n")
                row = e * w.shape[2] + k * P
                if not isinstance(row, int):
                    row = sp.snap(row)
                return rows[bass.ds(row, 2 * P), c:c + 1024].rearrange("(k p) n -> p k n", p=P)

            def load_expert(i, e):
                s = i % RAWM
                sp.dma_start(expert_raw(s).rearrange("p (k n) -> p k n", k=2), expert_piece(i % PB, e))\
                  .then_inc(s_rawm[s], 16)

            for i in range(RAW):
                sp.wait_ge(s_lo, Q_MOE - RAW + i + 1)
                load_expert(i, 0)
            sp.wait_ge(s_x1t, 4 * TT)
            sp.wait_ge(s_x1o, 16 * TT)
            for i in range(RAW, 8):
                load_expert(i, 0)
            for i in range(RAWM, AHEAD):
                sp.wait_ge(s_lop, i - RAWM + 1)
                load_expert(i, 0)
            sp.wait_ge(s_tab, 1)
            sp.wait_ge(s_xg, 16)
            for i in range(8, RAWM):
                load_expert(i, 0)

            def load_pieces(b, pieces, e):
                for i in pieces:
                    sp.wait_ge(s_lo, lo_count(b, i - RAWM))
                    load_expert(i, e)

            def this_block(b, e):
                load_pieces(b, range(AHEAD, PB), e)

            def next_block(b, e):
                load_pieces(b, range(PB, PB + AHEAD), e)

            with sp.Fori(0, E - 1) as b:
                this_block(b, b)
                next_block(b, b + 1)
            blocks = sp.value_load(tab[0:1, NBLK + 1:NBLK + 2], min_val=E, max_val=NBLK)
            with sp.Fori(E - 1, NBLK) as b:
                with sp.If(b < blocks):
                    this_block(b, sp.value_load(tab[0:1, bass.ds(b, 1)], min_val=0, max_val=E - 1))
                    with sp.If(b < blocks - 1):
                        next_block(b, sp.value_load(tab[0:1, bass.ds(b + 1, 1)], min_val=0, max_val=E - 1))
            for i in range(TT + 2):
                sp.wait_ge(s_lo, lo_count(blocks, i - RAWM))
                if i < TT:
                    sp.dma_start(xr[:, i, :], x1_d[i * P:(i + 1) * P, :]).then_inc(s_xr[i], 16)
                else:
                    sp.dma_start((lng2, lnb2)[i - TT][:], (ln2_g, ln2_b)[i - TT][0].partition_broadcast(P))\
                      .then_inc(s_lnp[2], 16)
            for t in range(TT - 1):
                sp.wait_ge(s_rows[t], 3)
                sp.dma_start(out[0, t * P:(t + 1) * P, :], xr[:, t, :]).then_inc(s_out, 16)
            for half in range(2):
                sp.wait_ge(s_rows[TT - 1], 3 + half)
                sp.dma_start(out[0, T - P:T, halves[half]], xr[:, TT - 1, halves[half]]).then_inc(s_out, 16)
            sp.wait_ge(s_out, 16 * (TT + 1))

        @block.gpsimd
        def _(pool):
            lk = Link(pool, s_plink)
            lk.link(pool.memset(ident[:], 0.0))
            pool.affine_select(out=ident[:], in_=ident[:], compare_op=ALU.not_equal, fill=1.0, base=0,
                               pattern=[[-1, P]], channel_multiplier=1).then_inc(s_const, 1)
            pool.memset(zeros[:], 0).then_inc(s_const, 1)
            pool.memset(zrow[:], 0.0).then_inc(s_const, 1)
            pool.iota(tokid[:], pattern=[[P, TT]], base=0, channel_multiplier=1).then_inc(s_const, 1)

            def add_shift(buf, shift, t, n):
                pool.wait_ge(s_xm, n)
                pool.tensor_tensor(buf[:, t, :], buf[:, t, :], shift[:], ALU.add).then_inc(s_rows[t], 1)

            def scale_shift(buf, gain, shift, t, n):
                pool.wait_ge(s_xn, n)
                lk.link(pool.tensor_tensor(buf[:, t, :], buf[:, t, :], gain[:], ALU.mult))
                pool.tensor_tensor(buf[:, t, :], buf[:, t, :], shift[:], ALU.add).then_inc(s_rows[t], 1)

            pool.wait_ge(s_lnp[0], 32)
            for t in range(2):
                add_shift(xin, lnb, t, t + 1)
            pool.wait_ge(s_ldt, 16)
            pool.tensor_copy(nat[:, 2, :].rearrange("g (r n) -> g r n", r=2),
                             ldt[:].unsqueeze(2).to_broadcast([GG, 2, N])).then_inc(s_nat, 1)
            for t in range(TT):
                pool.wait_ge(s_rows[t], 1)
            pool.memset(cv[:, :, 0:2], 0.0).then_inc(s_cz, 1)
            pool.wait_ge(s_const, 4)
            for c in range(2):
                cols = slice(c * 1024, (c + 1) * 1024)
                pool.dma_start(yb_d[0:E * P, cols].rearrange("(b p) n -> p b n", p=P)[64:P],
                               zrow[64:P, :].unsqueeze(1).to_broadcast([64, E, 1024])).then_inc(s_ybz, 16)
                for b in range(E, NBLK):
                    pool.dma_start(yb_d[b * P:(b + 1) * P, cols], zrow[:]).then_inc(s_ybz, 16)

            for half in range(2):
                if half == 0:
                    for c in range(2):
                        pool.wait_ge(s_ust[c], 16 * 12)
                else:
                    pool.wait_ge(s_y, 1)
                for j in range(STEP):
                    pool.dma_start(U[j * H:(j + 1) * H, :, :],
                                   u_d[half * DS // 2:(half + 1) * DS // 2, j, :]
                                   .rearrange("(g h) n -> h g n", h=H)).then_inc(s_u, 16)
                pool.wait_ge(s_kp, half + 1)
                for r in range(2):
                    pool.dma_start(kp_d[half * HG:(half + 1) * HG, r, :, :].rearrange("g h x -> h g x"),
                                   kpd[r * H:(r + 1) * H, :, :, :].rearrange("h g d c -> h g (d c)"))\
                        .then_inc(s_kps, 16)
                pool.wait_ge(s_kps, 32 * (half + 1))
                for i in range(STEP):
                    pool.dma_start(M[i * H:(i + 1) * H, :, :, :].rearrange("h g r x -> h (g r) x"),
                                   kp_d[half * HG:(half + 1) * HG, :, :, (7 - i) * H:(7 - i) * H + P]
                                   .rearrange("g r h x -> h (g r) x")).then_inc(s_m, 16)
                pool.wait_ge(s_yg, 4 * (half + 1))
                for j in range(STEP):
                    pool.dma_start(y_d[half * DS // 2:(half + 1) * DS // 2, j, :]
                                   .rearrange("(g h) n -> h g n", h=H),
                                   yst[j * H:(j + 1) * H, :, :, :].rearrange("h g r n -> h (g r) n"))\
                        .then_inc(s_yo, 16)
            pool.wait_ge(s_yo, 16 * 16)
            pool.dma_start(yraw[:, :, :], y_d.rearrange("(k p) j n -> p k (j n)", p=P)).then_inc(s_yl, 16)

            lk.link(pool.memset(square[:], 1.0))
            lk.link(pool.tensor_copy(onesb[:], square[:]))
            lk.link(pool.affine_select(out=square[:], in_=square[:], compare_op=ALU.is_gt, fill=0.0, base=0,
                                       pattern=[[1, P]], channel_multiplier=-1))
            lk.link(pool.tensor_copy(tri[:], square[:]))
            pool.memset(ones[:], 1.0).then_inc(s_const2, 1)
            lk.link(pool.iota(RI[:, 0, :], pattern=[[1, E]], base=0, channel_multiplier=0))
            lk.link(pool.tensor_copy(eio[:, 0, :], RI[:, 0, :]))
            lk.link(pool.iota(RI[:, 1, :], pattern=[[0, EG], [-1, EP]], base=EP, channel_multiplier=0))
            lk.link(pool.tensor_copy(eio[:, 1, :], RI[:, 1, :]))
            lk.link(pool.iota(RI[:, 2, :], pattern=[[-P, E]], base=P * (E - 1), channel_multiplier=0))
            lk.link(pool.tensor_copy(eio[:, 2, :], RI[:, 2, :]))
            lk.link(pool.iota(RI[:, 3, 0:EG], pattern=[[-1, EG]], base=EG, channel_multiplier=0))
            lk.link(pool.tensor_copy(gio[:], RI[:, 3, 0:EG]))

            for c in range(2):
                pool.wait_ge(s_sgo[c], 16 * 16)
            with pool.Fori(0, 8) as j:
                pool.wait_ge(s_gm, j + 2)
                for n, (src, row) in enumerate(((ya_d, j * UC), (sg_d, j * UC), (sg_d, j * UC + D))):
                    pool.dma_start(gin[:, n, :, :], src[bass.ds(row, UC), :]
                                   .rearrange("(c p) t -> p c t", p=P)).then_inc(s_gin, 16)

            pool.wait_ge(s_used, Q_WO)
            pool.wait_ge(s_x0o, 16 * TT)
            pool.dma_start(x1[:], x0_d.rearrange("(t p) d -> p t d", p=P)).then_inc(s_res, 16)
            pool.dma_start(lng1[:], ln1_g[0].partition_broadcast(P)).then_inc(s_lnp[1], 16)
            pool.dma_start(lnb1[:], ln1_b[0].partition_broadcast(P)).then_inc(s_lnp[1], 16)
            pool.dma_start(wr[:], w_router.rearrange("(k p) e -> p k e", p=P)).then_inc(s_lnp[1], 16)
            pool.dma_start(brb[:], b_router.partition_broadcast(P)).then_inc(s_lnp[1], 16)
            pool.wait_ge(s_gm, 10)
            pool.wait_ge(s_ml, 8)
            lk.link(pool.iota(RI[:, 0, 0:NOVER + 1], pattern=[[1, NOVER + 1]], base=0, channel_multiplier=0))
            pool.tensor_copy(ovn[:], RI[:, 0, 0:NOVER + 1]).then_inc(s_const2, 1)

            pool.wait_ge(s_lnp[1], 64)
            for t in (1, 3):
                scale_shift(x1, lng1, lnb1, t, TT + t + 1)
            for i in range(RM):
                pool.wait_ge(s_hi, Q_MOE + i + 1)
                pool.tensor_tensor(mlo[:, i, :], expert_raw(i), mhi[:, i, :].bitcast(F32), ALU.subtract)\
                    .then_inc(s_lop, 1)

            pool.wait_ge(s_zero, 16)
            pool.wait_ge(s_dst, 1)
            for t in range(TT):
                for k in range(2):
                    pool.indirect_dma_start(
                        out=tok_d[:, :], out_offset=bass.IndirectOffsetOnAxis(ap=dest[:, t, k:k + 1], axis=0),
                        in_=tokid[:, t:t + 1], in_offset=None).then_inc(s_sct, 16)
            pool.wait_ge(s_sct, 16 * 2 * TT)
            pool.wait_ge(s_x1o, 16 * TT)

            def gather_rows(n):
                pool.indirect_dma_start(
                    out=xg[0:n, :], out_offset=None, in_=x1_d[:, :],
                    in_offset=bass.IndirectOffsetOnAxis(ap=bidx[0:n, :], axis=0)).then_inc(s_xg, 16)

            def gather(b):
                if b:
                    pool.wait_ge(s_xt, 2 * b)
                pool.dma_start(bidx[:], tok_d[b * P:(b + 1) * P, :]).then_inc(s_bix, 16)
                pool.wait_ge(s_bix, b * 16 + 16)
                if 0 < b < E:
                    count = pool.value_load(tab[0:1, COUNTS + b:COUNTS + b + 1], min_val=0, max_val=T)
                    with pool.If(count <= 64):
                        gather_rows(64)
                    with pool.If(count > 64):
                        with pool.If(count <= 96):
                            gather_rows(96)
                        with pool.If(count > 96):
                            gather_rows(P)
                else:
                    gather_rows(P)

            gather(0)
            pool.wait_ge(s_tab, 1)
            for b in range(E):
                gather(b + 1)
            blocks = pool.value_load(tab[0:1, NBLK + 1:NBLK + 2], min_val=E, max_val=NBLK)
            for b in range(E, NBLK):
                with pool.If(blocks > b):
                    gather(b + 1)

            pool.wait_ge(s_used, blocks * PB + Q_MOE)
            pool.wait_ge(s_x1o, blocks * 32 + 16 * TT)
            lk.link(pool.tensor_tensor(back[:].rearrange("p t k -> p (t k)"), dest[:].rearrange("p t k -> p (t k)"),
                                       zeros[:, 0:2 * TT], ALU.add))
            pool.wait_ge(s_ybz, 16 * N_ZERO)
            for t in range(TT):
                for k in range(2):
                    pool.indirect_dma_start(
                        out=yg[:, t, k, :], out_offset=None, in_=yb_d[:, :],
                        in_offset=bass.IndirectOffsetOnAxis(ap=back[:, t, k:k + 1], axis=0)).then_inc(s_yr[t], 16)
            pool.wait_ge(s_lnp[2], 32)
            for t in range(3):
                scale_shift(xr, lng2, lnb2, t, 2 * TT + t + 1)

        @block.scalar
        def _(act):
            act.dma_start(lng[:], in_g.partition_broadcast(P)).then_inc(s_lnp[0], 16)
            act.dma_start(lnb[:], in_b.partition_broadcast(P)).then_inc(s_lnp[0], 16)
            def root(n, t):
                act.wait_ge(s_var, n + 1)
                act.activation(tmp4[:, t:t + 1], rstd[:, t:t + 1], ACT.Sqrt).then_inc(s_sq, 1)

            def normalise(buf, t, n, cols=slice(0, D)):
                act.wait_ge(s_rs, n)
                act.activation(buf[:, t, cols], buf[:, t, cols], ACT.Identity, bias=nmr[:, t:t + 1],
                               scale=rstd[:, t:t + 1]).then_inc(s_xn, 1)

            def rows_hi(t):
                for b in range(4):
                    act.wait_ge(s_tr, 4 * t + b + 1)
                    act.activation(xT_hi[:, 4 * b:4 * b + 4, t * P:(t + 1) * P],
                                   sets[t % 2][:, b, :].rearrange("p (k n) -> p k n", k=4), ACT.Copy)\
                       .then_inc(s_trh, 1)
                act.dma_start(x0_d[t * P:(t + 1) * P, :], xin[:, t, :]).then_inc(s_x0o, 16)

            def hi(q, s):
                act.wait_ge(s_raw[s], raw_count(q, s))
                if not isinstance(q, int) or q >= RD:
                    act.wait_ge(s_used, q - RD + 1)
                act.activation(whi[:, s % RD, :], raw[:, s, :], ACT.Copy).then_inc(s_hi, 1)

            def hi_expert(b, i):
                act.wait_ge(s_rawm[i % RAWM], b * (16 * PB // RAWM) + 16 * (i // RAWM + 1))
                act.wait_ge(s_used, b * PB + (Q_MOE + i - RM + 1))
                act.activation(mhi[:, i % RM, :], expert_raw(i % RAWM), ACT.Copy).then_inc(s_hi, 1)

            def raw_count(q, s):
                return (q - s) * (16 // RAW) + 16

            act.wait_ge(s_const, 4)
            act.activation(ahead[:, 2:3], ident[:, 0:1], ACT.Copy).then_inc(s_yb, 1)

            for t in range(TT):
                root(t, t)
                normalise(xin, t, t + 1)
            rows_hi(0)
            rows_hi(1)
            for q in range(2):
                hi(q, q)
            rows_hi(2)
            rows_hi(3)

            copies = [0]

            def leave(rows, view_out, view_in, func, buf, earlier, stored):
                if earlier:
                    act.wait_ge(stored, 16 * earlier)
                copies[0] += 1
                act.activation(view_out, view_in, func).then_inc(s_cp, 1)
                act.wait_ge(s_cp, copies[0])
                act.dma_start(rows, buf).then_inc(stored, 16)

            def after(m):
                if m < 0 or (m % 2 == 0 and not Q_OA <= m < Q_G):
                    return
                n = unit_of(m)
                if m < Q_U:
                    i, part = divmod(n, 3)
                    if part == 0:
                        act.wait_ge(s_used, m + 1)
                        act.wait_ge(s_cm, i)
                        act.activation(cx[:], dn[:, 2 * (n % 2):2 * (n % 2) + 2, :], ACT.Copy).then_inc(s_cx, 1)
                    if part == 2:
                        if i == 0:
                            act.wait_ge(s_x0o, 16 * TT)
                        act.wait_ge(s_pa, i + 1)
                        act.activation(pa_hi[:, 2 * i:2 * i + 2, :], ct[:], ACT.Copy).then_inc(s_pah, 1)
                elif m < Q_OA:
                    i = n - 12
                    act.wait_ge(s_used, m + 1)
                    for c in range(2):
                        leave(u_d[(2 * i + c) * P:(2 * i + c + 1) * P].rearrange("p j n -> p (j n)"),
                              ust[:, c, :].rearrange("p (j n) -> p j n", j=STEP),
                              dn[:, 2 * (n % 2) + c, :].rearrange("p (n j) -> p j n", j=STEP),
                              ACT.Copy, ust[:, c, :], i, s_ust[c])
                elif m < Q_G:
                    j = m - Q_OA
                    act.wait_ge(s_used, m + 1)
                    for c in range(2):
                        leave(ya_d[(2 * j + c) * P:(2 * j + c + 1) * P, :], ust[:, c, :],
                              dn[:, 2 * (n % 2) + c, :], ACT.Copy, ust[:, c, :], 4 + j, s_ust[c])
                else:
                    j = n - 24
                    act.wait_ge(s_used, m + 1)
                    for c in range(2):
                        leave(sg_d[(2 * j + c) * P:(2 * j + c + 1) * P, :], sgst[:, c, :],
                              dn[:, 2 * (n % 2) + c, :], ACT.Sigmoid, sgst[:, c, :], j, s_sgo[c])

            def c_ready():
                act.wait_ge(s_ctr, 1)
                for c in range(2):
                    for a in range(2):
                        for r in range(2):
                            rows = slice(r * N, (r + 1) * N)
                            last = act.activation(
                                Cc[rows, c, a * HG:(a + 1) * HG, :],
                                ex[rows, 2 * c + a, :].rearrange("p (g r h) -> p r g h", r=2, h=H)[:, r, :, :],
                                ACT.Copy)
                            last.then_inc(s_cc, 1)

            def v_ready(half, c):
                act.wait_ge(s_vtr, 2 * half + c + 1)
                if half == 0 and c == 0:
                    for tile in range(2):
                        act.wait_ge(s_ust[tile], 16 * 12)
                for b in range(4):
                    act.activation(V[:, c, 4 * b:4 * b + 4, :], ex[:, b, :], ACT.Copy).then_inc(s_v, 1)

            def chunk_inputs(half):
                act.wait_ge(s_bu, half + 1)
                for c in range(2):
                    for b in range(2):
                        act.activation(S[:, c, 8 * b:8 * b + 8, :], ex[:, 2 * c + b, :], ACT.Copy).then_inc(s_s, 1)

            def gelu_y(half):
                act.wait_ge(s_y, half + 1)
                for b in range(2):
                    for r in range(2):
                        act.activation(yst[:, 8 * b:8 * b + 8, r, :],
                                       ex[:, 2 * b + r, :].rearrange("p (g n) -> p g n", g=8),
                                       ACT.Gelu_apprx_tanh).then_inc(s_yg, 1)

            for q in range(Q_GLU):
                if q >= 2:
                    hi(q, q % RAW)
                after(q - 2)
                if q == 5:
                    c_ready()
                    act.wait_ge(s_ang, 1)
                    act.activation(prm[:, 10, :], prm[:, 8, :], ACT.Sin).then_inc(s_sin, 1)
                    act.activation(prm[:, 11, :], prm[:, 8, :], ACT.Sin, scale=0.5).then_inc(s_sin, 1)
                if q >= Q_G:
                    half, rel = divmod(q - Q_G, 16)
                    if rel == 6:
                        v_ready(half, 0)
                    if rel == 7:
                        v_ready(half, 1)
                    if rel == 8:
                        chunk_inputs(half)
                    if rel == 13:
                        gelu_y(half)
            hi(Q_GLU, 0)
            act.wait_ge(s_yl, 16)
            for k in range(8):
                act.activation(ys_hi[:, k, :].rearrange("p (n j) -> p j n", j=STEP),
                               yraw[:, k, :].rearrange("p (j n) -> p j n", j=STEP), ACT.Copy).then_inc(s_ysh, 1)
            hi(Q_GLU + 1, 1)
            after(Q_GLU - 1)

            for c in range(2):
                act.wait_ge(s_sgo[c], 16 * 16)
            with act.Fori(0, 4) as r:
                for i in range(2):
                    q = Q_GLU + 4 * r + 2 * i + 2
                    hi(q, (2 * i + 2) % RAW)
                    hi(q + 1, (2 * i + 3) % RAW)
                    j = r * 2 + i
                    act.wait_ge(s_used, j * 2 + (Q_GLU + 2))
                    act.wait_ge(s_gm, j + 2)
                    act.activation(sgt[:], (dn, ex)[i][:, 2:4, :], ACT.Sigmoid).then_inc(s_sgt, 1)
                    act.wait_ge(s_gm, j + 3)
                    act.activation(mx_hi[:, bass.ds(2 * j, 2), :], gm[:], ACT.Copy).then_inc(s_mh, 1)
            with act.Fori(0, 3) as r:
                for i in range(4):
                    hi(Q_WO + 4 * r + i + 2, (i + 2) % RAW)
            hi(Q_WO + 14, 2)
            hi(Q_WO + 15, 3)

            def logits_out(t):
                act.wait_ge(s_log, t + 1)
                act.activation(lgT[:, t, :], sets1[t % 2][0:E, 0, 0:P], ACT.Copy).then_inc(s_lgt, 1)

            def x1_out(t):
                act.wait_ge(s_rows[t], 2)
                act.dma_start(x1_d[t * P:(t + 1) * P, :], x1[:, t, :]).then_inc(s_x1o, 16)
                for n, b in enumerate((1, 2, 3, 0)):
                    act.wait_ge(s_x1t, 4 * t + n + 1)
                    if t >= 2 and n == 0:
                        act.wait_ge(s_log, t - 1)
                    act.activation(x1T[:, t % 2, 4 * b:4 * b + 4, :],
                                   sets1[t % 2][:, b, :].rearrange("p (k n) -> p k n", k=4), ACT.Copy)\
                       .then_inc(s_x1c, 1)
                    if t >= 2 and n == 0:
                        logits_out(t - 2)

            def ln1(t):
                root(TT + t, t)
                normalise(x1, t, TT + t + 1)

            ln1(0)
            ln1(1)
            x1_out(0)
            ln1(2)
            ln1(3)
            x1_out(1)
            x1_out(2)
            x1_out(3)
            logits_out(TT - 2)
            logits_out(TT - 1)
            for i in range(RM):
                hi_expert(0, i)

            def block_rows_hi(n, half, banks=dn):
                act.wait_ge(s_xt, n * 2 + half + 1)
                for c in range(2):
                    k = 8 * half + 4 * c
                    act.activation(xg_hi[:, k:k + 4, :], banks[:, c, :].rearrange("p (k n) -> p k n", k=4),
                                   ACT.Copy).then_inc(s_xh, 1)

            def store(b, half, n, cols):
                act.wait_ge(s_yb, b * 2 + 2 + half)
                act.dma_start(yb_d[bass.ds(b * P, n), cols], ybl[0:n, cols]).then_inc(s_x1o, 16)

            def block_half_out(b, half):
                cols = slice(1024 * half, 1024 * (half + 1))
                act.activation(ybl[:, cols].rearrange("p (c n) -> p c n", c=2), ex[:, 2 * half:2 * half + 2, :],
                               ACT.Copy).then_inc(s_yb, 1)
                count = act.value_load(tab[0:1, bass.ds(b + COUNTS, 1)], min_val=0, max_val=T)
                with act.If(count <= 64):
                    store(b, half, 64, cols)
                with act.If(count > 64):
                    with act.If(count <= 96):
                        store(b, half, 96, cols)
                    with act.If(count > 96):
                        store(b, half, P, cols)

            def this_block(b):
                for i in range(RM, PB):
                    hi_expert(b, i)
                    if i == 11:
                        act.wait_ge(s_used, b * PB + (Q_MOE + 8))
                        for c in range(2):
                            act.activation(hid[:, c * 512:(c + 1) * 512], dn[:, c, :], ACT.Silu)\
                               .then_inc(s_sil, 1)
                    if i == 19:
                        for c in range(2):
                            act.wait_ge(s_ht, b * 2 + c + 1)
                            act.activation(h_hi[:, 4 * c:4 * c + 4, :],
                                           dn[:, 2 + c, :].rearrange("p (k n) -> p k n", k=4), ACT.Copy)\
                               .then_inc(s_hh, 1)
                        block_rows_hi(b + 1, 0)
                    if i == 22:
                        block_rows_hi(b + 1, 1)
                act.wait_ge(s_used, b * PB + (Q_MOE + 20))
                act.wait_ge(s_x1o, b * 32 + 16 * TT)
                block_half_out(b, 0)

            def next_block(b):
                for i in range(PB, PB + RM):
                    hi_expert(b, i)

            def block_out(b):
                act.wait_ge(s_used, b * PB + (Q_MOE + 24))
                block_half_out(b, 1)

            block_rows_hi(0, 0)
            block_rows_hi(0, 1, ex)
            act.wait_ge(s_ybz, 16 * N_ZERO)
            act.wait_ge(s_tab, 1)
            with act.Fori(0, E - 1) as b:
                this_block(b)
                next_block(b)
                block_out(b)
            blocks = act.value_load(tab[0:1, NBLK + 1:NBLK + 2], min_val=E, max_val=NBLK)
            with act.Fori(E - 1, NBLK) as b:
                with act.If(b < blocks):
                    this_block(b)
                    with act.If(b < blocks - 1):
                        next_block(b)
                    block_out(b)

            for t in range(TT):
                act.wait_ge(s_xr[t], 16)
                act.activation(xr[:, t, :], xr[:, t, :], ACT.Copy, scale=ALPHA).then_inc(s_xa, 1)
            for t in range(TT):
                root(2 * TT + t, t)
                for cols in (slice(0, D),) if t < TT - 1 else halves:
                    normalise(xr, t, 2 * TT + t + 1, cols)

        @block.vector
        def _(dve):
            lk = Link(dve, s_link)
            link = lk.link
            tt, ts, stt = dve.tensor_tensor, dve.tensor_scalar, dve.scalar_tensor_tensor

            def lo(q, s):
                dve.wait_ge(s_hi, q + 1)
                tt(wlo[:, s % RD, :], raw[:, s, :], whi[:, s % RD, :].bitcast(F32), ALU.subtract).then_inc(s_lo, 1)

            def lo_expert(b, i):
                dve.wait_ge(s_hi, b * PB + (Q_MOE + i + 1))
                tt(mlo[:, i % RM, :], expert_raw(i % RAWM), mhi[:, i % RM, :].bitcast(F32), ALU.subtract)\
                    .then_inc(s_lo, 1)

            def stats(buf, t):
                for c in range(4):
                    lk.go(dve.bn_stats(bst[:, t, c, :], buf[:, t, c * 512:(c + 1) * 512]))
                lk.wait()
                link(dve.bn_aggr(mv[:, t, :], bst[:, t, :, :]))

            def row_scale(sl, n):
                ts(rstd[:, sl], mv[:, sl, 1], EPS, None, ALU.add).then_inc(s_var, 1)
                dve.wait_ge(s_sq, n)
                link(dve.reciprocal(nmr[:, sl], tmp4[:, sl]))
                link(tt(tmp4[:, sl], rstd[:, sl], nmr[:, sl], ALU.mult))
                link(tt(tmp4[:, sl], tmp4[:, sl], nmr[:, sl], ALU.mult))
                link(ts(tmp4[:, sl], tmp4[:, sl], -0.5, 1.5, ALU.mult, ALU.add))
                link(tt(rstd[:, sl], nmr[:, sl], tmp4[:, sl], ALU.mult))
                stt(nmr[:, sl], mv[:, sl, 0], -1.0, rstd[:, sl], ALU.mult, ALU.mult).then_inc(s_rs, 1)

            def scale_rows(buf, gain, t, n, cols=slice(0, D)):
                dve.wait_ge(s_xn, n)
                tt(buf[:, t, cols], buf[:, t, cols], gain[:, cols], ALU.mult).then_inc(s_xm, 1)

            def shift_rows(buf, shift, t, n, cols=slice(0, D)):
                dve.wait_ge(s_xm, n)
                tt(buf[:, t, cols], buf[:, t, cols], shift[:, cols], ALU.add).then_inc(s_rows[t], 1)

            def rows_lo(t):
                for b in range(4):
                    dve.wait_ge(s_trh, 4 * t + b + 1)
                    tt(xT_lo[:, 4 * b:4 * b + 4, t * P:(t + 1) * P],
                       sets[t % 2][:, b, :].rearrange("p (k n) -> p k n", k=4),
                       xT_hi[:, 4 * b:4 * b + 4, t * P:(t + 1) * P].bitcast(F32), ALU.subtract)\
                        .then_inc(s_trl, 1)

            dve.memset(ahead[:, 0:1], 0.0).then_inc(s_gm, 1)
            dve.memset(ahead[:, 3:4], 0.0).then_inc(s_gm, 1)

            for t in range(TT):
                dve.wait_ge(s_x[t], 16)
                stats(xin, t)
                row_scale(slice(t, t + 1), t + 1)
                if t == 1:
                    dve.wait_ge(s_lnp[0], 32)
                if t >= 1:
                    scale_rows(xin, lng, t - 1, t)
            shift_rows(xin, lnb, 2, 3)
            rows_lo(0)
            rows_lo(1)
            scale_rows(xin, lng, 3, 4)
            shift_rows(xin, lnb, 3, 4)
            rows_lo(2)
            lo(0, 0)
            rows_lo(3)

            def exp_of(dst, src, xc, k, r, p):
                link(ts(xc, src, -87.0, 88.0, ALU.max, ALU.min))
                link(ts(k, xc, 1.0 / math.log(2.0), MAGIC, ALU.mult, ALU.add))
                link(ts(k, k, MAGIC, None, ALU.subtract))
                link(stt(r, k, -0.693359375, xc, ALU.mult, ALU.add))
                link(stt(r, k, 0.693359375 - math.log(2.0), r, ALU.mult, ALU.add))
                link(ts(p, r, 1.0 / math.factorial(8), None, ALU.mult))
                for d in range(7, 0, -1):
                    link(stt(p, p, 1.0 / math.factorial(d), r, ALU.add, ALU.mult))
                link(ts(p, p, 1.0, None, ALU.add))
                link(ts(xc.bitcast(I32), k, 127.0, 2.0 ** 23, ALU.add, ALU.mult))
                link(tt(p, p, xc.bitcast(F32), ALU.mult))
                link(stt(dst, src, -87.0, p, ALU.is_ge, ALU.mult))

            def v_(i):
                return prm[:, i, :]

            def cmul(o_re, o_im, a, b, x_, y_):
                link(tt(x_, a[0], b[0], ALU.mult))
                link(tt(y_, a[1], b[1], ALU.mult))
                link(tt(x_, x_, y_, ALU.subtract))
                link(tt(y_, a[0], b[1], ALU.mult))
                link(tt(o_im, a[1], b[0], ALU.mult))
                link(tt(o_im, o_im, y_, ALU.add))
                link(dve.tensor_copy(o_re, x_))

            def parameters_1():
                dve.wait_ge(s_ptr, 1)
                dve.tensor_copy(prm[:, 0:3, :], ex[:, 0, 0:3 * GG].rearrange("p (i g) -> p i g", i=3))\
                    .then_inc(s_pcp, 1)
                dve.tensor_copy(dgv[:], ex[0:2 * H, 0, 3 * GG:4 * GG]).then_inc(s_pcp, 1)
                dve.tensor_copy(cw[:], ex[:, 0, 4 * GG:4 * GG + 24].rearrange("p (w a) -> p a w", w=3)).then_inc(s_pcp, 1)
                dve.wait_ge(s_pcp, 3)
                exp_of(v_(3), v_(2), v_(21), v_(22), v_(23), v_(24))
                link(ts(v_(4), v_(0), -1e-4, None, ALU.min))
                link(tt(v_(19), v_(4), v_(3), ALU.mult))
                exp_of(v_(5), v_(19), v_(21), v_(22), v_(23), v_(24))
                link(tt(v_(6), v_(1), v_(3), ALU.mult))
                c1, c2, c3 = two_pi_parts()
                link(ts(v_(7), v_(6), 1.0 / (2 * math.pi), MAGIC, ALU.mult, ALU.add))
                link(ts(v_(7), v_(7), MAGIC, None, ALU.subtract))
                link(stt(v_(8), v_(7), -c1, v_(6), ALU.mult, ALU.add))
                link(stt(v_(8), v_(7), -c2, v_(8), ALU.mult, ALU.add))
                link(stt(v_(8), v_(7), -c3, v_(8), ALU.mult, ALU.add))
                ts(v_(8), v_(8), -3.1415925, 3.1415925, ALU.max, ALU.min).then_inc(s_ang, 1)

            def parameters_2():
                dve.wait_ge(s_sin, 2)
                link(tt(v_(12), v_(11), v_(11), ALU.mult))
                link(ts(v_(12), v_(12), -2.0, 1.0, ALU.mult, ALU.add))
                link(tt(A1[:, 0, :], v_(5), v_(12), ALU.mult))
                link(tt(A1[:, 2, :], v_(5), v_(10), ALU.mult))
                link(ts(A1[:, 1, :], A1[:, 2, :], -1.0, None, ALU.mult))
                link(tt(v_(15), v_(4), v_(4), ALU.mult))
                link(tt(v_(19), v_(1), v_(1), ALU.mult))
                link(tt(v_(15), v_(15), v_(19), ALU.add))
                link(dve.reciprocal(v_(15), v_(15)))
                link(ts(v_(16), A1[:, 0, :], -1.0, None, ALU.add))
                link(tt(v_(17), v_(16), v_(4), ALU.mult))
                link(tt(v_(19), A1[:, 2, :], v_(1), ALU.mult))
                link(tt(v_(17), v_(17), v_(19), ALU.add))
                link(tt(v_(17), v_(17), v_(15), ALU.mult))
                link(tt(v_(18), A1[:, 2, :], v_(4), ALU.mult))
                link(tt(v_(19), v_(16), v_(1), ALU.mult))
                link(tt(v_(18), v_(18), v_(19), ALU.subtract))
                link(tt(v_(18), v_(18), v_(15), ALU.mult))
                a = (A1[:, 0, :], A1[:, 2, :])
                cmul(v_(25), v_(26), a, a, v_(19), v_(20))
                b = (v_(25), v_(26))
                cmul(v_(27), v_(28), b, b, v_(19), v_(20))
                b = (v_(27), v_(28))
                cmul(P8[:, 0, 0, :], P8[:, 0, 2, :], b, b, v_(19), v_(20))

            def parameters_3():
                a8 = (P8[:, 0, 0, :], P8[:, 0, 2, :])
                for i in range(1, STEP):
                    cmul(P8[:, i, 0, :], P8[:, i, 2, :], (P8[:, i - 1, 0, :], P8[:, i - 1, 2, :]), a8,
                         v_(19), v_(20))
                link(ts(P8[:, :, 1, :], P8[:, :, 2, :], -1.0, None, ALU.mult))
                co_re = v_(17).unsqueeze(2).to_broadcast([P, GG, H])
                co_im = v_(18).unsqueeze(2).to_broadcast([P, GG, H])
                link(tt(Bb[:, 0, :, :], braw[:, 0, :, :], co_re, ALU.mult))
                link(tt(Bb[:, 1, :, :], braw[:, 1, :, :], co_im, ALU.mult))
                link(tt(Bb[:, 0, :, :], Bb[:, 0, :, :], Bb[:, 1, :, :], ALU.subtract))
                link(tt(braw[:, 0, :, :], braw[:, 0, :, :], co_im, ALU.mult))
                link(tt(Bb[:, 1, :, :], braw[:, 1, :, :], co_re, ALU.mult))
                link(tt(Bb[:, 1, :, :], Bb[:, 1, :, :], braw[:, 0, :, :], ALU.add))
                link(tt(dmask[:], ident[0:2 * H, 0:H], ident[0:2 * H, H:2 * H], ALU.add))
                link(tt(dsk[:], dgv[:].unsqueeze(2).to_broadcast([2 * H, GG, H]),
                        dmask[:].unsqueeze(1).to_broadcast([2 * H, GG, H]), ALU.mult))

            def times_a(dst, src, half, op, done=None):
                g = slice(half * HG, (half + 1) * HG)
                ar = A1[:, 0, g].unsqueeze(1).to_broadcast([P, 2, HG]).unsqueeze(3).to_broadcast([P, 2, HG, H])
                ai = A1[:, 1:3, g].unsqueeze(3).to_broadcast([P, 2, HG, H])
                lk.go(tt(t1[:], src, ar, ALU.mult))
                lk.go(tt(t2[:], src[:, ::-1], ai, ALU.mult))
                lk.wait()
                if done is None:
                    link(tt(dst, t1[:], t2[:], op))
                else:
                    tt(dst, t1[:], t2[:], op).then_inc(done, 1)

            def vt_steps(half, steps):
                for i in steps:
                    if i == STEP - 1:
                        g = slice(half * HG, (half + 1) * HG)
                        link(dve.tensor_copy(VT[:, :, :, i, :], Bb[:, :, g, :]))
                    else:
                        times_a(VT[:, :, :, i, :], VT[:, :, :, i + 1, :], half, ALU.add)

            def w_steps(half, steps, done=None):
                for d in steps:
                    if d == 0:
                        g = slice(half * HG, (half + 1) * HG)
                        lk.go(dve.tensor_copy(W[:, 0, :, 0, :], Cc[:, 0, g, :]))
                        lk.go(ts(W[:, 1, :, 0, :], Cc[:, 1, g, :], -1.0, None, ALU.mult))
                        lk.wait()
                    else:
                        times_a(W[:, :, :, d, :], W[:, :, :, d - 1, :], half, ALU.subtract, done)

            def block_diagonal(half):
                g = slice(half * HG, (half + 1) * HG)
                link(dve.memset(Bbd[:], 0.0))
                lk.go(dve.tensor_copy(Bbd[0:N, :, :, 0, :], Bb[0:N, :, g, :]))
                dve.tensor_copy(Bbd[N:P, :, :, 1, :], Bb[N:P, :, g, :]).then_inc(s_vt, 1)
                lk.wait()

            Sb = S[:].rearrange("p c g (b i) -> p c g b i", i=STEP)
            u1 = t1[:].rearrange("p c g h -> p (c g h)")
            u2 = t2[:].rearrange("p c g h -> p (c g h)")

            def advance(half, power, dst, src, nb, done=None):
                g = slice(half * HG, (half + 1) * HG)
                shape = [P, 2, HG, nb]
                ar = P8[:, power - 1, 0, g].unsqueeze(1).to_broadcast([P, 2, HG]).unsqueeze(3).to_broadcast(shape)
                ai = P8[:, power - 1, 1:3, g].unsqueeze(3).to_broadcast(shape)
                x_ = u1[:, 0:2 * HG * nb].rearrange("p (c g b) -> p c g b", c=2, g=HG)
                y_ = u2[:, 0:2 * HG * nb].rearrange("p (c g b) -> p c g b", c=2, g=HG)
                lk.go(tt(x_, src, ar, ALU.mult))
                lk.go(tt(y_, src[:, ::-1], ai, ALU.mult))
                lk.wait()
                link(tt(dst, dst, x_, ALU.add))
                if done is None:
                    link(tt(dst, dst, y_, ALU.add))
                else:
                    tt(dst, dst, y_, ALU.add).then_inc(done, 1)

            def scan_inside(half, steps):
                for i in steps:
                    advance(half, 1, Sb[:, :, :, :, i], Sb[:, :, :, :, i - 1], STEP)

            def scan_over(half):
                for b in range(1, STEP):
                    advance(half, STEP, Sb[:, :, :, b:b + 1, STEP - 1], Sb[:, :, :, b - 1:b, STEP - 1], 1)

            def scan_back(half, places, done=None):
                for i in places:
                    advance(half, i + 1, Sb[:, :, :, 1:STEP, i], Sb[:, :, :, 0:STEP - 1, STEP - 1], STEP - 1, done)

            def pad_k(half):
                dve.wait_ge(s_k, half + 1)
                lk.go(dve.memset(kpd[:, :, 0:7, :], 0.0))
                for b in range(4):
                    lk.go(dve.tensor_copy(kpd[:, 4 * b:4 * b + 4, 7:15, :],
                                          ex[0:2 * H, b, :].rearrange("p (g d h) -> p g d h", g=4, h=H)))
                lk.wait()
                tt(kpd[:, :, 7, :], kpd[:, :, 7, :], dsk[:, half * HG:(half + 1) * HG, :], ALU.add)\
                    .then_inc(s_kp, 1)

            def conv_after(m):
                n = unit_of(m)
                i, part = divmod(n, 3)
                b2 = dn[:, 2 * (n % 2):2 * (n % 2) + 2, :]
                if part == 1:
                    dve.wait_ge(s_cx, i + 1)
                    dve.wait_ge(s_used, m + 1)
                    tt(cv[:, :, 2:], b2, cx[:], ALU.mult).then_inc(s_cm, 1)
                    dve.wait_ge(s_cm, i + 1)
                    for k in range(CONV_WIDTH):
                        for c in range(2):
                            w_ = cw[:, 2 * i + c, k:k + 1]
                            v = cv[:, c, k:k + T]
                            lk.go(ts(ct[:, c, :], v, w_, None, ALU.mult) if k == 0 else
                                  stt(ct[:, c, :], v, w_, ct[:, c, :], ALU.mult, ALU.add))
                        lk.wait()
                if part == 2:
                    dve.wait_ge(s_used, m + 1)
                    tt(ct[:], ct[:], b2, ALU.mult).then_inc(s_pa, 1)
                    dve.wait_ge(s_pah, i + 1)
                    tt(pa_lo[:, 2 * i:2 * i + 2, :], ct[:], pa_hi[:, 2 * i:2 * i + 2, :].bitcast(F32),
                       ALU.subtract).then_inc(s_pal, 1)
                    dve.wait_ge(s_pal, i + 1)

            for q in range(Q_GLU):
                if q >= 1:
                    lo(q, q % RAW)
                m = q - 2
                if 0 <= m < Q_U and m % 2 == 1:
                    if m == 3:
                        dve.wait_ge(s_cz, 1)
                        dve.wait_ge(s_prm, 16 * N_PRM)
                    conv_after(m)
                if q == 3:
                    parameters_1()
                if q == 6:
                    parameters_2()
                if q == 8:
                    dve.wait_ge(s_ybz, 16 * N_ZERO)
                    parameters_3()
                if q >= Q_G:
                    half, rel = divmod(q - Q_G, 16)
                    if rel == 1:
                        if half == 1:
                            dve.wait_ge(s_y, 1)
                            dve.wait_ge(s_yo, 16 * 8)
                        else:
                            dve.wait_ge(s_used, Q_G)
                        vt_steps(half, (7, 6, 5))
                    if rel == 2:
                        vt_steps(half, (4, 3, 2))
                    if rel == 3:
                        vt_steps(half, (1, 0))
                        block_diagonal(half)
                    if rel == 7:
                        dve.wait_ge(s_vtr, 2 * half + 2)
                        w_steps(half, (0, 1, 2, 3))
                    if rel == 8:
                        w_steps(half, (4, 5, 6))
                    if rel == 9:
                        w_steps(half, (7,))
                        w_steps(half, (8,), s_w)
                        dve.wait_ge(s_w, half + 1)
                        dve.wait_ge(s_s, 4 * (half + 1))
                        scan_inside(half, (1, 2, 3, 4))
                    if rel == 10:
                        scan_inside(half, (5, 6, 7))
                        scan_over(half)
                    if rel == 11:
                        pad_k(half)
                        scan_back(half, (0, 1, 2))
                    if rel == 12:
                        scan_back(half, (3, 4, 5))
                        scan_back(half, (6,), s_st)
                        dve.wait_ge(s_st, half + 1)
            lo(Q_GLU, 0)
            for k in range(8):
                dve.wait_ge(s_ysh, k + 1)
                tt(ys_lo[:, k, :].rearrange("p (n j) -> p j n", j=STEP),
                   yraw[:, k, :].rearrange("p (j n) -> p j n", j=STEP),
                   ys_hi[:, k, :].rearrange("p (n j) -> p j n", j=STEP).bitcast(F32), ALU.subtract)\
                    .then_inc(s_ysl, 1)
            lo(Q_GLU + 1, 1)

            base_n = lk.n
            with dve.Fori(0, 4) as r:
                for i in range(2):
                    q = Q_GLU + 4 * r + 2 * i + 2
                    lo(q, (2 * i + 2) % RAW)
                    lo(q + 1, (2 * i + 3) % RAW)
                    j = r * 2 + i
                    n = base_n + j * 3
                    dve.wait_ge(s_gin, j * 48 + 48)
                    dve.wait_ge(s_sgt, j + 1)
                    tt(gm[:], (dn, ex)[i][:, 0:2, :], sgt[:], ALU.mult).then_inc(s_link, 1)
                    tt(gin[:, 0, :, :], gin[:, 0, :, :], gin[:, 1, :, :], ALU.mult).then_inc(s_link, 1)
                    dve.wait_ge(s_link, n + 1)
                    tt(gm[:], gm[:], gin[:, 2, :, :], ALU.mult).then_inc(s_link, 1)
                    dve.wait_ge(s_link, n + 3)
                    tt(gm[:], gm[:], gin[:, 0, :, :], ALU.add).then_inc(s_gm, 1)
                    dve.wait_ge(s_mh, j + 1)
                    tt(mx_lo[:, bass.ds(2 * j, 2), :], gm[:], mx_hi[:, bass.ds(2 * j, 2), :].bitcast(F32),
                       ALU.subtract).then_inc(s_ml, 1)
                    dve.wait_ge(s_ml, j + 1)
            lk.n = base_n + 24

            def residual(c, banks):
                for t in range(TT):
                    stt(x1[:, t, bass.ds(c * 512, 512)], x1[:, t, bass.ds(c * 512, 512)], ALPHA,
                        banks[:, t, :], ALU.mult, ALU.add).then_inc(s_wof, 1)
                dve.wait_ge(s_wof, c * 4 + 4)
                for t in range(TT):
                    dve.bn_stats(bst[:, t, bass.ds(c, 1), :].rearrange("p o s -> p (o s)"),
                                 x1[:, t, bass.ds(c * 512, 512)]).then_inc(s_bst, 1)

            def wo_chunk(c, banks):
                dve.wait_ge(s_used, Q_WO + 4 * c + 4)
                residual(c, banks)

            dve.wait_ge(s_res, 16)
            for c in range(3):
                for i in range(4):
                    lo(Q_WO + 4 * c + i + 2, (i + 2) % RAW)
                wo_chunk(c, (dn, ex)[c % 2])
            lo(Q_WO + 14, 2)
            lo(Q_WO + 15, 3)

            def last_chunk(t):
                if t < TT - 1:
                    dve.wait_ge(s_wt, t + 1)
                else:
                    dve.wait_ge(s_used, Q_MOE)
                stt(x1[:, t, 3 * 512:], x1[:, t, 3 * 512:], ALPHA, ex[:, t, :], ALU.mult, ALU.add).then_inc(s_wof, 1)
                dve.wait_ge(s_wof, 12 + t + 1)
                link(dve.bn_stats(bst[:, t, 3, :], x1[:, t, 3 * 512:]))
                link(dve.bn_aggr(mv[:, t, :], bst[:, t, :, :]))
                row_scale(slice(t, t + 1), TT + t + 1)

            def finish(t, n):
                scale_rows(x1, lng1, t, TT + t + 1)
                shift_rows(x1, lnb1, t, n)

            dve.wait_ge(s_bst, 12)
            last_chunk(0)
            last_chunk(1)
            dve.wait_ge(s_lnp[1], 64)
            finish(0, TT + 1)
            last_chunk(2)
            last_chunk(3)
            finish(2, TT + 2)
            def rv(i):
                return R[:, i, :, :]

            def rg(i):
                return R[:, i, :, :].rearrange("p t (g e) -> p t g e", e=EP)

            def rs(i):
                return R[:, i, :, 0:EG]

            def over_e(ap):
                return ap.unsqueeze(3).to_broadcast([P, TT, EG, EP])

            def over_16(ap):
                return ap.unsqueeze(2).to_broadcast([P, TT, E])

            dve.wait_ge(s_const2, 2)
            for t in range(TT):
                dve.wait_ge(s_lgx, t + 1)
                tt(R[:, 0, t, :], sets1[t % 2][:, 0, P:P + E], brb[:], ALU.add).then_inc(s_lgc, 1)
            dve.wait_ge(s_lgc, TT)
            one = R[:, 1, :, 0]
            link(dve.tensor_reduce(one, rv(0), AX.X, ALU.max))
            link(tt(rv(0), rv(0), over_16(one), ALU.subtract))
            exp_of(rv(2), rv(0), rv(3), rv(4), rv(5), rv(6))
            link(dve.tensor_reduce(one, rv(2), AX.X, ALU.add))
            link(dve.reciprocal(one, one))
            link(tt(rv(2), rv(2), over_16(one), ALU.mult))
            place_e = eio[:, 1, :].rearrange("p (g e) -> p g e", e=EP).unsqueeze(1).to_broadcast([P, TT, EG, EP])

            def first_max(p_, m, oh, w_):
                link(dve.tensor_reduce(rs(m), rg(p_), AX.X, ALU.max))
                link(tt(rg(w_), rg(p_), over_e(rs(m)), ALU.is_equal))
                link(tt(rg(w_), rg(w_), place_e, ALU.mult))
                link(dve.tensor_reduce(rs(23), rg(w_), AX.X, ALU.max))
                link(tt(rg(oh), rg(w_), over_e(rs(23)), ALU.is_equal))

            first_max(2, 7, 8, 9)
            link(stt(rv(10), rv(8), -2.0, rv(2), ALU.mult, ALU.add))
            first_max(10, 11, 12, 9)
            link(tt(rs(13), rs(7), rs(11), ALU.add))
            link(dve.tensor_reduce(one, rs(13), AX.X, ALU.max))
            link(tt(rs(14), rs(13), one.unsqueeze(2).to_broadcast([P, TT, EG]), ALU.is_equal))
            link(tt(rs(14), rs(14), gio[:].unsqueeze(1).to_broadcast([P, TT, EG]), ALU.mult))
            link(dve.tensor_reduce(one, rs(14), AX.X, ALU.max))
            link(tt(rs(15), rs(14), one.unsqueeze(2).to_broadcast([P, TT, EG]), ALU.is_equal))
            lk.go(tt(rg(16), rg(8), over_e(rs(15)), ALU.mult))
            lk.go(tt(rg(17), rg(12), over_e(rs(15)), ALU.mult))
            lk.wait()
            tt(mask[:], rv(16), rv(17), ALU.add).then_inc(s_msk, 1)
            link(tt(rs(13), rs(13), rs(15), ALU.mult))
            link(tt(rs(7), rs(7), rs(15), ALU.mult))
            link(tt(rs(11), rs(11), rs(15), ALU.mult))
            link(dve.tensor_reduce(one, rs(13), AX.X, ALU.add))
            link(dve.reciprocal(one, one))
            for k, i in enumerate((7, 11)):
                link(dve.tensor_reduce(R[:, 19, :, 0], rs(i), AX.X, ALU.add))
                link(tt(wts[:, :, k], R[:, 19, :, 0], one, ALU.mult))
            dve.wait_ge(s_rnk, 1)
            link(dve.tensor_copy(R[:, 20, :, :], dn[:, 3, 0:TT * E].rearrange("p (t e) -> p t e", t=TT)))
            cnt, ov, inc, kk = R[:, 21, 0, :], R[:, 21, 1, :], R[:, 21, 2, :], R[:, 21, 3, :]
            link(dve.tensor_copy(cnt, dn[:, 3, TT * E:(TT + 1) * E]))
            link(ts(ov, cnt, float(P), None, ALU.is_gt))
            for m in (2, 3):
                link(stt(ov, cnt, float(m * P), ov, ALU.is_gt, ALU.add))
            link(dve.tensor_tensor_scan(inc, ones[:], ov, 0.0, ALU.mult, ALU.add))
            link(tt(kk, inc, ov, ALU.subtract))
            link(stt(kk, kk, float(P), eio[:, 2, :], ALU.mult, ALU.add))
            link(ts(rv(22), rv(20), float(P), None, ALU.is_ge))
            link(tt(rv(22), rv(22), kk.unsqueeze(1).to_broadcast([P, TT, E]), ALU.mult))
            link(tt(rv(22), rv(22), rv(20), ALU.add))
            link(stt(rv(22), eio[:, 0, :].unsqueeze(1).to_broadcast([P, TT, E]), float(P), rv(22),
                     ALU.mult, ALU.add))
            for k, i in enumerate((16, 17)):
                link(tt(rv(9), rv(i), rv(22), ALU.mult))
                link(dve.tensor_reduce(R[:, 19, :, k], rv(9), AX.X, ALU.add))
            dve.tensor_copy(dest[:], R[:, 19, :, 0:2]).then_inc(s_dst, 1)
            link(tt(ovk[:], inc.unsqueeze(1).to_broadcast([P, NOVER + 1, E]),
                    ovn[:].unsqueeze(2).to_broadcast([P, NOVER + 1, E]), ALU.is_le))
            link(dve.tensor_reduce(R[:, 23, 0, 0:NOVER + 1], ovk[:], AX.X, ALU.add))
            link(ts(R[:, 23, 0, 0:NOVER + 1], R[:, 23, 0, 0:NOVER + 1], float(E - 1), None, ALU.min))
            lk.go(dve.tensor_copy(tab[:, COUNTS:COUNTS + E], cnt))
            lk.go(dve.memset(tab[:, COUNTS + E:COUNTS + NBLK], P))
            lk.go(dve.tensor_copy(tab[:, 0:E], eio[:, 0, :]))
            lk.go(dve.tensor_copy(tab[:, E:NBLK + 1], R[:, 23, 0, 0:NOVER + 1]))
            lk.wait()
            ts(tab[:, NBLK + 1:NBLK + 2], inc[:, E - 1:E], float(E), None, ALU.add).then_inc(s_tab, 1)

            def block_rows_lo(n, half, banks=dn):
                for c in range(2):
                    dve.wait_ge(s_xh, n * 4 + 2 * half + c + 1)
                    k = 8 * half + 4 * c
                    tt(xg_lo[:, k:k + 4, :], banks[:, c, :].rearrange("p (k n) -> p k n", k=4),
                       xg_hi[:, k:k + 4, :].bitcast(F32), ALU.subtract).then_inc(s_xl, 1)

            def this_block(b):
                for i in range(RM, PB):
                    lo_expert(b, i)
                    if i == 18:
                        dve.wait_ge(s_used, b * PB + (Q_MOE + 16))
                        for c in range(2):
                            dve.wait_ge(s_sil, b * 2 + c + 1)
                            tt(hid[:, c * 512:(c + 1) * 512], hid[:, c * 512:(c + 1) * 512], dn[:, 2 + c, :],
                               ALU.mult).then_inc(s_hm, 1)
                    if i == 19:
                        for c in range(2):
                            dve.wait_ge(s_hh, b * 2 + c + 1)
                            tt(h_lo[:, 4 * c:4 * c + 4, :], dn[:, 2 + c, :].rearrange("p (k n) -> p k n", k=4),
                               h_hi[:, 4 * c:4 * c + 4, :].bitcast(F32), ALU.subtract).then_inc(s_hl, 1)
                        block_rows_lo(b + 1, 0)
                    if i == 22:
                        block_rows_lo(b + 1, 1)

            def next_block(b):
                for i in range(PB, PB + RM):
                    lo_expert(b, i)

            block_rows_lo(0, 0)
            block_rows_lo(0, 1, ex)
            with dve.Fori(0, E - 1) as b:
                this_block(b)
                next_block(b)
            blocks = dve.value_load(tab[0:1, NBLK + 1:NBLK + 2], min_val=E, max_val=NBLK)
            with dve.Fori(E - 1, NBLK) as b:
                with dve.If(b < blocks):
                    this_block(b)
                    with dve.If(b < blocks - 1):
                        next_block(b)

            for t in range(TT):
                dve.wait_ge(s_xa, t + 1)
                dve.wait_ge(s_yr[t], 32)
                link(stt(xr[:, t, :], yg[:, t, 0, :], wts[:, t, 0:1], xr[:, t, :], ALU.mult, ALU.add))
                link(stt(xr[:, t, :], yg[:, t, 1, :], wts[:, t, 1:2], xr[:, t, :], ALU.mult, ALU.add))
                stats(xr, t)
                row_scale(slice(t, t + 1), 2 * TT + t + 1)
            dve.wait_ge(s_lnp[2], 32)
            for half in range(2):
                scale_rows(xr, lng2, TT - 1, 3 * TT + half, halves[half])
                shift_rows(xr, lnb2, TT - 1, TT + 3 + half, halves[half])

        @block.tensor
        def _(pe):
            pe.wait_ge(s_const, 4)
            for t in range(TT):
                pe.wait_ge(s_rows[t], 1)
                for b in range(4):
                    if t >= 2:
                        pe.wait_ge(s_trl, 4 * (t - 2) + b + 1)
                    for k in range(4):
                        mm = pe.transpose(sets[t % 2][:, b, k * P:(k + 1) * P],
                                          xin[:, t, (4 * b + k) * P:(4 * b + k + 1) * P], ident[:])
                    mm.then_inc(s_tr, 1)

            def three(o, w, wl, r_, rl, first, last):
                pe.matmul(o, lhsT=w, rhs=r_, start=first, stop=False)
                pe.matmul(o, lhsT=w, rhs=rl, start=False, stop=False)
                return pe.matmul(o, lhsT=wl, rhs=r_, start=False, stop=last)

            def unit_piece(q, s, par, rhs, k0, first, last, banks=dn):
                hi_, lo_ = rhs
                h = whi[:, s % RD, :].rearrange("p (k n) -> p k n", k=8)
                l = wlo[:, s % RD, :].rearrange("p (k n) -> p k n", k=8)
                pe.wait_ge(s_lo, q + 1)
                for k in range(8):
                    for c in range(2):
                        cs = slice(c * P, (c + 1) * P)
                        mm = three(banks[:, 2 * par + c, :], h[:, k, cs], l[:, k, cs],
                                   hi_[:, k0 + k, :], lo_[:, k0 + k, :], first and k == 0, last and k == 7)
                mm.then_inc(s_used, 1)

            def banks_free(n):
                if n < 2:
                    return
                m = n - 2
                if m < 12:
                    pe.wait_ge((s_cx, s_cm, s_pa)[m % 3], m // 3 + 1)
                elif m < 16:
                    pe.wait_ge(s_cp, 2 * (m - 11))
                elif m < 40:
                    pe.wait_ge(s_cp, 8 + 2 * (m - 15))

            def parameter_transposes():
                pe.wait_ge(s_prm, 16 * N_PRM)
                pe.wait_ge(s_trl, 16)
                pe.wait_ge(s_nat, 1)
                for i in range(3):
                    pe.transpose(ex[:, 0, i * GG:(i + 1) * GG], nat[:, i, :], ident[0:GG, 0:GG])
                pe.transpose(ex[0:2 * H, 0, 3 * GG:4 * GG], dnat[:], ident[0:GG, 0:GG])
                mm = pe.transpose(ex[:, 0, 4 * GG:4 * GG + 24], cwn[:], ident[0:24, 0:24])
                mm.then_inc(s_ptr, 1)

            def c_transposes():
                pe.wait_ge(s_pcp, 3)
                for c in range(2):
                    for a in range(8):
                        mm = pe.transpose(ex[:, 2 * c + a // 4, (a % 4) * P:(a % 4 + 1) * P],
                                          cnat[:, c, a, :, :].rearrange("p o n -> p (o n)"), ident[:])
                mm.then_inc(s_ctr, 1)

            def vt_transposes(half, c):
                if c == 0:
                    pe.wait_ge(s_vt, half + 1)
                    if half == 0:
                        pe.wait_ge(s_cc, 8)
                    else:
                        pe.wait_ge(s_yg, 4)
                else:
                    pe.wait_ge(s_v, 8 * half + 4)
                for g in range(HG):
                    mm = pe.transpose(ex[:, g // 4, (g % 4) * P:(g % 4 + 1) * P],
                                      VT[:, c, g, :, :].rearrange("p i h -> p (i h)"), ident[:])
                mm.then_inc(s_vtr, 1)

            def chunk_inputs(half):
                pe.wait_ge(s_u, 16 * 8 * (half + 1))
                pe.wait_ge(s_v, 8 * (half + 1))
                for c in range(2):
                    for g in range(HG):
                        for r in range(2):
                            slot = c * HG + g
                            mm = pe.matmul(ex[r * N:(r + 1) * N, slot // 8, (slot % 8) * NCH:(slot % 8 + 1) * NCH],
                                           lhsT=V[:, c, g, r * N:(r + 1) * N], rhs=U[:, 2 * g + r, :],
                                           start=True, stop=True)
                mm.then_inc(s_bu, 1)

            def kernels(half):
                pe.wait_ge(s_w, half + 1)
                pe.wait_ge(s_s, 4 * (half + 1))
                for g in range(HG):
                    for c in range(2):
                        mm = pe.matmul(ex[0:2 * H, g // 4, (g % 4) * P:(g % 4 + 1) * P],
                                       lhsT=Bbd[:, c, g, :, :].rearrange("p r h -> p (r h)"),
                                       rhs=W[:, c, g, 0:STEP, :].rearrange("p d h -> p (d h)"),
                                       start=(c == 0), stop=(c == 1))
                mm.then_inc(s_k, 1)

            def outputs(half):
                pe.wait_ge(s_st, half + 1)
                pe.wait_ge(s_m, 16 * 8 * (half + 1))
                pe.wait_ge(s_kp, half + 1)
                for g in range(HG):
                    for r in range(2):
                        o = ex[:, 2 * (g // 8) + r, (g % 8) * NCH:(g % 8 + 1) * NCH]
                        rows = slice(r * N, (r + 1) * N)
                        pe.matmul(o, lhsT=M[:, g, r, :], rhs=U[:, 2 * g + r, :], start=True, stop=False)
                        for c in range(2):
                            mm = pe.matmul(o[:, 1:], lhsT=W[rows, c, g, 1:, :].rearrange("p d h -> p (d h)"),
                                           rhs=S[rows, c, g, 0:NCH - 1], start=False, stop=(c == 1))
                mm.then_inc(s_y, 1)

            pe.wait_ge(s_trl, 16)
            for q in range(Q_GLU):
                n = unit_of(q)
                if q < Q_OA or q >= Q_G:
                    if q % 2 == 0:
                        banks_free(n)
                    unit_piece(q, q % RAW, n % 2, (xT_hi, xT_lo), 8 * (q % 2), q % 2 == 0, q % 2 == 1)
                else:
                    banks_free(n)
                    if q == Q_OA:
                        pe.wait_ge(s_pal, 4)
                    unit_piece(q, q % RAW, n % 2, (pa_hi, pa_lo), 0, True, True)
                if q == 1:
                    parameter_transposes()
                if q == 3:
                    c_transposes()
                if q >= Q_G:
                    half, rel = divmod(q - Q_G, 16)
                    if rel == 4:
                        vt_transposes(half, 0)
                    if rel == 5:
                        vt_transposes(half, 1)
                    if rel == 6:
                        chunk_inputs(half)
                    if rel == 9:
                        kernels(half)
                    if rel == 11:
                        outputs(half)
            pe.wait_ge(s_ysl, 8)
            pe.wait_ge(s_yg, 8)
            with pe.Fori(0, 4) as r:
                for i in range(2):
                    j = r * 2 + i
                    q = j * 2 + Q_GLU
                    if i == 0:
                        pe.wait_ge(s_cp, 56)
                    pe.wait_ge(s_gm, j + 1)
                    unit_piece(q, (2 * i) % RAW, 0, (ys_hi, ys_lo), 0, True, True, (dn, ex)[i])
                    unit_piece(q + 1, (2 * i + 1) % RAW, 1, (ys_hi, ys_lo), 0, True, True, (dn, ex)[i])

            pe.wait_ge(s_ml, 7)
            for c in range(4):
                banks = (dn, ex)[c % 2]
                if c == 1:
                    pe.wait_ge(s_gm, 10)
                if c >= 2:
                    pe.wait_ge(s_wof, 4 * (c - 1))
                for i in range(4):
                    q = Q_WO + 4 * c + i
                    h = whi[:, q % RD, :].rearrange("p (k n) -> p k n", k=4)
                    l = wlo[:, q % RD, :].rearrange("p (k n) -> p k n", k=4)
                    pe.wait_ge(s_lo, q + 1)
                    if c == 0 and i == 3:
                        pe.wait_ge(s_ml, 8)
                    last = c == 3 and i == 3
                    for n in range(4 * TT):
                        (t, k) = divmod(n, 4) if last else divmod(n, TT)[::-1]
                        kk, ts_ = 4 * i + k, slice(t * P, (t + 1) * P)
                        mm = tokens_by(pe, banks[:, t, :], mx_hi[:, kk, ts_], mx_lo[:, kk, ts_],
                                       h[:, k, :], l[:, k, :], kk == 0, kk == KD - 1)
                        if last and k == 3 and t < TT - 1:
                            mm.then_inc(s_wt, 1)
                    mm.then_inc(s_used, 1)

            def router(t):
                pe.wait_ge(s_x1c, 4 * t + 4)
                for k in range(KD):
                    mm = pe.matmul(sets1[t % 2][0:E, 0, 0:P], lhsT=wr[:, k, :], rhs=x1T[:, t % 2, k, :],
                                   start=(k == 0), stop=(k == KD - 1))
                mm.then_inc(s_log, 1)

            def logits_transpose(t):
                pe.wait_ge(s_lgt, t + 1)
                pe.transpose(sets1[t % 2][:, 0, P:P + E], lgT[:, t, :], ident[0:E, 0:E]).then_inc(s_lgx, 1)

            pe.wait_ge(s_lnp[1], 64)
            for t in range(TT):
                pe.wait_ge(s_rows[t], 2)
                if t < 2:
                    pe.wait_ge(s_wof, (12, 16)[t])
                for b in (1, 2, 3, 0):
                    if b == 0:
                        if t >= 2:
                            logits_transpose(t - 2)
                        if t >= 1:
                            router(t - 1)
                        if t >= 2:
                            pe.wait_ge(s_lgc, t - 1)
                    for k in range(4):
                        mm = pe.transpose(sets1[t % 2][:, b, k * P:(k + 1) * P],
                                          x1[:, t, (4 * b + k) * P:(4 * b + k + 1) * P], ident[:])
                    mm.then_inc(s_x1t, 1)
            logits_transpose(TT - 2)
            router(TT - 1)
            logits_transpose(TT - 1)
            pe.wait_ge(s_const2, 2)
            pe.wait_ge(s_msk, 1)
            for t in range(TT + 1):
                o = dn[:, 3, t * E:(t + 1) * E]
                for t_ in range(t):
                    mm = pe.matmul(o, lhsT=onesb[:], rhs=mask[:, t_, :], start=(t_ == 0), stop=(t_ == t - 1 and t == TT))
                if t < TT:
                    mm = pe.matmul(o, lhsT=tri[:], rhs=mask[:, t, :], start=(t == 0), stop=True)
            mm.then_inc(s_rnk, 1)

            def rows_transpose(n, half, banks=dn):
                if half == 0:
                    pe.wait_ge(s_xg, n * 16 + 16)
                elif banks is dn:
                    pe.wait_ge(s_xl, n * 4 + 2)
                for k in range(8):
                    mm = pe.transpose(banks[:, k // 4, (k % 4) * P:(k % 4 + 1) * P],
                                      xg[:, (8 * half + k) * P:(8 * half + k + 1) * P], ident[:])
                mm.then_inc(s_xt, 1)

            def expert_matmuls(s, banks, xh, xl, k0, first, last):
                h = mhi[:, s % RM, :].rearrange("p (k n) -> p k n", k=2)
                l = mlo[:, s % RM, :].rearrange("p (k n) -> p k n", k=2)
                for k in range(2):
                    for c in range(2):
                        cs = slice(c * 512, (c + 1) * 512)
                        mm = tokens_by(pe, banks[c], xh[:, k0 + k, :], xl[:, k0 + k, :], h[:, k, cs], l[:, k, cs],
                                       first and k == 0, last and k == 1)
                mm.then_inc(s_used, 1)

            def expert_piece(b, i):
                if isinstance(b, int):
                    pe.wait_ge(s_lop, i + 1)
                else:
                    pe.wait_ge(s_lo, lo_count(b, i))
                i = i % PB
                if i < 16:
                    banks = [dn[:, 2 * (i // 8) + c, :] for c in range(2)]
                    expert_matmuls(i % RM, banks, xg_hi, xg_lo, 2 * (i % 8), i % 8 == 0, i % 8 == 7)
                else:
                    banks = [ex[:, 2 * ((i - 16) // 4) + c, :] for c in range(2)]
                    expert_matmuls(i % RM, banks, h_hi, h_lo, 2 * (i % 4), i % 4 == 0, i % 4 == 3)

            def this_block(b):
                for i in range(3, 16):
                    expert_piece(b, i)
                pe.wait_ge(s_sil, b * 2 + 2)
                rows_transpose(b + 1, 0)
                for c in range(2):
                    pe.wait_ge(s_hm, b * 2 + c + 1)
                    for k in range(4):
                        mm = pe.transpose(dn[:, 2 + c, k * P:(k + 1) * P],
                                          hid[:, (4 * c + k) * P:(4 * c + k + 1) * P], ident[:])
                    mm.then_inc(s_ht, 1)
                pe.wait_ge(s_hl, b * 2 + 2)
                pe.wait_ge(s_yb, b * 2 + 1)
                for i in range(16, 19):
                    expert_piece(b, i)
                rows_transpose(b + 1, 1)
                for i in range(19, PB):
                    expert_piece(b, i)

            def next_block(b):
                pe.wait_ge(s_xl, b * 4 + 8)
                for i in range(PB, PB + 3):
                    expert_piece(b, i)

            pe.wait_ge(s_dst, 1)
            rows_transpose(0, 0)
            rows_transpose(0, 1, ex)
            pe.wait_ge(s_xl, 2)
            for i in range(3):
                expert_piece(0, i)
            pe.wait_ge(s_lop, RM)
            pe.wait_ge(s_xl, 4)
            with pe.Fori(0, E - 1) as b:
                this_block(b)
                next_block(b)
            pe.wait_ge(s_tab, 1)
            blocks = pe.value_load(tab[0:1, NBLK + 1:NBLK + 2], min_val=E, max_val=NBLK)
            with pe.Fori(E - 1, NBLK) as b:
                with pe.If(b < blocks):
                    this_block(b)
                    with pe.If(b < blocks - 1):
                        next_block(b)


_INS = ["x", "in_g", "in_b", "w_in", "conv_w", "w_out_a", "ssm_a_re", "ssm_a_im", "ssm_log_dt",
        "ssm_b_re", "ssm_b_im", "ssm_c_re", "ssm_c_im", "ssm_d", "w_glu", "w_o",
        "ln1_g", "ln1_b", "ln2_g", "ln2_b", "w_router", "b_router", "w_gate", "w_up", "w_down"]


def kernel(**inputs):
    import numpy as _np
    import concourse.bacc as _bacc
    from concourse import mybir as _mybir
    from concourse.bass_utils import run_bass_kernel_spmd as _run

    nc = _bacc.Bacc("TRN2", target_bir_lowering=False, num_devices=1)
    arrays, args = {}, []
    for name in _INS:
        a = _np.ascontiguousarray(inputs[name])
        arrays[f"in_{name}"] = a
        args.append(nc.dram_tensor(f"in_{name}", a.shape, _mybir.dt.from_np(a.dtype), kind="ExternalInput").ap())
    out = nc.dram_tensor("out", (1, T, D), _mybir.dt.float32, kind="ExternalOutput").ap()
    build_trunk(nc, *args, out)
    r = _run(nc, [arrays], core_ids=[0])
    return r.results[0]["out"]
```
